# Optimizing a Trainium2 kernel written in Bass

```python
import math
import jax, jax.numpy as jnp
from jax import lax
import numpy as np

D_MODEL = 2048
BATCH = 1
SEQ = 1024
DEPTH = 1

HEAD_DIM = 64
N_HEADS_DIL = 12
DIL_PATTERNS = ((128, 1), (512, 4), (2048, 16))
DIL_BLOCK = 128
N_HEADS_GLA = 4
GLA_DK = 128
GLA_DV = 256
GLA_GATE_RANK = 16
GLA_TAU = 16.0
GLA_CHUNK = 64
N_HEADS_MEM = 4
MEM_LEN = 256
REL_BUCKETS = 32
REL_MAX_DIST = 2048
EPS = 1e-6
NEG_INF = -1e30

D_DIL = N_HEADS_DIL * HEAD_DIM
D_GLA_K = N_HEADS_GLA * GLA_DK
D_GLA_V = N_HEADS_GLA * GLA_DV
D_MEM = N_HEADS_MEM * HEAD_DIM
D_MIX = D_DIL + D_GLA_V + D_MEM
IN_SIZES = (D_DIL, D_DIL, D_DIL,
            D_GLA_K, D_GLA_K, D_GLA_V,
            GLA_GATE_RANK,
            D_MEM,
            D_MIX)
D_IN_PROJ = sum(IN_SIZES)
IN_SPLIT_IDX = tuple(int(i) for i in np.cumsum(IN_SIZES)[:-1])

kernel_name = "hybrid_dilated_gla_memory_block"

def rmsnorm(x, w):
    xf = x.astype(jnp.float32)
    y = xf * lax.rsqrt(jnp.mean(xf * xf, axis=-1, keepdims=True) + EPS)
    return (y * w.astype(jnp.float32)).astype(x.dtype)

def t5_bucket(dist):
    max_exact = REL_BUCKETS // 2
    n = jnp.maximum(dist, 1).astype(jnp.float32)
    large = max_exact + (jnp.log(n / max_exact) / math.log(REL_MAX_DIST / max_exact)
                         * (REL_BUCKETS - max_exact)).astype(jnp.int32)
    large = jnp.minimum(large, REL_BUCKETS - 1)
    return jnp.where(dist < max_exact, dist, large)

def dilated_attention(q, k, v, rel_bias):
    B, S, H, Dh = q.shape
    BLK = DIL_BLOCK
    i = jnp.arange(BLK)[:, None]
    m = jnp.arange(2 * BLK)[None, :]
    rel = i - m + BLK
    outs, lses = [], []
    for window, dil in DIL_PATTERNS:
        back = window // dil
        assert back <= BLK
        L = S // dil
        nb = -(-L // BLK)
        Lp = nb * BLK

        def to_sub(t):
            return t.reshape(B, L, dil, H, Dh).transpose(0, 2, 3, 1, 4)

        qs, ks, vs = to_sub(q), to_sub(k), to_sub(v)
        qb = jnp.pad(qs, ((0, 0),) * 3 + ((0, Lp - L), (0, 0))).reshape(B, dil, H, nb, BLK, Dh)

        def band(t):
            tp = jnp.pad(t, ((0, 0),) * 3 + ((BLK, Lp - L), (0, 0)))
            prev = tp[..., :Lp, :].reshape(B, dil, H, nb, BLK, Dh)
            cur = tp[..., BLK:, :].reshape(B, dil, H, nb, BLK, Dh)
            return jnp.concatenate([prev, cur], axis=-2)

        kb, vb = band(ks), band(vs)
        key_idx = jnp.arange(nb)[:, None, None] * BLK - BLK + m[None]
        mask = (rel >= 0)[None] & (rel <= back)[None] & (key_idx >= 0)
        bias = rel_bias.astype(jnp.float32)[t5_bucket(jnp.clip(rel, 0, back) * dil)]
        bias = bias.transpose(2, 0, 1)
        logits = jnp.einsum('bghnqc,bghnkc->bghnqk', qb.astype(jnp.float32), kb.astype(jnp.float32))
        logits = logits + bias[None, None, :, None]
        logits = jnp.where(mask[None, None, None], logits, NEG_INF)
        mx = jnp.max(logits, axis=-1, keepdims=True)
        p = jnp.exp(logits - mx)
        den = jnp.sum(p, axis=-1, keepdims=True)
        o = jnp.einsum('bghnqk,bghnkc->bghnqc', p, vb.astype(jnp.float32)) / den
        lse = (mx + jnp.log(den))[..., 0]
        o = o.reshape(B, dil, H, Lp, Dh)[..., :L, :].transpose(0, 3, 1, 2, 4).reshape(B, S, H, Dh)
        lse = lse.reshape(B, dil, H, Lp)[..., :L].transpose(0, 3, 1, 2).reshape(B, S, H)
        outs.append(o)
        lses.append(lse)
    w = jax.nn.softmax(jnp.stack(lses, axis=0), axis=0)
    out = jnp.sum(w[..., None] * jnp.stack(outs, axis=0), axis=0)
    return out.astype(q.dtype)

def gla_attention(q, k, v, log_alpha, norm_w):
    B, S, H, dk = q.shape
    dv = v.shape[-1]
    C = GLA_CHUNK
    N = S // C
    f32 = lambda t: t.astype(jnp.float32).reshape(B, N, C, H, t.shape[-1])
    qc, kc, vc, la = f32(q), f32(k), f32(v), f32(log_alpha)
    b = jnp.cumsum(la, axis=2)
    b_last = b[:, :, -1:]
    q_t = qc * jnp.exp(b)
    k_t = kc * jnp.exp(-b)
    k_s = kc * jnp.exp(b_last - b)
    causal = jnp.tril(jnp.ones((C, C), dtype=bool))
    A = jnp.einsum('bnqhc,bnkhc->bnhqk', q_t, k_t)
    A = jnp.where(causal, A, 0.0)
    o_intra = jnp.einsum('bnhqk,bnkhv->bnqhv', A, vc)
    kv = jnp.einsum('bnkhc,bnkhv->bnhcv', k_s, vc)
    decay = jnp.exp(b_last[:, :, 0])

    def step(state, inp):
        dec, kv_n = inp
        return dec[..., None] * state + kv_n, state

    _, states = lax.scan(step, jnp.zeros((B, H, dk, dv), jnp.float32),
                         (jnp.moveaxis(decay, 1, 0), jnp.moveaxis(kv, 1, 0)))
    states = jnp.moveaxis(states, 0, 1)
    o_inter = jnp.einsum('bnqhc,bnhcv->bnqhv', q_t, states)
    o = (o_intra + o_inter).reshape(B, S, H, dv)
    return rmsnorm(o, norm_w).astype(q.dtype)

def memory_attention(q, mem_n, w_mem_kv):
    B, M, _ = mem_n.shape
    kv = mem_n @ w_mem_kv
    mk, mv = jnp.split(kv, 2, axis=-1)
    mk = mk.reshape(B, M, N_HEADS_MEM, HEAD_DIM)
    mv = mv.reshape(B, M, N_HEADS_MEM, HEAD_DIM)
    logits = jnp.einsum('bshc,bmhc->bhsm', q.astype(jnp.float32), mk.astype(jnp.float32))
    p = jax.nn.softmax(logits, axis=-1)
    return jnp.einsum('bhsm,bmhc->bshc', p, mv.astype(jnp.float32)).astype(q.dtype)

def setup_inputs(seed: int = 0) -> dict:
    key = jax.random.key(seed)
    ks = jax.random.split(key, 12)
    nrm = lambda k, shape, s: jax.random.normal(k, shape, jnp.float32) * s
    return {
        "x": nrm(ks[0], (BATCH, SEQ, D_MODEL), 1.0),
        "mem": nrm(ks[1], (BATCH, MEM_LEN, D_MODEL), 1.0),
        "norm_pre_w": 1.0 + nrm(ks[2], (DEPTH, D_MODEL), 0.02),
        "w_in": nrm(ks[3], (DEPTH, D_MODEL, D_IN_PROJ), D_MODEL ** -0.5),
        "rel_bias": nrm(ks[4], (REL_BUCKETS, N_HEADS_DIL), 0.1),
        "w_gla_gate2": nrm(ks[5], (DEPTH, GLA_GATE_RANK, D_GLA_K), GLA_GATE_RANK ** -0.5),
        "b_gla_gate": nrm(ks[6], (DEPTH, D_GLA_K), 0.1),
        "gla_norm_w": 1.0 + nrm(ks[7], (DEPTH, GLA_DV), 0.02),
        "mem_norm_w": 1.0 + nrm(ks[8], (DEPTH, D_MODEL), 0.02),
        "w_mem_kv": nrm(ks[9], (DEPTH, D_MODEL, 2 * D_MEM), D_MODEL ** -0.5),
        "w_out": nrm(ks[10], (DEPTH, D_MIX, D_MODEL), D_MIX ** -0.5),
        "norm_post_w": 1.0 + nrm(ks[11], (DEPTH, D_MODEL), 0.02),
    }

def reference(x, mem, norm_pre_w, w_in, rel_bias, w_gla_gate2, b_gla_gate, gla_norm_w,
              mem_norm_w, w_mem_kv, w_out, norm_post_w):
    B, S, _ = x.shape
    for l in range(DEPTH):
        h = rmsnorm(x, norm_pre_w[l])
        proj = h @ w_in[l]
        dq, dk, dv, gq, gk, gv, g_lr, mq, gate = jnp.split(proj, IN_SPLIT_IDX, axis=-1)
        a = dilated_attention(dq.reshape(B, S, N_HEADS_DIL, HEAD_DIM) * (HEAD_DIM ** -0.5),
                              dk.reshape(B, S, N_HEADS_DIL, HEAD_DIM),
                              dv.reshape(B, S, N_HEADS_DIL, HEAD_DIM), rel_bias)
        log_alpha = jax.nn.log_sigmoid((g_lr @ w_gla_gate2[l] + b_gla_gate[l]).astype(jnp.float32)) / GLA_TAU
        o_gla = gla_attention(gq.reshape(B, S, N_HEADS_GLA, GLA_DK) * (GLA_DK ** -0.5),
                              gk.reshape(B, S, N_HEADS_GLA, GLA_DK),
                              gv.reshape(B, S, N_HEADS_GLA, GLA_DV),
                              log_alpha.reshape(B, S, N_HEADS_GLA, GLA_DK), gla_norm_w[l])
        o_mem = memory_attention(mq.reshape(B, S, N_HEADS_MEM, HEAD_DIM) * (HEAD_DIM ** -0.5),
                                 rmsnorm(mem, mem_norm_w[l]), w_mem_kv[l])
        mix = jnp.concatenate([a.reshape(B, S, D_DIL), o_gla.reshape(B, S, D_GLA_V),
                               o_mem.reshape(B, S, D_MEM)], axis=-1)
        y = (mix * jax.nn.silu(gate)) @ w_out[l]
        x = x + rmsnorm(y, norm_post_w[l])
    return x


_drawn_inputs = setup_inputs


def setup_inputs(seed=0):
    import zlib

    import numpy as np

    out = dict(_drawn_inputs(seed))
    spreads = {}
    factors = {'rel_bias': 6.885, 'gla_norm_w': 4.005, 'mem_norm_w': 8.0, 'norm_post_w': 4.111}
    for name, (base, spread) in spreads.items():
        noise = np.random.default_rng([zlib.crc32(name.encode()), seed]).standard_normal(out[name].shape)
        drawn = base * np.exp(spread * noise) if base else spread * noise
        out[name] = __import__('jax').numpy.asarray(drawn.astype(out[name].dtype))
    for name, factor in factors.items():
        out[name] = (out[name] * factor).astype(out[name].dtype)
    return out
```

```python
from contextlib import ExitStack

import numpy as np

import concourse.bass as bass
from concourse import mybir

F32 = mybir.dt.float32
F32R = mybir.dt.float32r
I32 = mybir.dt.int32
ALU = mybir.AluOpType
ACT = mybir.ActivationFunctionType
AXX = mybir.AxisListType.X

P = 128
D = 2048
KT = D // P
SEQ = 1024
HALF = 512
NBLK = SEQ // P
DH = 64
N_DIL, N_GLA, N_MEM = 12, 4, 4
DV = 256
MEM = 256
CHUNK = 64
TAU = 16.0
RANK = 16
BUCKETS = 32
EPS = 1e-6
PATTERNS = ((128, 1), (512, 4), (2048, 16))
NEG = 1e30

C_DQ = 0
C_DK = C_DQ + N_DIL * DH
C_DV = C_DK + N_DIL * DH
C_GQ = C_DV + N_DIL * DH
C_GK = C_GQ + N_GLA * P
C_GV = C_GK + N_GLA * P
C_LR = C_GV + N_GLA * DV
C_MQ = C_LR + RANK
C_GATE = C_MQ + N_MEM * DH
X_DIL, X_GLA, X_MEM = 0, N_DIL // 2, N_DIL // 2 + 2 * N_GLA

T_LR = 4
T_GV0 = T_LR + 1
T_G = T_GV0 + 1
T_DV0 = T_G + 6 * N_GLA - 1
T_D = T_DV0 + 1
T_MQ0 = T_D + 4 * (N_DIL // 2) - 1
T_END = T_MQ0 + 4

TABLE = SEQ + P
GROUPS = [(i, j, min(4, i + 1 - j)) for i in range(NBLK) for j in range(0, i + 1, 4)]
NG = len(GROUPS)
QK_AT = {0: 0, 1: 1, 2: 2, 3: 3, 4: 4, 6: 5, 8: 6, 10: 7}
TURN_AT = 2


MEM_SLOTS = [([], [0, 1], [])] + [([k - 1], [k + 1], []) for k in range(1, 15)] + [([14, 15], [], [3])]
for _slot, _half in ((5, 0), (9, 1), (13, 2)):
    MEM_SLOTS[_slot][2].append(_half)


def t5_bucket(dist):
    half = BUCKETS // 2
    n = np.maximum(dist, 1).astype(np.float32)
    large = half + (np.log(n / np.float32(half)) / np.float32(np.log(2048 / half)) * np.float32(half)).astype(np.int32)
    return np.where(dist < half, dist, np.minimum(large, BUCKETS - 1))


def distance_table():
    dist = SEQ - 1 - np.arange(TABLE)
    count = np.zeros(TABLE, np.float32)
    for window, dil in PATTERNS:
        count += (dist >= 0) & (dist <= window) & (dist % dil == 0)
    out = np.zeros((BUCKETS + 1, TABLE), np.float32)
    out[t5_bucket(np.maximum(dist, 0)), np.arange(TABLE)] = -1.0
    out[BUCKETS] = np.where(count > 0, -np.log(np.maximum(count, 1)), NEG)
    return out


def build(nc, x, mem, norm_pre_w, w_in, rel_bias, w_gla_gate2, b_gla_gate, gla_norm_w, mem_norm_w,
          w_mem_kv, w_out, norm_post_w, dist_table, bias_rows, bias_tables, mix, out):
    x, mem, out = x[0], mem[0], out[0]
    w_in, w_mem_kv, w_out, w_gate2 = w_in[0], w_mem_kv[0], w_out[0], w_gla_gate2[0]

    with ExitStack() as ctx:
        def sb(name, shape, dt=F32, stack=ctx):
            return stack.enter_context(nc.sbuf_tensor(name, shape, dt))

        def sem(name):
            return ctx.enter_context(nc.semaphore(name))

        hT_hi = sb("hT_hi", [P, KT, SEQ], F32R)
        hT_lo = sb("hT_lo", [P, KT, SEQ], F32R)
        w_raw = sb("w_raw", [P, 2, 512])
        w_hi = sb("w_hi", [P, 4, 512], F32R)
        w_lo = sb("w_lo", [P, 4, 512], F32R)
        mkh = sb("mkh", [P, N_MEM, MEM], F32R)
        mkl = sb("mkl", [P, N_MEM // 2, MEM], F32R)
        mv = sb("mv", [P, N_MEM, MEM // P, P], F32R)
        ident = sb("ident", [P, P])
        pad = sb("pad", [P, 2])
        nw = sb("nw", [P, 2])
        negmax = sb("negmax", [P, NBLK])
        den = sb("den", [P, NBLK])
        rden = sb("rden", [P, NBLK])
        with ExitStack() as ph:
            xs = sb("xs", [P, 7, D], F32, ph)
            nwT = sb("nwT", [P, 2, KT], F32, ph)
            st = sb("st", [P, 4, 10], F32, ph)
            rel_sb = sb("rel_sb", [BUCKETS + 1, N_DIL], F32, ph)
            vtm = sb("vtm", [P, MEM], F32, ph)
        with ExitStack() as ph:
            qs = sb("qs", [P, 2, SEQ], F32R, ph)
            kh = sb("kh", [P, 2, SEQ], F32R, ph)
            kl = sb("kl", [P, SEQ], F32R, ph)
            vv = sb("vv", [P, 2, NBLK, P], F32R, ph)
            pT_hi = sb("pT_hi", [P, 2, 512], F32R, ph)
            pT_lo = sb("pT_lo", [P, 2, 512], F32R, ph)
            sc = sb("sc", [P, 2, SEQ], F32, ph)
            tab = sb("tab", [P, 2, SEQ], F32, ph)
            gate = sb("gate", [P, SEQ], F32, ph)
            mixb = sb("mixb", [P, SEQ], F32, ph)
            otmp = sb("otmp", [P, HALF], F32, ph)
        with ExitStack() as ph:
            ggate = sb("ggate", [P, 2, SEQ], F32, ph)
            gq = sb("gq", [P, SEQ], F32, ph)
            gk = sb("gk", [P, SEQ], F32, ph)
            bcum = sb("bcum", [P, SEQ], F32, ph)
            e1 = sb("e1", [P, SEQ], F32, ph)
            e2 = sb("e2", [P, SEQ], F32, ph)
            ks = sb("ks", [P, NBLK, P], F32, ph)
            gv = sb("gv", [P, NBLK, DV], F32, ph)
            am = sb("am", [P, 2, P], F32, ph)
            state = sb("state", [P, 4, DV], F32, ph)
            osb = sb("osb", [P, NBLK, DV], F32, ph)
            mixo = sb("mixo", [P, 2, HALF], F32, ph)
            lrT = sb("lrT", [RANK, SEQ], F32, ph)
            w2h = sb("w2h", [RANK, P], F32, ph)
            bgh = sb("bgh", [P, 1], F32, ph)
            ones = sb("ones", [P, CHUNK], F32, ph)
            amask = sb("amask", [P, P], I32, ph)
            dec = sb("dec", [P, 2 * NBLK], F32, ph)
            gst = sb("gst", [P, 4, NBLK], F32, ph)
        with ExitStack() as ph:
            y = sb("y", [P, 4, D], F32, ph)
            wpost = sb("wpost", [P, D], F32, ph)
            stg = sb("stg", [P, 4, HALF], F32, ph)
            xr = sb("xr", [P, 3, D // 2], F32, ph)
            ssy = sb("ssy", [P, 4, 4], F32, ph)
            yst = sb("yst", [P, 4, 4], F32, ph)
        tab_sb = xs[0:BUCKETS + 1, 5, 0:TABLE]
        brow = xs[0:N_DIL, 6, 0:TABLE]

        ps = ctx.enter_context(nc.psum_tensor("ps", [P, 8, 512], F32))
        L, TB, OB = 4, 6, 7

        raw_landed = [sem("raw_landed0"), sem("raw_landed1")]
        hi_done, lo_done = sem("hi_done"), sem("lo_done")
        unit_used = sem("unit_used")
        evac_act, evac_dve = sem("evac_act"), sem("evac_dve")
        s_id = sem("s_id")
        s_small = sem("s_small")
        s_rel = sem("s_rel")
        s_bias, s_biasc, s_biasw, s_rep = sem("s_bias"), sem("s_biasc"), sem("s_biasw"), sem("s_rep")
        x_in = [sem(f"x_in{i}") for i in range(7)]
        x_sq, x_v, x_sqrt, x_rc, x_scaled = sem("x_sq"), sem("x_v"), sem("x_sqrt"), sem("x_rc"), sem("x_scaled")
        x_turned, x_hi, x_lo = sem("x_turned"), sem("x_hi"), sem("x_lo")
        v_turned, v_act, v_dve = sem("v_turned"), sem("v_act"), sem("v_dve")
        keys_a = sem("keys_a")
        carried = sem("carried")
        J = {kind: {n: sem(f"{kind}_{n}") for n in (
            "logits", "negmax", "exps", "rden", "probs", "turned", "hi", "lo", "half", "ocopy", "osum")}
            for kind in ("dil", "mem")}
        tab_landed = [sem("tab_landed0"), sem("tab_landed1")]
        gated, mix_stored = sem("gated"), sem("mix_stored")
        g_par, g_z, g_abs, g_exp, g_min, g_ln, g_la, g_scan, g_rest = (sem(n) for n in (
            "g_par", "g_z", "g_abs", "g_exp", "g_min", "g_ln", "g_la", "g_scan", "g_rest"))
        g_e1, g_qt, g_e2, g_kt, g_e3, g_ks = (sem(n) for n in ("g_e1", "g_qt", "g_e2", "g_kt", "g_e3", "g_ks"))
        g_kturned, g_kcopied, g_a, g_am, g_kv, g_st = (sem(n) for n in (
            "g_kturned", "g_kcopied", "g_a", "g_am", "g_kv", "g_st"))
        g_o, g_ocopied, g_v, g_sqrt, g_scaled = (sem(n) for n in ("g_o", "g_ocopied", "g_v", "g_sqrt", "g_scaled"))
        g_turned, g_mixo, g_rc = sem("g_turned"), sem("g_mixo"), sem("g_rc")
        g_stored = [sem("g_stored0"), sem("g_stored1")]
        g_zero = sem("g_zero")
        stg_in = [sem(f"stg_in{i}") for i in range(4)]
        m_hi, m_lo = sem("m_hi"), sem("m_lo")
        y_done, y_copied, y_sq = sem("y_done"), sem("y_copied"), sem("y_sq")
        y_sum, y_sqrt, y_scaled, y_w, y_out = (sem(n) for n in ("y_sum", "y_sqrt", "y_scaled", "y_w", "y_out"))
        xr_in = [sem(f"xr_in{i}") for i in range(3)]
        wpost_in, y_rc = sem("wpost_in"), sem("y_rc")
        out_stored = sem("out_stored")

        def proj(par, a=0, b=P, n=SEQ):
            return ps[a:b, 2 * par:2 * par + 2, :].rearrange("p a b -> p (a b)")[:, 0:n]

        def logits(i, w):
            bank = i % 2 if w <= 512 else 0
            return ps[:, L:L + 2, :].rearrange("p a b -> p (a b)")[:, bank * 512:bank * 512 + w]

        def r32(ap):
            return ap.bitcast(F32)

        block = ctx.enter_context(nc.Block())

        @block.sync
        def _(sp):
            def unit(T, j, src):
                if not (isinstance(T, int) and 4 * T + j < 2):
                    sp.wait_ge(lo_done, 4 * T + j - 1)
                sp.dma_start(w_raw[:, j % 2, :].rearrange("p (k c) -> p k c", c=src.shape[-1]), src).then_inc(raw_landed[j % 2], 16)

            def tile(T, w, col):
                v = w.rearrange("(k p) c -> p k c", p=P)
                for j in range(4):
                    unit(T, j, v[:, 4 * j:4 * j + 4, bass.ds(col, P)])

            for n in range(10):
                src = mem[n * P:(n + 1) * P, :] if n < 2 else x[(n - 2) * P:(n - 1) * P, :]
                if n >= 7:
                    sp.wait_ge(x_turned, KT if n < 9 else 2 * KT)
                if n == 5:
                    sp.wait_ge(s_bias, 1)
                if n == 6:
                    sp.wait_ge(s_biasw, 16)
                sp.dma_start(xs[:, n % 7, :], src).then_inc(x_in[n % 7], 16)
                if n == 6:
                    tile(0, w_mem_kv, 0)
            for T in range(1, 4):
                tile(T, w_mem_kv, T * P)
            tile(T_LR, w_in, C_LR)
            tile(T_GV0, w_in, C_GV)
            for h in range(N_DIL):
                sp.dma_start(bias_tables[h].rearrange("(p n) -> p n", n=TABLE),
                             bias_rows[h:h + 1, :].to_broadcast([P, TABLE])).then_inc(s_rep, 16)

            def gla_params(h):
                sp.dma_start(w2h[:, :], w_gate2[:, bass.ds(h * P, P)]).then_inc(g_par, 16)
                sp.dma_start(bgh[:, :], b_gla_gate[0:1, bass.ds(h * P, P)].rearrange("a p -> p a")).then_inc(g_par, 16)

            def gla_tiles(h, T):
                tile(T, w_in, C_GV + P + h * DV)
                tile(T + 1, w_in, C_GK + h * P)
                tile(T + 2, w_in, C_GQ + h * P)
                tile(T + 3, w_in, C_GATE + X_GLA * P + h * (2 * P))
                tile(T + 4, w_in, C_GATE + (X_GLA + 1) * P + h * (2 * P))

            sp.wait_ge(x_turned, 3 * KT)
            gla_params(0)
            with sp.Fori(0, N_GLA - 1) as h:
                gla_tiles(h, T_G + 6 * h)
                sp.wait_ge(g_min, h + 1)
                gla_params(h + 1)
                tile(T_G + 6 * h + 5, w_in, C_GV + DV + h * DV)
            gla_tiles(N_GLA - 1, T_G + 6 * (N_GLA - 1))
            tile(T_DV0, w_in, C_DV)

            def tables(g):
                for hd in range(2):
                    src = bias_tables[bass.ds(2 * g + hd, 1), P - 1:P - 1 + P * (TABLE - 1)]
                    src = src.rearrange("a (p n) -> (a p) n", n=TABLE - 1)[:, 0:SEQ]
                    sp.dma_start(tab[:, hd, :], src).then_inc(tab_landed[hd], 16)

            tile(T_D, w_in, C_DK)
            sp.wait_ge(s_rep, 16 * N_DIL)
            sp.wait_ge(g_mixo, 4 * N_GLA)
            tables(0)
            with sp.Fori(0, N_DIL // 2 - 1) as g:
                T = T_D + 4 * g
                tile(T + 1, w_in, C_DQ + g * P)
                tile(T + 2, w_in, C_GATE + X_DIL * P + g * P)
                tile(T + 3, w_in, C_DV + P + g * P)
                tile(T + 4, w_in, C_DK + P + g * P)
                sp.wait_ge(J["dil"]["negmax"], 2 * NBLK * g + 2 * NBLK)
                tables(g + 1)
            gl = N_DIL // 2 - 1
            tile(T_D + 4 * gl + 1, w_in, C_DQ + gl * P)
            tile(T_D + 4 * gl + 2, w_in, C_GATE + (X_DIL + gl) * P)
            for j in range(2):
                tile(T_MQ0 + 2 * j, w_in, C_MQ + j * P)
                tile(T_MQ0 + 2 * j + 1, w_in, C_GATE + (X_MEM + j) * P)

            def piece(hf, k):
                n = 16 * hf + k
                if n >= 4:
                    sp.wait_ge(m_lo, n - 3)
                sp.dma_start(stg[:, n % 4, :], mix[k * P:(k + 1) * P, hf * HALF:(hf + 1) * HALF]).then_inc(stg_in[n % 4], 16)

            def out_unit(hf, n, k):
                u = 4 * T_END + 64 * hf + 16 * n + k
                sp.wait_ge(lo_done, u - 1)
                sp.dma_start(w_raw[:, k % 2, :], w_out[k * P:(k + 1) * P, bass.ds(n * 512, 512)]).then_inc(raw_landed[k % 2], 16)

            for k in range(4):
                out_unit(0, 0, k)
            sp.wait_ge(mix_stored, 16 * (N_DIL // 2 + 3))
            for q in range(2):
                sp.wait_ge(g_stored[q], 32 * N_GLA)
            sp.wait_ge(unit_used, 4 * T_END)
            for k in range(16):
                if k >= 4:
                    out_unit(0, 0, k)
                piece(0, k)
            sp.dma_start(wpost[:, :], norm_post_w[0:1, :].to_broadcast([P, D])).then_inc(wpost_in, 16)
            for k in range(16):
                piece(1, k)

            def residual(hf):
                for n in range(8 * hf, 8 * hf + 8):
                    if n >= 3:
                        sp.wait_ge(y_out, n - 2)
                    sp.dma_start(xr[:, n % 3, :], x[n // 2 * P:(n // 2 + 1) * P, n % 2 * 1024:(n % 2 + 1) * 1024]).then_inc(xr_in[n % 3], 16)

            with sp.Fori(1, 4) as n:
                for k in range(16):
                    out_unit(0, n, k)
            for k in range(16):
                out_unit(1, 0, k)
            for k in range(2):
                out_unit(1, 1, k)
            residual(0)
            for k in range(2, 16):
                out_unit(1, 1, k)
            with sp.Fori(2, 4) as n:
                for k in range(16):
                    out_unit(1, n, k)
            residual(1)

        @block.gpsimd
        def _(pool):
            pool.memset(ident[:, :], 0.0).then_inc(s_id, 1)
            pool.memset(rel_sb[:, :], 1.0).then_inc(s_id, 1)
            pool.wait_ge(s_id, 2)
            pool.affine_select(out=ident[:, :], in_=ident[:, :], compare_op=ALU.not_equal, fill=1.0, base=0,
                               pattern=[[-1, P]], channel_multiplier=1).then_inc(s_id, 1)
            pool.sem_inc(mix_stored, 16)
            pool.wait_ge(x_turned, 3 * KT)
            pool.memset(amask[:, :], 1).then_inc(g_zero, 1)
            pool.memset(am[:, :, :], 0.0).then_inc(g_zero, 1)
            pool.memset(ones[:, :], 1.0).then_inc(g_zero, 1)
            pool.wait_ge(g_zero, 3)
            pool.affine_select(out=amask[:, :], in_=amask[:, :], compare_op=ALU.is_ge, fill=0.0, base=0,
                               pattern=[[1, P]], channel_multiplier=-1).then_inc(g_zero, 1)
            pool.wait_ge(g_zero, 4)
            pool.affine_select(out=amask[:, CHUNK:P], in_=amask[:, CHUNK:P], compare_op=ALU.is_ge, fill=0.0,
                               base=-CHUNK, pattern=[[0, CHUNK]], channel_multiplier=1).then_inc(g_zero, 1)

            def gate_pair(kind, g, tiles):
                pool.wait_ge(J[kind]["osum"], 4 * g + 4)
                pool.wait_ge(evac_act, tiles)
                pool.tensor_tensor(mixb[:, :], mixb[:, :], gate[:, :], ALU.mult).then_inc(gated, 1)

            with pool.Fori(0, N_DIL // 2) as g:
                gate_pair("dil", g, T_D + 4 * g + 3)
            for j in range(2):
                gate_pair("mem", j, T_MQ0 + 2 * j + 2)

            for hf in range(2):
                for m in range(4):
                    for c in range(2):
                        n = 8 * hf + 2 * m + c
                        pool.wait_ge(xr_in[n % 3], 16 * (n // 3 + 1))
                        pool.wait_ge(y_w, n + 1)
                        ya = y[:, m, c * 1024:(c + 1) * 1024]
                        pool.tensor_tensor(ya, ya, xr[:, n % 3, :], ALU.add).then_inc(y_out, 1)

        @block.scalar
        def _(act):
            def split(T, j):
                act.wait_ge(raw_landed[j % 2], 16 * (2 * T + j // 2 + 1))
                if not isinstance(T, int) or T > 0:
                    act.wait_ge(unit_used, 4 * T + j - 3)
                act.activation(w_hi[:, j % 4, :], w_raw[:, j % 2, :], ACT.Copy).then_inc(hi_done, 1)

            def tile(T, par, kind, job=None, arg=None):
                for k in range(KT):
                    if k in (4, 8, 12):
                        split(T + 1, k // 4 - 1)
                    if job:
                        job(k)
                act.wait_ge(unit_used, 4 * T + 4)
                kind(T, par, arg)
                split(T + 1, 3)

            act.dma_start(nwT[:, 0, :], mem_norm_w.rearrange("a (k p) -> p (a k)", p=P)).then_inc(s_small, 16)
            act.dma_start(nwT[:, 1, :], norm_pre_w.rearrange("a (k p) -> p (a k)", p=P)).then_inc(s_small, 16)
            act.dma_start(nw[:, :], gla_norm_w.rearrange("a (k p) -> p (a k)", p=P)).then_inc(s_small, 16)
            act.dma_start(tab_sb, dist_table).then_inc(s_rel, 16)
            act.wait_ge(s_id, 2)
            act.dma_start(rel_sb[0:BUCKETS, :], rel_bias).then_inc(s_rel, 16)
            act.wait_ge(s_bias, 1)
            act.activation(brow, ps[0:N_DIL, L:L + 3, :].rearrange("p a b -> p (a b)")[:, 0:TABLE], ACT.Copy).then_inc(s_biasc, 1)
            act.wait_ge(s_biasc, 1)
            act.dma_start(bias_rows, brow).then_inc(s_biasw, 16)

            def squares(n):
                act.wait_ge(x_in[n % 7], 16 * (n // 7 + 1))
                if n > 0:
                    act.wait_ge(x_sq, n)
                act.activation(ps[:, 0:4, :].rearrange("p a b -> p (a b)"), xs[:, n % 7, :], ACT.Square,
                               accum_out=st[:, 0, n:n + 1]).then_inc(x_sq, 1)

            def root(q, lo, hi):
                act.wait_ge(x_v, q + 1)
                act.activation(st[:, 1, lo:hi], st[:, 0, lo:hi], ACT.Sqrt).then_inc(x_sqrt, 1)

            def turn_hi(q, base, width, w):
                for k in range(KT):
                    n = KT * q + k
                    act.wait_ge(x_turned, n + 1)
                    act.activation(hT_hi[:, k, base:base + width], ps[:, L + k % 4, 0:width], ACT.Copy,
                                   scale=nwT[:, w, k:k + 1]).then_inc(x_hi, 1)

            act.wait_ge(s_small, 48)
            for n in (0, 1):
                squares(n)
            root(0, 0, 2)
            turn_hi(0, 512, MEM, 0)
            for n in range(2, 6):
                squares(n)
            root(1, 2, 6)
            for j in range(4):
                split(0, j)
            turn_hi(1, 0, HALF, 1)

            def stacked_hi(dst_a, dst_b, par, n):
                for dst, r, ready in ((dst_a, slice(0, DH), keys_a), (dst_b, slice(DH, P), evac_act)):
                    act.activation(dst[0:DH, :], proj(par, r.start, r.stop, n), ACT.Copy)
                    act.activation(dst[DH:P, :], proj(par, r.start, r.stop, n), ACT.Copy).then_inc(ready, 1)

            def ev_mk(T, par, j):
                stacked_hi(mkh[:, 2 * j, :], mkh[:, 2 * j + 1, :], par, MEM)

            def ev_mv(T, par, j):
                if j > 0:
                    act.wait_ge(v_turned, j)
                act.activation(vtm[:, :], proj(par, 0, P, MEM), ACT.Copy).then_inc(evac_act, 1)
                act.wait_ge(v_turned, j + 1)
                act.activation(mv[:, 2 * j:2 * j + 2, :, 0:DH],
                               ps[:, TB, 0:MEM].rearrange("p (b h c) -> p h b c", h=2, c=DH), ACT.Copy).then_inc(v_act, 1)

            def ev_lr(T, par, _):
                act.activation(lrT[:, 0:HALF], ps[0:RANK, 2 * par, :], ACT.Copy).then_inc(evac_act, 1)

            def ev_copy(T, par, dst):
                act.activation(dst[:, 0:HALF], ps[:, 2 * par, :], ACT.Copy).then_inc(evac_act, 1)

            def ev_gate(T, par, dst):
                act.activation(dst, proj(par), ACT.Silu).then_inc(evac_act, 1)

            def ev_kd(T, par, _):
                stacked_hi(kh[:, 0, :], kh[:, 1, :], par, SEQ)

            def ev_qd(T, par, _):
                for hd, r, ready in ((0, slice(0, DH), keys_a), (1, slice(DH, P), evac_act)):
                    act.activation(qs[r, hd, :], proj(par, r.start, r.stop), ACT.Copy, scale=-DH ** -0.5).then_inc(ready, 1)

            def gla_v(first, j):
                def job(k):
                    if k == 1:
                        act.wait_ge(v_turned, first + 1)
                        act.activation(gv[:, 0:4, j * P:(j + 1) * P], ps[:, TB, :].rearrange("p (b c) -> p b c", c=P), ACT.Copy).then_inc(v_act, 1)
                return job

            def dil_v(first):
                def job(k):
                    if k in (1, 2):
                        act.wait_ge(v_turned, first + k)
                        act.activation(vv[:, :, 4 * k - 4:4 * k, 0:DH],
                                       ps[:, TB, :].rearrange("p (b h c) -> p h b c", h=2, c=DH), ACT.Copy).then_inc(v_act, 1)
                return job

            def soft(kind, a, hd, width):
                s = J[kind]
                causal = kind == "dil"
                ng = NG if causal else NBLK
                groups = GROUPS if causal else [(i, 0, 2) for i in range(NBLK)]

                def exps(i):
                    w = width(i)
                    act.wait_ge(s["negmax"], NBLK * a + i + 1)
                    src = sc[:, i % 2, 0:w] if causal else logits(i, w)
                    act.activation(sc[:, i % 2, 0:w], src, ACT.Exp, bias=negmax[:, i:i + 1], scale=-1.0,
                                   accum_out=den[:, i:i + 1]).then_inc(s["exps"], 1)

                def hi(n):
                    i, j, nb = groups[n]
                    act.wait_ge(s["turned"], ng * a + n + 1)
                    act.activation(pT_hi[:, n % 2, 0:nb * P], ps[:, TB, 0:nb * P], ACT.Copy).then_inc(s["hi"], 1)

                def half(q):
                    r = slice(hd * DH, hd * DH + DH)
                    act.wait_ge(s["half"], 2 * a + q + 1)
                    act.activation(otmp[r, :], ps[DH:P, OB, :], ACT.Copy).then_inc(s["ocopy"], 1)

                return exps, hi, half

            def causal_job(a, hd):
                exps, hi, half = soft("dil", a, hd, lambda i: (i + 1) * P)

                def job(k):
                    n = k - TURN_AT
                    if 0 <= n < NG:
                        hi(n)
                    if k in QK_AT:
                        exps(QK_AT[k])
                    if n == 4:
                        half(0)
                    if n == NG:
                        half(1)
                return job

            def mem_job(j):
                def parts(n):
                    return soft("mem", 2 * j + n // NBLK, n // NBLK, lambda i: MEM)

                def job(k):
                    turned, scored, halves = MEM_SLOTS[k]
                    for n in turned:
                        parts(n)[1](n % NBLK)
                    for n in scored:
                        parts(n)[0](n % NBLK)
                    for q in halves:
                        parts(4 * q)[2](q % 2)
                return job

            def store_mix(n, group):
                act.wait_ge(gated, n)
                act.dma_start(mix[bass.ds(group * P, P), :], mixb[:, :]).then_inc(mix_stored, 16)

            def gla(h, part):
                def job(k0):
                    k = k0 + 16 * part
                    if k == 0:
                        act.wait_ge(g_par, 32 * h + 32)
                        act.wait_ge(g_z, h + 1)
                        act.activation(e1[:, :], ps[:, L:L + 2, :].rearrange("p a b -> p (a b)"), ACT.Abs, bias=bgh[:, 0:1]).then_inc(g_abs, 1)
                        act.wait_ge(g_abs, h + 1)
                        act.activation(e1[:, :], e1[:, :], ACT.Exp, scale=-1.0).then_inc(g_exp, 1)
                        act.wait_ge(g_exp, h + 1)
                        act.activation(e1[:, :], e1[:, :], ACT.Ln, bias=1.0).then_inc(g_ln, 1)
                    if k == 5:
                        act.wait_ge(g_scan, h + 1)
                        act.activation(e1[:, :], bcum[:, :], ACT.Exp, scale=1.0 / TAU).then_inc(g_e1, 1)
                        act.wait_ge(g_rest, h + 1)
                        act.activation(e2[:, :], e2[:, :], ACT.Exp, scale=1.0 / TAU).then_inc(g_e3, 1)
                        act.wait_ge(g_qt, h + 1)
                        act.activation(e1[:, :], bcum[:, :], ACT.Exp, scale=-1.0 / TAU).then_inc(g_e2, 1)
                    if k in (10, 11):
                        q = k - 10
                        act.wait_ge(g_kturned, 2 * h + q + 1)
                        act.activation(ks[:, 4 * q:4 * q + 4, :], ps[:, TB, :].rearrange("p (b c) -> p b c", c=P), ACT.Copy).then_inc(g_kcopied, 1)
                    if 13 <= k < 29 and k % 2 == 1:
                        i = (k - 13) // 2
                        act.wait_ge(g_o, 8 * h + i + 1)
                        act.activation(osb[:, i, :], ps[:, OB, 0:DV], ACT.Copy)
                        act.activation(e1[:, 0:DV], ps[:, OB, 0:DV], ACT.Square, accum_out=gst[:, 0, i:i + 1]).then_inc(g_ocopied, 1)
                    if k == 28:
                        act.wait_ge(g_v, h + 1)
                        act.activation(gst[:, 2, :], gst[:, 1, :], ACT.Sqrt).then_inc(g_sqrt, 1)
                    if 32 <= k < 36:
                        q = k - 32
                        act.wait_ge(g_mixo, 4 * h + q + 1)
                        rows = bass.ds((X_GLA + q // 2) * P + h * (2 * P), P)
                        act.dma_start(mix[rows, (q % 2) * HALF:(q % 2 + 1) * HALF], mixo[:, q % 2, :]).then_inc(g_stored[q % 2], 16)
                    if k == 47:
                        for q in range(2):
                            act.wait_ge(g_stored[q], 32 * h + 32)
                return job

            for T in range(2):
                tile(T, T % 2, ev_mk, None, T)
            for T in range(2, 4):
                tile(T, T % 2, ev_mv, None, T - 2)
            for n in range(6, 10):
                act.wait_ge(evac_dve, 4)
                squares(n)
            root(2, 6, 10)
            turn_hi(2, HALF, HALF, 1)

            tile(T_LR, T_LR % 2, ev_lr)
            tile(T_GV0, T_GV0 % 2, ev_copy, None, e2)

            def gla_head(h, last):
                T = T_G + 6 * h
                tile(T, 0, ev_copy, gla_v(2 + 4 * h, 0), e2)
                tile(T + 1, 1, ev_copy, gla_v(4 + 4 * h, 1), gk)
                tile(T + 2, 0, ev_copy, None, gq)
                tile(T + 3, 1, ev_gate, gla(h, 0), ggate[:, 0, :])
                tile(T + 4, 0, ev_gate, gla(h, 1), ggate[:, 1, :])
                tile(T + 5, 1, ev_copy, gla(h, 2), sc[:, 0, :] if last else e2)

            with act.Fori(0, N_GLA - 1) as h:
                gla_head(h, False)
            gla_head(N_GLA - 1, True)

            V0 = 2 + 4 * N_GLA

            def dil_pair(g, T, last):
                tile(T, 0, ev_kd, dil_v(V0 + 2 * g))
                tile(T + 1, 1, ev_qd)
                tile(T + 2, 0, ev_gate, causal_job(2 * g, 0), gate[:, :])
                if last:
                    tile(T + 3, 1, ev_qd, causal_job(2 * g + 1, 1))
                else:
                    tile(T + 3, 1, ev_copy, causal_job(2 * g + 1, 1), sc[:, 0, :])
                store_mix(g + 1, X_DIL + g)

            with act.Fori(0, N_DIL // 2 - 1) as g:
                dil_pair(g, T_D + 4 * g, False)
            dil_pair(N_DIL // 2 - 1, T_D + 4 * (N_DIL // 2 - 1), True)
            tile(T_MQ0 + 1, (T_MQ0 + 1) % 2, ev_gate, mem_job(0), gate[:, :])
            store_mix(N_DIL // 2 + 1, X_MEM)
            tile(T_MQ0 + 2, T_MQ0 % 2, ev_qd)
            tile(T_MQ0 + 3, (T_MQ0 + 1) % 2, ev_gate, mem_job(1), gate[:, :])
            store_mix(N_DIL // 2 + 2, X_MEM + 1)

            def osplit(hf, n, k):
                half_u = 2 * T_END + 32 * hf + 8 * n + k // 2
                act.wait_ge(raw_landed[k % 2], 16 * half_u + 16)
                act.wait_ge(unit_used, 4 * T_END + 64 * hf + 16 * n + k - 3)
                act.activation(w_hi[:, k % 4, :], w_raw[:, k % 2, :], ACT.Copy).then_inc(hi_done, 1)

            def piece(hf, k):
                n = 16 * hf + k
                act.wait_ge(stg_in[n % 4], 16 * (n // 4 + 1))
                act.activation(hT_hi[:, k, hf * HALF:(hf + 1) * HALF], stg[:, n % 4, :], ACT.Copy).then_inc(m_hi, 1)

            def y_squares(hf, n, m, odd):
                act.wait_ge(y_copied, 16 * hf + 4 * n + m + 1)
                b = ps[:, 4 * odd + m, :]
                act.activation(b, b, ACT.Square, accum_out=ssy[:, m, bass.ds(n, 1)]).then_inc(y_sq, 1)

            def finish(hf):
                act.wait_ge(y_sum, hf + 1)
                act.activation(yst[:, 1, :], yst[:, 0, :], ACT.Sqrt).then_inc(y_sqrt, 1)
                for m in range(4):
                    act.wait_ge(y_rc, 5 * hf + 5)
                    act.activation(y[:, m, :], y[:, m, :], ACT.Copy, scale=yst[:, 2, m:m + 1]).then_inc(y_scaled, 1)
                    if m > 0:
                        store(hf, m - 1)
                store(hf, 3)

            def store(hf, m):
                row = (4 * hf + m) * P
                act.wait_ge(y_out, 8 * hf + 2 * m + 2)
                act.dma_start(out[row:row + P, :], y[:, m, :]).then_inc(out_stored, 16)

            act.wait_ge(evac_dve, T_END)
            act.wait_ge(evac_act, T_END)
            act.sem_inc(y_sq, 8)
            for k in range(16):
                piece(0, k)
                if k >= 4:
                    osplit(0, 0, k)
            for k in range(16):
                piece(1, k)
            for m in range(4):
                y_squares(0, 0, m, 0)

            def chunk(hf, n):
                for k in range(16):
                    osplit(hf, n, k)
                for m in range(4):
                    y_squares(hf, n, m, n % 2)

            for n in range(1, 4):
                chunk(0, n)
            for k in range(16):
                osplit(1, 0, k)
            finish(0)
            for m in range(4):
                y_squares(1, 0, m, 0)
            for n in range(1, 4):
                chunk(1, n)
            finish(1)
            act.wait_ge(out_stored, 16 * 8)

        @block.vector
        def _(dve):
            def carry(s, n):
                dve.wait_ge(s, n)
                dve.sem_inc(carried, 1)

            def split(T, j):
                dve.wait_ge(hi_done, 4 * T + j + 1)
                dve.tensor_tensor(w_lo[:, j % 4, :], w_raw[:, j % 2, :], r32(w_hi[:, j % 4, :]), ALU.subtract).then_inc(lo_done, 1)

            def tile(T, par, kind, job=None, arg=None):
                for k in range(KT):
                    if k in (4, 8, 12):
                        split(T + 1, k // 4 - 1)
                    if job:
                        job(k)
                dve.wait_ge(unit_used, 4 * T + 4)
                kind(T, par, arg)
                split(T + 1, 3)

            def inverse_root(v, root, t, out_, chain, c0):
                dve.reciprocal(out_, root).then_inc(chain, 1)
                dve.wait_ge(chain, c0 + 1)
                dve.tensor_tensor(t, out_, v, ALU.mult).then_inc(chain, 1)
                dve.wait_ge(chain, c0 + 2)
                dve.scalar_tensor_tensor(t, t, -0.5, out_, ALU.mult, ALU.mult).then_inc(chain, 1)
                dve.wait_ge(chain, c0 + 3)
                dve.scalar_tensor_tensor(out_, t, 1.5, out_, ALU.add, ALU.mult).then_inc(chain, 1)
                dve.wait_ge(chain, c0 + 4)

            def scale_rows(q, lo, hi):
                dve.wait_ge(x_sq, hi)
                dve.tensor_scalar(st[:, 0, lo:hi], st[:, 0, lo:hi], 1.0 / D, EPS, ALU.mult, ALU.add).then_inc(x_v, 1)
                dve.wait_ge(x_sqrt, q + 1)
                inverse_root(st[:, 0, lo:hi], st[:, 1, lo:hi], st[:, 3, lo:hi], st[:, 2, lo:hi], x_rc, 4 * q)
                for n in range(lo, hi):
                    dve.tensor_scalar(xs[:, n % 7, :], xs[:, n % 7, :], st[:, 2, n:n + 1], None, ALU.mult).then_inc(x_scaled, 1)

            def turn_lo(q, base, width, w):
                for k in range(KT):
                    n = KT * q + k
                    dve.wait_ge(x_hi, n + 1)
                    dve.scalar_tensor_tensor(hT_lo[:, k, base:base + width], ps[:, L + k % 4, 0:width], nwT[:, w, k:k + 1],
                                             r32(hT_hi[:, k, base:base + width]), ALU.mult, ALU.subtract).then_inc(x_lo, 1)

            dve.wait_ge(s_small, 48)
            scale_rows(0, 0, 2)
            turn_lo(0, 512, MEM, 0)
            scale_rows(1, 2, 6)
            for j in range(4):
                split(0, j)
            turn_lo(1, 0, HALF, 1)

            def stacked_lo(T, dst, hi_a, hi_b, par, n, count):
                for r, hi, ready, c, done in ((slice(0, DH), hi_a, keys_a, count, None), (slice(DH, P), hi_b, evac_act, T + 1, evac_dve)):
                    dve.wait_ge(ready, c)
                    ins = dve.tensor_tensor(dst[r, :], proj(par, r.start, r.stop, n), r32(hi[r, :]), ALU.subtract)
                    if done:
                        ins.then_inc(done, 1)

            def ev_mk(T, par, j):
                stacked_lo(T, mkl[:, j, :], mkh[:, 2 * j, :], mkh[:, 2 * j + 1, :], par, MEM, j + 1)

            def ev_mv(T, par, j):
                dve.wait_ge(v_act, j + 1)
                v = mv[:, 2 * j:2 * j + 2, :, :]
                dve.tensor_tensor(v[:, :, :, DH:P], ps[:, TB, 0:MEM].rearrange("p (b h c) -> p h b c", h=2, c=DH),
                                  r32(v[:, :, :, 0:DH]), ALU.subtract).then_inc(v_dve, 1)
                dve.sem_inc(evac_dve, 1)

            def ev_lr(T, par, _):
                dve.tensor_copy(lrT[:, HALF:SEQ], ps[0:RANK, 2 * par + 1, :]).then_inc(evac_dve, 1)

            def ev_copy(T, par, dst):
                dve.tensor_copy(dst[:, HALF:SEQ], ps[:, 2 * par + 1, :]).then_inc(evac_dve, 1)

            def ev_none(T, par, _):
                dve.sem_inc(evac_dve, 1)

            def ev_kd(T, par, count):
                stacked_lo(T, kl, kh[:, 0, :], kh[:, 1, :], par, SEQ, count)

            def ev_qd(T, par, count):
                for hd, r, o, ready, c, done in ((0, slice(0, DH), slice(DH, P), keys_a, count, None),
                                                 (1, slice(DH, P), slice(0, DH), evac_act, T + 1, evac_dve)):
                    dve.wait_ge(ready, c)
                    ins = dve.scalar_tensor_tensor(qs[o, hd, :], proj(par, r.start, r.stop), -DH ** -0.5, r32(qs[r, hd, :]),
                                                   ALU.mult, ALU.subtract)
                    if done:
                        ins.then_inc(done, 1)

            def gla_v(first, j):
                def job(k):
                    if k == 1:
                        dve.wait_ge(v_turned, first + 2)
                        dve.tensor_copy(gv[:, 4:8, j * P:(j + 1) * P], ps[:, TB, :].rearrange("p (b c) -> p b c", c=P)).then_inc(v_dve, 1)
                return job

            def dil_v(before):
                def job(k):
                    if k in (1, 2):
                        dve.wait_ge(v_act, before + k)
                        v = vv[:, :, 4 * k - 4:4 * k, :]
                        dve.tensor_tensor(v[:, :, :, DH:P], ps[:, TB, :].rearrange("p (b h c) -> p h b c", h=2, c=DH),
                                          r32(v[:, :, :, 0:DH]), ALU.subtract).then_inc(v_dve, 1)
                return job

            def soft(kind, a, hd, width, pairs):
                s = J[kind]
                causal = kind == "dil"
                groups = GROUPS if causal else [(i, 0, 2) for i in range(NBLK)]
                ng = len(groups)

                def scores(i):
                    w = width(i)
                    if causal:
                        if i >= 2:
                            carry(s["turned"], ng * a + len([g for g in groups if g[0] <= i - 2]))
                        carry(s["logits"], NBLK * a + i + 1)
                        if i == 0:
                            carry(tab_landed[hd], pairs)
                        dve.tensor_tensor_reduce(sc[:, i % 2, 0:w], logits(i, w), tab[:, hd, SEQ - w:SEQ], 1.0, 3e38,
                                                 ALU.add, ALU.min, negmax[:, i:i + 1]).then_inc(s["negmax"], 1)
                    else:
                        dve.wait_ge(s["logits"], NBLK * a + i + 1)
                        dve.tensor_reduce(negmax[:, i:i + 1], logits(i, w), AXX, ALU.min).then_inc(s["negmax"], 1)

                def norm(i):
                    w = width(i)
                    dve.wait_ge(s["exps"], NBLK * a + i + 1)
                    dve.reciprocal(rden[:, i:i + 1], den[:, i:i + 1]).then_inc(s["rden"], 1)
                    dve.wait_ge(s["rden"], NBLK * a + i + 1)
                    dve.tensor_scalar(sc[:, i % 2, 0:w], sc[:, i % 2, 0:w], rden[:, i:i + 1], None, ALU.mult).then_inc(s["probs"], 1)

                def lo(n):
                    nb = groups[n][2]
                    dve.wait_ge(s["hi"], ng * a + n + 1)
                    dve.tensor_tensor(pT_lo[:, n % 2, 0:nb * P], ps[:, TB, 0:nb * P], r32(pT_hi[:, n % 2, 0:nb * P]),
                                      ALU.subtract).then_inc(s["lo"], 1)

                def half(q):
                    r = slice(hd * DH, hd * DH + DH)
                    dve.wait_ge(s["ocopy"], 2 * a + q + 1)
                    dve.tensor_tensor(mixb[r, q * HALF:(q + 1) * HALF], ps[0:DH, OB, :], otmp[r, :], ALU.add).then_inc(s["osum"], 1)

                return scores, norm, lo, half

            def causal_job(a, hd, g):
                scores, norm, lo, half = soft("dil", a, hd, lambda i: (i + 1) * P, 16 * g + 16)

                def job(k):
                    n = k - TURN_AT
                    if k - 1 in QK_AT:
                        norm(QK_AT[k - 1])
                    if 0 <= n < NG:
                        lo(n)
                    if k in QK_AT:
                        scores(QK_AT[k])
                    if n == 4:
                        if hd == 0:
                            dve.wait_ge(mix_stored, 16 * g + 16)
                        half(0)
                    if n == NG:
                        half(1)
                return job

            def mem_job(j):
                def parts(n):
                    return soft("mem", 2 * j + n // NBLK, n // NBLK, lambda i: MEM, None)

                def job(k):
                    turned, scored, halves = MEM_SLOTS[k]
                    for n in turned:
                        parts(n)[1](n % NBLK)
                        parts(n)[2](n % NBLK)
                    for n in scored:
                        parts(n)[0](n % NBLK)
                    for q in halves:
                        if q == 0:
                            dve.wait_ge(mix_stored, 16 * (N_DIL // 2 + j) + 16)
                        parts(4 * q)[3](q % 2)
                return job

            def gla(h, part):
                def job(k0):
                    k = k0 + 16 * part
                    if k == 0:
                        dve.memset(state[:, 0, :], 0.0)
                        dve.wait_ge(g_abs, h + 1)
                        dve.tensor_scalar(e2[:, :], ps[:, L:L + 2, :].rearrange("p a b -> p (a b)"), bgh[:, 0:1], 0.0,
                                          ALU.add, ALU.min).then_inc(g_min, 1)
                        dve.wait_ge(g_min, h + 1)
                        dve.wait_ge(g_ln, h + 1)
                        dve.tensor_tensor(e2[:, :], e2[:, :], e1[:, :], ALU.subtract).then_inc(g_la, 1)
                    if k == 1:
                        dve.wait_ge(g_la, h + 1)
                        for c in range(2 * NBLK):
                            r = slice(c * CHUNK, (c + 1) * CHUNK)
                            scan = dve.tensor_tensor_scan(bcum[:, r], ones[:, :], e2[:, r], 0.0, ALU.mult, ALU.add)
                        scan.then_inc(g_scan, 1)
                    if k == 4:
                        dve.wait_ge(g_scan, h + 1)
                        b = bcum[:, :].rearrange("p (c t) -> p c t", t=CHUNK)
                        dve.tensor_tensor(e2[:, :].rearrange("p (c t) -> p c t", t=CHUNK),
                                          b[:, :, CHUNK - 1:CHUNK].to_broadcast([P, 2 * NBLK, CHUNK]), b, ALU.subtract).then_inc(g_rest, 1)
                    if k == 6:
                        dve.wait_ge(g_e1, h + 1)
                        dve.wait_ge(evac_act, T_G + 6 * h + 3)
                        dve.wait_ge(evac_dve, T_G + 6 * h + 3)
                        dve.scalar_tensor_tensor(gq[:, :], gq[:, :], P ** -0.5, e1[:, :], ALU.mult, ALU.mult)
                        dve.tensor_copy(dec[:, :], e1[:, :].rearrange("p (c t) -> p c t", t=CHUNK)[:, :, CHUNK - 1]).then_inc(g_qt, 1)
                        dve.wait_ge(g_e2, h + 1)
                        dve.tensor_tensor(bcum[:, :], gk[:, :], e1[:, :], ALU.mult).then_inc(g_kt, 1)
                        dve.wait_ge(g_e3, h + 1)
                        dve.tensor_tensor(gk[:, :], gk[:, :], e2[:, :], ALU.mult).then_inc(g_ks, 1)
                    if 12 <= k < 28 and k % 2 == 0:
                        i = (k - 12) // 2
                        if i >= 2:
                            carry(g_o, 8 * h + i - 1)
                        carry(g_a, 8 * h + i + 1)
                        dve.copy_predicated(am[:, i % 2, :], amask[:, :], ps[:, TB, 0:P]).then_inc(g_am, 1)
                        for c in range(2):
                            n = 2 * i + c
                            if n == 2 * NBLK - 1:
                                continue
                            if n >= 3:
                                dve.wait_ge(g_o, 8 * h + (n - 3) // 2 + 1)
                            if n >= 1:
                                dve.wait_ge(g_st, 15 * h + n)
                            dve.wait_ge(g_kv, 15 * h + n + 1)
                            dve.scalar_tensor_tensor(state[:, (n + 1) % 4, :], state[:, n % 4, :], dec[:, n:n + 1],
                                                     ps[:, L + c, 0:DV], ALU.mult, ALU.add).then_inc(g_st, 1)
                    if k == 28:
                        dve.wait_ge(g_ocopied, 8 * h + 8)
                        dve.tensor_scalar(gst[:, 1, :], gst[:, 0, :], 1.0 / DV, EPS, ALU.mult, ALU.add).then_inc(g_v, 1)
                    if k == 29:
                        dve.wait_ge(g_sqrt, h + 1)
                        inverse_root(gst[:, 1, :], gst[:, 2, :], gst[:, 3, :], gst[:, 0, :], g_rc, 4 * h)
                        for i in range(NBLK):
                            last = dve.tensor_scalar(osb[:, i, :], osb[:, i, :], gst[:, 0, i:i + 1], None, ALU.mult)
                        last.then_inc(g_scaled, 1)
                    if 32 <= k < 36:
                        q = k - 32
                        j, t = q // 2, q % 2
                        dve.wait_ge(evac_act, T_G + 6 * h + 5)
                        if j == 1:
                            dve.wait_ge(g_stored[t], 32 * h + 16)
                        dve.wait_ge(g_turned, 4 * h + q + 1)
                        dve.scalar_tensor_tensor(mixo[:, t, :], ps[:, TB, :], nw[:, j:j + 1], ggate[:, j, t * HALF:(t + 1) * HALF],
                                                 ALU.mult, ALU.mult).then_inc(g_mixo, 1)
                    if k == 47:
                        for t in range(2):
                            dve.wait_ge(g_stored[t], 32 * h + 32)
                return job

            for T in range(2):
                tile(T, T % 2, ev_mk, None, T)
            for T in range(2, 4):
                tile(T, T % 2, ev_mv, None, T - 2)
            scale_rows(2, 6, 10)
            turn_lo(2, HALF, HALF, 1)
            tile(T_LR, T_LR % 2, ev_lr)
            tile(T_GV0, T_GV0 % 2, ev_copy, None, e2)

            def gla_head(h, last):
                T = T_G + 6 * h
                tile(T, 0, ev_copy, gla_v(2 + 4 * h, 0), e2)
                tile(T + 1, 1, ev_copy, gla_v(4 + 4 * h, 1), gk)
                tile(T + 2, 0, ev_copy, None, gq)
                tile(T + 3, 1, ev_none, gla(h, 0))
                tile(T + 4, 0, ev_none, gla(h, 1))
                tile(T + 5, 1, ev_copy, gla(h, 2), sc[:, 0, :] if last else e2)

            dve.wait_ge(g_zero, 5)
            with dve.Fori(0, N_GLA - 1) as h:
                gla_head(h, False)
            gla_head(N_GLA - 1, True)

            V0 = 2 + 2 * N_GLA

            def dil_pair(g, T, last):
                tile(T, 0, ev_kd, dil_v(V0 + 2 * g), 2 + 2 * g + 1)
                tile(T + 1, 1, ev_qd, None, 2 + 2 * g + 2)
                tile(T + 2, 0, ev_none, causal_job(2 * g, 0, g))
                if last:
                    tile(T + 3, 1, ev_qd, causal_job(2 * g + 1, 1, g), 2 + 2 * g + 3)
                else:
                    tile(T + 3, 1, ev_copy, causal_job(2 * g + 1, 1, g), sc[:, 0, :])

            with dve.Fori(0, N_DIL // 2 - 1) as g:
                dil_pair(g, T_D + 4 * g, False)
            dil_pair(N_DIL // 2 - 1, T_D + 4 * (N_DIL // 2 - 1), True)
            tile(T_MQ0 + 1, (T_MQ0 + 1) % 2, ev_none, mem_job(0))
            tile(T_MQ0 + 2, T_MQ0 % 2, ev_qd, None, 2 + N_DIL + 2)
            tile(T_MQ0 + 3, (T_MQ0 + 1) % 2, ev_none, mem_job(1))

            def osplit(hf, n, k):
                dve.wait_ge(hi_done, 4 * T_END + 64 * hf + 16 * n + k + 1)
                dve.tensor_tensor(w_lo[:, k % 4, :], w_raw[:, k % 2, :], r32(w_hi[:, k % 4, :]), ALU.subtract).then_inc(lo_done, 1)

            def piece(hf, k):
                n = 16 * hf + k
                dve.wait_ge(m_hi, n + 1)
                r = slice(hf * HALF, (hf + 1) * HALF)
                dve.tensor_tensor(hT_lo[:, k, r], stg[:, n % 4, :], r32(hT_hi[:, k, r]), ALU.subtract).then_inc(m_lo, 1)

            def y_copy(hf, n, m):
                if m < 3:
                    dve.wait_ge(y_done, 12 * hf + 3 * n + m + 1)
                else:
                    dve.wait_ge(unit_used, 4 * T_END + 64 * hf + 16 * n + 16)
                if hf == 1 and n == 0:
                    dve.wait_ge(out_stored, 16 * 4)
                dve.tensor_copy(y[:, m, n * 512:(n + 1) * 512], ps[:, 4 * (n % 2) + m, :]).then_inc(y_copied, 1)

            def finish(hf):
                dve.wait_ge(y_sq, 8 + 16 * hf + 16)
                dve.tensor_reduce(yst[:, 0, :], ssy[:, :, :], AXX, ALU.add).then_inc(y_rc, 1)
                dve.wait_ge(y_rc, 5 * hf + 1)
                dve.tensor_scalar(yst[:, 0, :], yst[:, 0, :], 1.0 / D, EPS, ALU.mult, ALU.add).then_inc(y_sum, 1)
                dve.wait_ge(y_sqrt, hf + 1)
                inverse_root(yst[:, 0, :], yst[:, 1, :], yst[:, 3, :], yst[:, 2, :], y_rc, 5 * hf + 1)
                dve.wait_ge(wpost_in, 16)
                for m in range(4):
                    dve.wait_ge(y_scaled, 4 * hf + m + 1)
                    for c in range(2):
                        r = slice(c * 1024, (c + 1) * 1024)
                        dve.tensor_tensor(y[:, m, r], y[:, m, r], wpost[:, r], ALU.mult).then_inc(y_w, 1)

            for k in range(16):
                piece(0, k)
                if k >= 4:
                    osplit(0, 0, k)
            for k in range(16):
                piece(1, k)
            for m in range(4):
                y_copy(0, 0, m)

            def chunk(hf, n):
                for k in range(16):
                    osplit(hf, n, k)
                for m in range(4):
                    y_copy(hf, n, m)

            for n in range(1, 4):
                chunk(0, n)
            for k in range(16):
                osplit(1, 0, k)
            finish(0)
            for m in range(4):
                y_copy(1, 0, m)
            for n in range(1, 4):
                chunk(1, n)
            finish(1)

        @block.tensor
        def _(pe):
            def tile(T, par, job=None, cols=SEQ):
                halves = [(0, HALF), (1, HALF)] if cols == SEQ else [(0, cols)]
                base = 0 if cols == SEQ else HALF
                if not isinstance(T, int) or T >= 2:
                    pe.wait_ge(evac_act, T - 1)
                    pe.wait_ge(evac_dve, T - 1)
                for k in range(KT):
                    j = k // 4
                    if k % 4 == 0:
                        pe.wait_ge(lo_done, 4 * T + j + 1)
                    whi = w_hi[:, j, (k % 4) * P:(k % 4 + 1) * P]
                    wlo = w_lo[:, j, (k % 4) * P:(k % 4 + 1) * P]
                    for w, h, first, final in ((whi, hT_hi, True, False), (whi, hT_lo, False, False), (wlo, hT_hi, False, True)):
                        for q, n in halves:
                            mm = pe.matmul(ps[:, 2 * par + q, 0:n], w, h[:, k, base + q * HALF:base + q * HALF + n],
                                           start=(k == 0 and first), stop=(k == KT - 1 and final))
                    if k % 4 == 3:
                        mm.then_inc(unit_used, 1)
                    if job:
                        job(k)

            pe.wait_ge(s_rel, 32)
            pe.wait_ge(s_id, 3)
            for c in range(3):
                n = min(512, TABLE - 512 * c)
                mm = pe.matmul(ps[0:N_DIL, L + c, 0:n], rel_sb[:, :], tab_sb[:, 512 * c:512 * c + n], start=True, stop=True)
            mm.then_inc(s_bias, 1)
            pe.wait_ge(s_biasc, 1)

            def turn(q, tiles):
                for k in range(KT):
                    n = KT * q + k
                    if k == 0:
                        pe.wait_ge(x_scaled, tiles[-1] + 1)
                    if n >= 4:
                        pe.wait_ge(x_lo, n - 3)
                    for b, t in enumerate(tiles):
                        mm = pe.transpose(ps[:, L + k % 4, b * P:(b + 1) * P], xs[:, t % 7, k * P:(k + 1) * P], ident[:, :])
                    mm.then_inc(x_turned, 1)

            def turn_values(first, src, blocks, group):
                for b, t in enumerate(blocks):
                    mm = pe.transpose(ps[:, TB, b * P:(b + 1) * P], src[:, t * P:(t + 1) * P], ident[:, :])
                mm.then_inc(v_turned, 1)

            def mem_values(j):
                pe.wait_ge(evac_act, 3 + j)
                pe.wait_ge(x_lo, 2 * KT)
                if j > 0:
                    pe.wait_ge(v_dve, j)
                turn_values(j, vtm, (0, 1), 0)

            turn(0, range(0, 2))
            turn(1, range(2, 6))
            pe.wait_ge(x_lo, 2 * KT)
            pe.wait_ge(x_sq, 6)
            tile(0, 0, None, MEM)
            tile(1, 1, None, MEM)
            tile(2, 0, None, MEM)
            tile(3, 1, lambda k: mem_values(0) if k == 2 else None, MEM)
            mem_values(1)
            pe.wait_ge(v_dve, 2)
            turn(2, range(6, 10))
            pe.wait_ge(x_lo, 3 * KT)

            def gla_v(T, q):
                def job(k):
                    if k == 0:
                        pe.wait_ge(evac_act, T)
                        pe.wait_ge(evac_dve, T)
                        pe.wait_ge(v_dve, 2 + q)
                        turn_values(0, vsrc[0], range(0, 4), 0)
                    if k == 1:
                        pe.wait_ge(v_act, 2 + q + 1)
                        turn_values(0, vsrc[0], range(4, 8), 1)
                return job

            vsrc = [e2]
            NV = 2 + 2 * N_GLA

            def dil_v(T, g):
                def job(k):
                    if k == 0:
                        pe.wait_ge(evac_act, T)
                        pe.wait_ge(evac_dve, T)
                        turn_values(0, sc[:, 0, :], range(0, 4), 0)
                    if k == 1:
                        pe.wait_ge(v_dve, NV + 2 * g + 1)
                        turn_values(0, sc[:, 0, :], range(4, 8), 1)
                return job

            def soft(kind, a, hd, width, keys_hi, keys_lo, values, j):
                s = J[kind]
                causal = kind == "dil"
                groups = GROUPS if causal else [(i, 0, 2) for i in range(NBLK)]
                ng = len(groups)

                def scores(i):
                    w = width(i)
                    if i >= 2:
                        pe.wait_ge(s["negmax" if causal else "exps"], NBLK * a + (i - 1 if w <= 512 else i))
                    out_ = logits(i, w)
                    hi_rows = slice(hd * DH, hd * DH + DH)
                    for c in range(0, w, 512):
                        n = min(512, w - c)
                        pe.matmul(out_[:, c:c + n], qs[:, hd, i * P:(i + 1) * P], keys_hi[:, c:c + n], start=True, stop=False)
                        mm = pe.matmul(out_[:, c:c + n], qs[hi_rows, hd, i * P:(i + 1) * P], keys_lo[hi_rows, c:c + n], start=False, stop=True)
                    mm.then_inc(s["logits"], 1)

                def turned(n):
                    i, jb, nb = groups[n]
                    if jb == 0:
                        pe.wait_ge(s["probs"], NBLK * a + i + 1)
                    if n >= 1:
                        pe.wait_ge(s["lo"], ng * a + n)
                    for b in range(nb):
                        mm = pe.transpose(ps[:, TB, b * P:(b + 1) * P], sc[:, i % 2, (jb + b) * P:(jb + b + 1) * P], ident[:, :])
                    mm.then_inc(s["turned"], 1)

                def values_(n):
                    i, jb, nb = groups[n]
                    pe.wait_ge(s["lo"], ng * a + n + 1)
                    if i == 4 and jb == 0:
                        pe.wait_ge(s["osum"], 2 * a + 1)
                    last = i if causal else 1
                    for b in range(nb):
                        for part in (pT_hi, pT_lo):
                            mm = pe.matmul(ps[:, OB, (i % 4) * P:(i % 4 + 1) * P], values[:, jb + b, :], part[:, n % 2, b * P:(b + 1) * P],
                                           start=(jb + b == 0 and part is pT_hi), stop=(jb + b == last and part is pT_lo))
                    if i % 4 == 3 and jb + nb - 1 == last:
                        mm.then_inc(s["half"], 1)

                return scores, turned, values_

            def causal_job(a, hd, g):
                scores, turned, values_ = soft("dil", a, hd, lambda i: (i + 1) * P, kh[:, hd, :], kl[:, :], vv[:, hd, :, :], None)

                def job(k):
                    n = k - TURN_AT
                    if k == 0 and hd == 0:
                        pe.wait_ge(evac_dve, T_D + 4 * g + 2)
                        pe.wait_ge(v_dve, NV + 2 * g + 2)
                    if 1 <= n <= NG:
                        if n == 1 and hd == 1:
                            pe.wait_ge(J["dil"]["osum"], 2 * a)
                        values_(n - 1)
                    if 0 <= n < NG:
                        turned(n)
                    if k in QK_AT:
                        scores(QK_AT[k])
                return job

            def mem_job(j):
                def parts(n):
                    hd = n // NBLK
                    return soft("mem", 2 * j + hd, hd, lambda i: MEM, mkh[:, 2 * j + hd, :], mkl[:, j, :], mv[:, 2 * j + hd, :, :], j)

                def used(n):
                    if n == 0:
                        pe.wait_ge(J["dil" if j == 0 else "mem"]["osum"], 2 * N_DIL if j == 0 else 4)
                    if n == NBLK:
                        pe.wait_ge(J["mem"]["osum"], 4 * j + 2)
                    parts(n)[2](n % NBLK)

                def job(k):
                    turned_, scored, _ = MEM_SLOTS[k]
                    if k == 0:
                        pe.wait_ge(evac_dve, T_MQ0 + 2 * j + 1)
                    if k >= 2:
                        used(k - 2)
                    for n in turned_:
                        if n == 15:
                            used(14)
                        if n == NBLK:
                            pe.wait_ge(J["mem"]["lo"], (2 * j + 1) * NBLK)
                        parts(n)[1](n % NBLK)
                    for n in scored:
                        if n in (NBLK, NBLK + 1):
                            pe.wait_ge(J["mem"]["exps"], 2 * NBLK * j + n - 1)
                        parts(n)[0](n % NBLK)
                    if k == 15:
                        used(15)
                return job

            def gla(h, part):
                def job(k0):
                    k = k0 + 16 * part
                    if k == 0:
                        pe.wait_ge(g_par, 32 * h + 32)
                        for q in range(2):
                            mm = pe.matmul(ps[:, L + q, :], w2h[:, :], lrT[:, q * HALF:(q + 1) * HALF], start=True, stop=True)
                        mm.then_inc(g_z, 1)
                    if k in (10, 11):
                        q = k - 10
                        if q == 0:
                            pe.wait_ge(g_ks, h + 1)
                            pe.wait_ge(v_dve, 2 + 2 * h + 2)
                        else:
                            pe.wait_ge(g_kcopied, 2 * h + 1)
                        for b in range(4):
                            t = 4 * q + b
                            mm = pe.transpose(ps[:, TB, b * P:(b + 1) * P], gk[:, t * P:(t + 1) * P], ident[:, :])
                        mm.then_inc(g_kturned, 1)
                    if 12 <= k < 28 and k % 2 == 0:
                        i = (k - 12) // 2
                        blk = slice(i * P, (i + 1) * P)
                        if i == 0:
                            pe.wait_ge(g_kcopied, 2 * h + 2)
                            pe.wait_ge(g_kt, h + 1)
                            pe.wait_ge(g_min, h + 1)
                        else:
                            pe.wait_ge(g_am, 8 * h + i)
                            pe.wait_ge(g_st, 15 * h + 2 * i)
                        pe.matmul(ps[:, TB, 0:P], bcum[:, blk], gq[:, blk], start=True, stop=True).then_inc(g_a, 1)
                        for c in range(2):
                            if 2 * i + c == 2 * NBLK - 1:
                                continue
                            r = slice(c * CHUNK, (c + 1) * CHUNK)
                            pe.matmul(ps[:, L + c, 0:DV], ks[r, i, :], gv[r, i, :], start=True, stop=True).then_inc(g_kv, 1)
                    if 13 <= k < 29 and k % 2 == 1:
                        i = (k - 13) // 2
                        pe.wait_ge(g_am, 8 * h + i + 1)
                        pe.wait_ge(g_st, 15 * h + min(2 * i + 1, 15))
                        if i >= 1:
                            pe.wait_ge(g_ocopied, 8 * h + i)
                        pe.matmul(ps[:, OB, 0:DV], am[:, i % 2, :], gv[:, i, :], start=True, stop=False)
                        for c in range(2):
                            t = i * P + c * CHUNK
                            mm = pe.matmul(ps[c * CHUNK:(c + 1) * CHUNK, OB, 0:DV], gq[:, t:t + CHUNK], state[:, (2 * i + c) % 4, :],
                                           start=False, stop=True)
                        mm.then_inc(g_o, 1)
                    if 32 <= k < 36:
                        q = k - 32
                        j, t = q // 2, q % 2
                        if q == 0:
                            pe.wait_ge(g_scaled, h + 1)
                        else:
                            pe.wait_ge(g_mixo, 4 * h + q)
                        for b in range(4):
                            mm = pe.transpose(ps[:, TB, b * P:(b + 1) * P], osb[:, 4 * t + b, j * P:(j + 1) * P], ident[:, :])
                        mm.then_inc(g_turned, 1)
                return job

            pe.wait_ge(x_sq, 10)
            tile(T_LR, T_LR % 2)
            tile(T_GV0, T_GV0 % 2)

            def gla_head(h):
                T = T_G + 6 * h
                tile(T, 0, gla_v(T, 2 * h))
                tile(T + 1, 1, gla_v(T + 1, 2 * h + 1))
                tile(T + 2, 0)
                tile(T + 3, 1, gla(h, 0))
                tile(T + 4, 0, gla(h, 1))
                tile(T + 5, 1, gla(h, 2))

            with pe.Fori(0, N_GLA) as h:
                gla_head(h)

            def dil_pair(g):
                T = T_D + 4 * g
                tile(T, 0, dil_v(T, g))
                tile(T + 1, 1)
                tile(T + 2, 0, causal_job(2 * g, 0, g))
                tile(T + 3, 1, causal_job(2 * g + 1, 1, g))

            with pe.Fori(0, N_DIL // 2) as g:
                dil_pair(g)
            tile(T_MQ0 + 1, (T_MQ0 + 1) % 2, mem_job(0))
            tile(T_MQ0 + 2, T_MQ0 % 2)
            tile(T_MQ0 + 3, (T_MQ0 + 1) % 2, mem_job(1))

            for hf in range(2):
                with pe.Fori(0, 4, 2) as n2:
                    for odd in range(2):
                        for k in range(KT):
                            pe.wait_ge(lo_done, 4 * T_END + 64 * hf + 16 * n2 + 16 * odd + k + 1)
                            pe.wait_ge(m_lo, 16 * hf + k + 1)
                            for m in range(4):
                                bank = ps[:, 4 * odd + m, :]
                                if k == 0:
                                    pe.wait_ge(y_sq, 16 * hf + 4 * n2 + 4 * odd + m + 1)
                                t = slice(hf * HALF + m * P, hf * HALF + (m + 1) * P)
                                pe.matmul(bank, hT_hi[:, k, t], w_hi[:, k % 4, :], start=(k == 0), stop=False)
                                pe.matmul(bank, hT_hi[:, k, t], w_lo[:, k % 4, :], start=False, stop=False)
                                mm = pe.matmul(bank, hT_lo[:, k, t], w_hi[:, k % 4, :], start=False, stop=(k == KT - 1))
                                if m == 3:
                                    mm.then_inc(unit_used, 1)
                                elif k == KT - 1:
                                    mm.then_inc(y_done, 1)


_INS = ['x', 'mem', 'norm_pre_w', 'w_in', 'rel_bias', 'w_gla_gate2', 'b_gla_gate', 'gla_norm_w',
        'mem_norm_w', 'w_mem_kv', 'w_out', 'norm_post_w']


def kernel(**inputs):
    import numpy as _np
    import concourse.bacc as _bacc
    from concourse import mybir as _mybir
    from concourse.bass_utils import run_bass_kernel_spmd as _run

    nc = _bacc.Bacc("TRN2", target_bir_lowering=False, num_devices=1, dynamic_dma_scratch_size=1024)
    arrays, args = {}, []
    for name in _INS:
        a = _np.ascontiguousarray(inputs[name])
        arrays[f"in_{name}_dram"] = a
        args.append(nc.dram_tensor(f"in_{name}_dram", a.shape, _mybir.dt.from_np(a.dtype), kind="ExternalInput").ap())
    arrays["dist_table_dram"] = distance_table()
    f32 = _mybir.dt.float32
    args.append(nc.dram_tensor("dist_table_dram", (BUCKETS + 1, TABLE), f32, kind="ExternalInput").ap())
    args.append(nc.dram_tensor("bias_rows", (N_DIL, TABLE), f32, kind="Internal").ap())
    args.append(nc.dram_tensor("bias_tables", (N_DIL, P * TABLE), f32, kind="Internal").ap())
    args.append(nc.dram_tensor("mix", (D, SEQ), f32, kind="Internal").ap())
    args.append(nc.dram_tensor("out_dram", (1, SEQ, D), f32, kind="ExternalOutput").ap())
    with nc.allow_non_contiguous_dma(reason="norm weights and gate biases, one element a partition"):
        build(nc, *args)
    r = _run(nc, [arrays], core_ids=[0])
    return r.results[0]["out_dram"]
```

```python
from contextlib import ExitStack

import numpy as np

import concourse.bass as bass
from concourse import mybir

F32 = mybir.dt.float32
F32R = mybir.dt.float32r
I32 = mybir.dt.int32
ALU = mybir.AluOpType
ACT = mybir.ActivationFunctionType
AXX = mybir.AxisListType.X

P = 128
D = 2048
KT = D // P
SEQ = 1024
HALF = 512
NBLK = SEQ // P
DH = 64
N_DIL, N_GLA, N_MEM = 12, 4, 4
DV = 256
MEM = 256
CHUNK = 64
TAU = 16.0
RANK = 16
BUCKETS = 32
EPS = 1e-6
PATTERNS = ((128, 1), (512, 4), (2048, 16))
NEG = 1e30

C_DQ = 0
C_DK = C_DQ + N_DIL * DH
C_DV = C_DK + N_DIL * DH
C_GQ = C_DV + N_DIL * DH
C_GK = C_GQ + N_GLA * P
C_GV = C_GK + N_GLA * P
C_LR = C_GV + N_GLA * DV
C_MQ = C_LR + RANK
C_GATE = C_MQ + N_MEM * DH
X_DIL, X_GLA, X_MEM = 0, N_DIL // 2, N_DIL // 2 + 2 * N_GLA

T_LR = 4
T_GV0 = T_LR + 1
T_G = T_GV0 + 1
T_DV0 = T_G + 6 * N_GLA - 1
T_D = T_DV0 + 1
T_MQ0 = T_D + 4 * (N_DIL // 2) - 1
T_END = T_MQ0 + 4

TABLE = SEQ + P
GROUPS = [(i, j, min(4, i + 1 - j)) for i in range(NBLK) for j in range(0, i + 1, 4)]
NG = len(GROUPS)
QK_AT = {0: 0, 1: 1, 3: 2, 4: 3, 5: 4, 7: 5, 9: 6, 11: 7}
TURN_AT = {n + (3 if n < 4 else 4): n for n in range(NG)}
USE_AT = {r + 1: n for r, n in TURN_AT.items()}
HALF_AT = {max(r for r, n in USE_AT.items() if GROUPS[n][0] == 4 * q + 3): q for q in range(2)}
START = (1, 15)
VALUES_AT = 5
MEM_QK_AT = {3 * n // 2: n for n in range(2 * NBLK)}
MEM_TURN_AT = {3 * n // 2 + 2: n for n in range(2 * NBLK)}
MEM_USE_AT = {3 * n // 2 + 3: n for n in range(2 * NBLK)}
MEM_HALF_AT = {3 * (4 * q + 3) // 2 + 3: q for q in range(4)}

CHUNKS = 8
UNITS = [(c, k) for c in range(CHUNKS - 2) for k in range(KT)] + [(CHUNKS - 2, k) for k in range(4)]
for _k in range(KT):
    UNITS += ([(CHUNKS - 2, _k + 4)] if _k < KT - 4 else []) + [(CHUNKS - 1, _k)]
UNIT_NO = {u: 4 * T_END + i for i, u in enumerate(UNITS)}


def splits_at(c, k):
    if c < CHUNKS - 2 or (c == CHUNKS - 2 and k < KT - 4):
        now = [(c + (k + 4) // KT, (k + 4) % KT)]
    else:
        now = []
    return now + ([(CHUNKS - 1, k)] if c == CHUNKS - 2 else [])


PIECES = [(0, k) for k in range(KT - 1)] + [(1, k) for k in range(KT - 1)]
DIRECT = KT - 1


def piece_no(n):
    return n + 1 if n < DIRECT else n + 3


def pieces_at(c, k):
    if c == -1:
        return [k - 5] if k >= 5 else []
    if c == 0:
        return [k + 11] if k < 4 else []
    return [DIRECT + k] if c == 1 and k < KT - 1 else []


DIRECT_AT = 13


def t5_bucket(dist):
    half = BUCKETS // 2
    n = np.maximum(dist, 1).astype(np.float32)
    large = half + (np.log(n / np.float32(half)) / np.float32(np.log(2048 / half)) * np.float32(half)).astype(np.int32)
    return np.where(dist < half, dist, np.minimum(large, BUCKETS - 1))


def distance_table():
    dist = SEQ - 1 - np.arange(TABLE)
    count = np.zeros(TABLE, np.float32)
    for window, dil in PATTERNS:
        count += (dist >= 0) & (dist <= window) & (dist % dil == 0)
    out = np.zeros((BUCKETS + 1, TABLE), np.float32)
    out[t5_bucket(np.maximum(dist, 0)), np.arange(TABLE)] = -1.0
    out[BUCKETS] = np.where(count > 0, -np.log(np.maximum(count, 1)), NEG)
    return out


def build(nc, x, mem, norm_pre_w, w_in, rel_bias, w_gla_gate2, b_gla_gate, gla_norm_w, mem_norm_w,
          w_mem_kv, w_out, norm_post_w, dist_table, bias_rows, bias_tables, mix, out):
    x, mem, out = x[0], mem[0], out[0]
    w_in, w_mem_kv, w_out, w_gate2 = w_in[0], w_mem_kv[0], w_out[0], w_gla_gate2[0]

    with ExitStack() as ctx:
        def sb(name, shape, dt=F32, stack=ctx):
            return stack.enter_context(nc.sbuf_tensor(name, shape, dt))

        def sem(name):
            return ctx.enter_context(nc.semaphore(name))

        hT_hi = sb("hT_hi", [P, KT, SEQ], F32R)
        hT_lo = sb("hT_lo", [P, KT, SEQ], F32R)
        w_raw = sb("w_raw", [P, 2, 512])
        w_hi = sb("w_hi", [P, 4, 512], F32R)
        w_lo = sb("w_lo", [P, 4, 512], F32R)
        mkh = sb("mkh", [P, N_MEM, MEM], F32R)
        mkl = sb("mkl", [P, N_MEM // 2, MEM], F32R)
        mv = sb("mv", [P, N_MEM, MEM // P, P], F32R)
        ident = sb("ident", [P, P])
        pad = sb("pad", [P, 2])
        nw = sb("nw", [P, 2])
        negmax = sb("negmax", [P, NBLK])
        den = sb("den", [P, NBLK])
        rden = sb("rden", [P, NBLK])
        with ExitStack() as ph:
            xs = sb("xs", [P, 7, D], F32, ph)
            nwT = sb("nwT", [P, 2, KT], F32, ph)
            st = sb("st", [P, 4, 10], F32, ph)
            rel_sb = sb("rel_sb", [BUCKETS + 1, N_DIL], F32, ph)
            vtm = sb("vtm", [P, MEM], F32, ph)
        with ExitStack() as ph:
            kh = sb("kh", [P, 2, SEQ], F32R, ph)
            kl = sb("kl", [P, SEQ], F32R, ph)
            vv = sb("vv", [P, 2, NBLK, P], F32R, ph)
            tab = sb("tab", [P, 2, SEQ], F32, ph)
            qs = sb("qs", [P, 2, SEQ], F32R, ph)
            pT_hi = sb("pT_hi", [P, 2, 512], F32R, ph)
            pT_lo = sb("pT_lo", [P, 2, 512], F32R, ph)
            sc = sb("sc", [P, 2, SEQ], F32, ph)
            gate = sb("gate", [P, SEQ], F32, ph)
            mixb = sb("mixb", [P, SEQ], F32, ph)
            otmp = sb("otmp", [P, HALF], F32, ph)
        with ExitStack() as ph:
            ggate = sb("ggate", [P, 2, SEQ], F32, ph)
            gq = sb("gq", [P, SEQ], F32, ph)
            gk = sb("gk", [P, SEQ], F32, ph)
            bcum = sb("bcum", [P, SEQ], F32, ph)
            e1 = sb("e1", [P, SEQ], F32, ph)
            e2 = sb("e2", [P, SEQ], F32, ph)
            ks = sb("ks", [P, NBLK, P], F32, ph)
            gv = sb("gv", [P, NBLK, DV], F32, ph)
            am = sb("am", [P, 2, P], F32, ph)
            state = sb("state", [P, 4, DV], F32, ph)
            osb = sb("osb", [P, NBLK, DV], F32, ph)
            mixo = sb("mixo", [P, 2, HALF], F32, ph)
            lrT = sb("lrT", [RANK, SEQ], F32, ph)
            w2h = sb("w2h", [RANK, P], F32, ph)
            bgh = sb("bgh", [P, 1], F32, ph)
            ones = sb("ones", [P, CHUNK], F32, ph)
            amask = sb("amask", [P, P], I32, ph)
            dec = sb("dec", [P, 2 * NBLK], F32, ph)
            gst = sb("gst", [P, 4, NBLK], F32, ph)
        with ExitStack() as ph:
            stg = sb("stg", [P, 4, HALF], F32, ph)
            wpost = sb("wpost", [P, D], F32, ph)
            xr = sb("xr", [P, 3, D // 2], F32, ph)
            y = sb("y", [P, 4, D], F32, ph)
            ssy = sb("ssy", [P, 4, 4], F32, ph)
            yst = sb("yst", [P, 4, 4], F32, ph)
        tab_sb = xs[0:BUCKETS + 1, 5, 0:TABLE]
        brow = xs[0:N_DIL, 6, 0:TABLE]

        ps = ctx.enter_context(nc.psum_tensor("ps", [P, 8, 512], F32))
        L, TB, OB = 4, 6, 7

        raw_landed = [sem("raw_landed0"), sem("raw_landed1")]
        hi_done, lo_done = sem("hi_done"), sem("lo_done")
        unit_used = sem("unit_used")
        evac_act, evac_dve = sem("evac_act"), sem("evac_dve")
        s_id = sem("s_id")
        s_small = sem("s_small")
        s_rel = sem("s_rel")
        s_bias, s_biasc, s_biasw, s_rep = sem("s_bias"), sem("s_biasc"), sem("s_biasw"), sem("s_rep")
        x_in = [sem(f"x_in{i}") for i in range(7)]
        x_sq, x_v, x_sqrt, x_rc, x_scaled = sem("x_sq"), sem("x_v"), sem("x_sqrt"), sem("x_rc"), sem("x_scaled")
        x_turned, x_hi, x_lo = sem("x_turned"), sem("x_hi"), sem("x_lo")
        v_turned, v_act, v_dve = sem("v_turned"), sem("v_act"), sem("v_dve")
        keys_a = sem("keys_a")
        lo_a = sem("lo_a")
        carried = sem("carried")
        J = {kind: {n: sem(f"{kind}_{n}") for n in (
            "logits", "negmax", "exps", "rden", "probs", "turned", "hi", "lo", "half", "ocopy", "osum")}
            for kind in ("dil", "mem")}
        tab_landed = [sem("tab_landed0"), sem("tab_landed1")]
        gated, mix_stored = sem("gated"), sem("mix_stored")
        g_par, g_z, g_abs, g_exp, g_min, g_ln, g_la, g_scan, g_rest = (sem(n) for n in (
            "g_par", "g_z", "g_abs", "g_exp", "g_min", "g_ln", "g_la", "g_scan", "g_rest"))
        g_e1, g_qt, g_e2, g_kt, g_e3, g_ks = (sem(n) for n in ("g_e1", "g_qt", "g_e2", "g_kt", "g_e3", "g_ks"))
        g_kturned, g_kcopied, g_a, g_am, g_kv, g_st = (sem(n) for n in (
            "g_kturned", "g_kcopied", "g_a", "g_am", "g_kv", "g_st"))
        g_o, g_ocopied, g_v, g_sqrt, g_scaled = (sem(n) for n in ("g_o", "g_ocopied", "g_v", "g_sqrt", "g_scaled"))
        g_turned, g_mixo, g_rc = sem("g_turned"), sem("g_mixo"), sem("g_rc")
        g_stored = [sem("g_stored0"), sem("g_stored1")]
        g_zero = sem("g_zero")
        stg_in = [sem(f"stg_in{i}") for i in range(4)]
        m_hi, m_lo = sem("m_hi"), sem("m_lo")
        y_done, y_copied, y_sq = sem("y_done"), sem("y_copied"), sem("y_sq")
        y_sum, y_sqrt, y_out = sem("y_sum"), sem("y_sqrt"), sem("y_out")
        xr_in = [sem(f"xr_in{i}") for i in range(3)]
        wpost_in, y_rc = sem("wpost_in"), sem("y_rc")
        out_stored = sem("out_stored")

        def proj(par, a=0, b=P, n=SEQ):
            return ps[a:b, 2 * par:2 * par + 2, :].rearrange("p a b -> p (a b)")[:, 0:n]

        def logits(i, w):
            bank = i % 2 if w <= 512 else 0
            return ps[:, L:L + 2, :].rearrange("p a b -> p (a b)")[:, bank * 512:bank * 512 + w]

        def r32(ap):
            return ap.bitcast(F32)

        block = ctx.enter_context(nc.Block())

        @block.sync
        def _(sp):
            def unit(T, j, src):
                if not (isinstance(T, int) and 4 * T + j < 2):
                    sp.wait_ge(lo_done, 4 * T + j - 1)
                sp.dma_start(w_raw[:, j % 2, :].rearrange("p (k c) -> p k c", c=src.shape[-1]), src).then_inc(raw_landed[j % 2], 16)

            def tile(T, w, col):
                v = w.rearrange("(k p) c -> p k c", p=P)
                for j in range(4):
                    unit(T, j, v[:, 4 * j:4 * j + 4, bass.ds(col, P)])

            for n in range(10):
                src = mem[n * P:(n + 1) * P, :] if n < 2 else x[(n - 2) * P:(n - 1) * P, :]
                if n >= 7:
                    sp.wait_ge(x_turned, KT if n < 9 else 2 * KT)
                if n == 5:
                    sp.wait_ge(s_bias, 1)
                if n == 6:
                    sp.wait_ge(s_biasw, 16)
                sp.dma_start(xs[:, n % 7, :], src).then_inc(x_in[n % 7], 16)
                if n == 6:
                    tile(0, w_mem_kv, 0)
            for T in range(1, 4):
                tile(T, w_mem_kv, T * P)
            tile(T_LR, w_in, C_LR)
            tile(T_GV0, w_in, C_GV)
            for h in range(N_DIL):
                sp.dma_start(bias_tables[h].rearrange("(p n) -> p n", n=TABLE),
                             bias_rows[h:h + 1, :].to_broadcast([P, TABLE])).then_inc(s_rep, 16)

            def gla_params(h):
                sp.dma_start(w2h[:, :], w_gate2[:, bass.ds(h * P, P)]).then_inc(g_par, 16)
                sp.dma_start(bgh[:, :], b_gla_gate[0:1, bass.ds(h * P, P)].rearrange("a p -> p a")).then_inc(g_par, 16)

            def gla_tiles(h, T):
                tile(T, w_in, C_GV + P + h * DV)
                tile(T + 1, w_in, C_GK + h * P)
                tile(T + 2, w_in, C_GQ + h * P)
                tile(T + 3, w_in, C_GATE + X_GLA * P + h * (2 * P))
                tile(T + 4, w_in, C_GATE + (X_GLA + 1) * P + h * (2 * P))

            sp.wait_ge(x_turned, 3 * KT)
            gla_params(0)
            with sp.Fori(0, N_GLA - 1) as h:
                gla_tiles(h, T_G + 6 * h)
                sp.wait_ge(g_min, h + 1)
                gla_params(h + 1)
                tile(T_G + 6 * h + 5, w_in, C_GV + DV + h * DV)
            gla_tiles(N_GLA - 1, T_G + 6 * (N_GLA - 1))
            tile(T_DV0, w_in, C_DV)

            def tables(g):
                for hd in range(2):
                    src = bias_tables[bass.ds(2 * g + hd, 1), P - 1:P - 1 + P * (TABLE - 1)]
                    src = src.rearrange("a (p n) -> (a p) n", n=TABLE - 1)[:, 0:SEQ]
                    sp.dma_start(tab[:, hd, :], src).then_inc(tab_landed[hd], 16)

            tile(T_D, w_in, C_DK)
            sp.wait_ge(s_rep, 16 * N_DIL)
            sp.wait_ge(g_mixo, 4 * N_GLA)
            tables(0)
            with sp.Fori(0, N_DIL // 2 - 1) as g:
                T = T_D + 4 * g
                tile(T + 1, w_in, C_DQ + g * P)
                tile(T + 2, w_in, C_GATE + X_DIL * P + g * P)
                tile(T + 3, w_in, C_DV + P + g * P)
                tile(T + 4, w_in, C_DK + P + g * P)
                sp.wait_ge(J["dil"]["negmax"], 2 * NBLK * g + 2 * NBLK)
                tables(g + 1)
            gl = N_DIL // 2 - 1
            tile(T_D + 4 * gl + 1, w_in, C_DQ + gl * P)
            tile(T_D + 4 * gl + 2, w_in, C_GATE + (X_DIL + gl) * P)
            for j in range(2):
                tile(T_MQ0 + 2 * j, w_in, C_MQ + j * P)
                tile(T_MQ0 + 2 * j + 1, w_in, C_GATE + (X_MEM + j) * P)

            def piece(n):
                hf, k = PIECES[n]
                if n >= 4:
                    sp.wait_ge(m_lo, piece_no(n - 4))
                if n < KT - 2:
                    sp.wait_ge(mix_stored, 16 * (min(n, N_DIL // 2 - 1) + 2))
                else:
                    sp.wait_ge(mix_stored, 16 * (N_DIL // 2 + 2))
                sp.dma_start(stg[:, n % 4, :], mix[k * P:(k + 1) * P, hf * HALF:(hf + 1) * HALF]).then_inc(stg_in[n % 4], 16)

            def out_unit(c, k):
                u = UNIT_NO[c, k]
                sp.wait_ge(lo_done, u - 1)
                sp.dma_start(w_raw[:, u % 2, :], w_out[k * P:(k + 1) * P, c % 4 * 512:(c % 4 + 1) * 512]).then_inc(raw_landed[u % 2], 16)

            def residual(n):
                if n >= 3:
                    sp.wait_ge(y_out, n - 2)
                sp.dma_start(xr[:, n % 3, :], x[n // 2 * P:(n // 2 + 1) * P, n % 2 * 1024:(n % 2 + 1) * 1024]).then_inc(xr_in[n % 3], 16)

            for q in range(2):
                sp.wait_ge(g_stored[q], 32 * N_GLA)
            sp.wait_ge(mix_stored, 16 * (N_DIL // 2 + 1))
            for k in range(KT):
                if k in (4, 8, 12):
                    out_unit(0, k // 4 - 1)
                for n in pieces_at(-1, k):
                    piece(n)
            out_unit(0, 3)
            for c in range(CHUNKS):
                for k in range(KT):
                    for unit_ in splits_at(c, k):
                        out_unit(*unit_)
                    for n in pieces_at(c, k):
                        piece(n)
                    if c == 0 and k == KT // 2:
                        sp.dma_start(wpost[:, :], norm_post_w[0:1, :].to_broadcast([P, D])).then_inc(wpost_in, 16)
                    if c == 3 and k >= KT - 3:
                        residual(k - (KT - 3))
                    if c == 4 and k >= 5 and k - 2 < 8:
                        residual(k - 2)
            for n in range(8, 16):
                residual(n)

        @block.gpsimd
        def _(pool):
            pool.memset(ident[:, :], 0.0).then_inc(s_id, 1)
            pool.memset(rel_sb[:, :], 1.0).then_inc(s_id, 1)
            pool.wait_ge(s_id, 2)
            pool.affine_select(out=ident[:, :], in_=ident[:, :], compare_op=ALU.not_equal, fill=1.0, base=0,
                               pattern=[[-1, P]], channel_multiplier=1).then_inc(s_id, 1)
            pool.sem_inc(mix_stored, 16)
            pool.wait_ge(x_turned, 3 * KT)
            pool.memset(amask[:, :], 1).then_inc(g_zero, 1)
            pool.memset(am[:, :, :], 0.0).then_inc(g_zero, 1)
            pool.memset(ones[:, :], 1.0).then_inc(g_zero, 1)
            pool.wait_ge(g_zero, 3)
            pool.affine_select(out=amask[:, :], in_=amask[:, :], compare_op=ALU.is_ge, fill=0.0, base=0,
                               pattern=[[1, P]], channel_multiplier=-1).then_inc(g_zero, 1)
            pool.wait_ge(g_zero, 4)
            pool.affine_select(out=amask[:, CHUNK:P], in_=amask[:, CHUNK:P], compare_op=ALU.is_ge, fill=0.0,
                               base=-CHUNK, pattern=[[0, CHUNK]], channel_multiplier=1).then_inc(g_zero, 1)

            def gate_pair(kind, g, tiles):
                pool.wait_ge(J[kind]["osum"], 4 * g + 4)
                pool.wait_ge(evac_act, tiles)
                pool.tensor_tensor(mixb[:, :], mixb[:, :], gate[:, :], ALU.mult).then_inc(gated, 1)

            with pool.Fori(0, N_DIL // 2) as g:
                gate_pair("dil", g, T_D + 4 * g + 3)
            for j in range(2):
                gate_pair("mem", j, T_MQ0 + 2 * j + 2)

        @block.scalar
        def _(act):
            def split(T, j):
                act.wait_ge(raw_landed[j % 2], 16 * (2 * T + j // 2 + 1))
                if not isinstance(T, int) or T > 0:
                    act.wait_ge(unit_used, 4 * T + j - 3)
                act.activation(w_hi[:, j % 4, :], w_raw[:, j % 2, :], ACT.Copy).then_inc(hi_done, 1)

            def tile(T, par, kind, job=None, arg=None):
                for k in range(KT):
                    if k in (4, 8, 12):
                        split(T + 1, k // 4 - 1)
                    if job:
                        job(k)
                act.wait_ge(unit_used, 4 * T + 4)
                kind(T, par, arg)
                split(T + 1, 3)

            act.dma_start(nwT[:, 0, :], mem_norm_w.rearrange("a (k p) -> p (a k)", p=P)).then_inc(s_small, 16)
            act.dma_start(nwT[:, 1, :], norm_pre_w.rearrange("a (k p) -> p (a k)", p=P)).then_inc(s_small, 16)
            act.dma_start(nw[:, :], gla_norm_w.rearrange("a (k p) -> p (a k)", p=P)).then_inc(s_small, 16)
            act.dma_start(tab_sb, dist_table).then_inc(s_rel, 16)
            act.wait_ge(s_id, 2)
            act.dma_start(rel_sb[0:BUCKETS, :], rel_bias).then_inc(s_rel, 16)
            act.wait_ge(s_bias, 1)
            act.activation(brow, ps[0:N_DIL, L:L + 3, :].rearrange("p a b -> p (a b)")[:, 0:TABLE], ACT.Copy).then_inc(s_biasc, 1)
            act.wait_ge(s_biasc, 1)
            act.dma_start(bias_rows, brow).then_inc(s_biasw, 16)

            def squares(n):
                act.wait_ge(x_in[n % 7], 16 * (n // 7 + 1))
                if n > 0:
                    act.wait_ge(x_sq, n)
                act.activation(ps[:, 0:4, :].rearrange("p a b -> p (a b)"), xs[:, n % 7, :], ACT.Square,
                               accum_out=st[:, 0, n:n + 1]).then_inc(x_sq, 1)

            def root(q, lo, hi):
                act.wait_ge(x_v, q + 1)
                act.activation(st[:, 1, lo:hi], st[:, 0, lo:hi], ACT.Sqrt).then_inc(x_sqrt, 1)

            def turn_hi(q, base, width, w):
                for k in range(KT):
                    n = KT * q + k
                    act.wait_ge(x_turned, n + 1)
                    act.activation(hT_hi[:, k, base:base + width], ps[:, L + k % 4, 0:width], ACT.Copy,
                                   scale=nwT[:, w, k:k + 1]).then_inc(x_hi, 1)

            act.wait_ge(s_small, 48)
            for n in (0, 1):
                squares(n)
            root(0, 0, 2)
            turn_hi(0, 512, MEM, 0)
            for n in range(2, 6):
                squares(n)
            root(1, 2, 6)
            for j in range(4):
                split(0, j)
            turn_hi(1, 0, HALF, 1)

            def stacked_hi(dst_a, dst_b, par, n):
                for dst, r, ready in ((dst_a, slice(0, DH), keys_a), (dst_b, slice(DH, P), evac_act)):
                    act.activation(dst[0:DH, :], proj(par, r.start, r.stop, n), ACT.Copy)
                    act.activation(dst[DH:P, :], proj(par, r.start, r.stop, n), ACT.Copy).then_inc(ready, 1)

            def ev_mk(T, par, j):
                stacked_hi(mkh[:, 2 * j, :], mkh[:, 2 * j + 1, :], par, MEM)

            def ev_mv(T, par, j):
                if j > 0:
                    act.wait_ge(v_turned, j)
                act.activation(vtm[:, :], proj(par, 0, P, MEM), ACT.Copy).then_inc(evac_act, 1)
                act.wait_ge(v_turned, j + 1)
                act.activation(mv[:, 2 * j:2 * j + 2, :, 0:DH],
                               ps[:, TB, 0:MEM].rearrange("p (b h c) -> p h b c", h=2, c=DH), ACT.Copy).then_inc(v_act, 1)

            def ev_lr(T, par, _):
                act.activation(lrT[:, 0:HALF], ps[0:RANK, 2 * par, :], ACT.Copy).then_inc(evac_act, 1)

            def ev_copy(T, par, dst):
                act.activation(dst[:, 0:HALF], ps[:, 2 * par, :], ACT.Copy).then_inc(evac_act, 1)

            def ev_gate(T, par, dst):
                act.activation(dst, proj(par), ACT.Silu).then_inc(evac_act, 1)

            def ev_kd(T, par, _):
                stacked_hi(kh[:, 0, :], kh[:, 1, :], par, SEQ)

            def ev_qd(T, par, _):
                for hd, r, ready in ((0, slice(0, DH), keys_a), (1, slice(DH, P), evac_act)):
                    act.activation(qs[r, hd, :], proj(par, r.start, r.stop), ACT.Copy, scale=-DH ** -0.5).then_inc(ready, 1)

            def gla_v(first, j):
                def job(k):
                    if k == VALUES_AT + 1:
                        act.wait_ge(v_turned, first + 1)
                        act.activation(gv[:, 0:4, j * P:(j + 1) * P], ps[:, TB, :].rearrange("p (b c) -> p b c", c=P), ACT.Copy).then_inc(v_act, 1)
                return job

            def dil_v(first):
                def job(k):
                    if k in (VALUES_AT, VALUES_AT + 1):
                        q = k - VALUES_AT
                        act.wait_ge(v_turned, first + q + 1)
                        act.activation(vv[:, :, 4 * q:4 * q + 4, 0:DH],
                                       ps[:, TB, :].rearrange("p (b h c) -> p h b c", h=2, c=DH), ACT.Copy).then_inc(v_act, 1)
                return job

            def soft(kind, a, hd, width):
                s = J[kind]
                causal = kind == "dil"
                ng = NG if causal else NBLK
                groups = GROUPS if causal else [(i, 0, 2) for i in range(NBLK)]

                def exps(i):
                    w = width(i)
                    act.wait_ge(s["negmax"], NBLK * a + i + 1)
                    src = sc[:, i % 2, 0:w] if causal else logits(i, w)
                    act.activation(sc[:, i % 2, 0:w], src, ACT.Exp, bias=negmax[:, i:i + 1], scale=-1.0,
                                   accum_out=den[:, i:i + 1]).then_inc(s["exps"], 1)

                def hi(n):
                    i, j, nb = groups[n]
                    act.wait_ge(s["turned"], ng * a + n + 1)
                    act.activation(pT_hi[:, n % 2, 0:nb * P], ps[:, TB, 0:nb * P], ACT.Copy).then_inc(s["hi"], 1)

                def half(q):
                    r = slice(hd * DH, hd * DH + DH)
                    act.wait_ge(s["half"], 2 * a + q + 1)
                    act.activation(otmp[r, :], ps[DH:P, OB, :], ACT.Copy).then_inc(s["ocopy"], 1)

                return exps, hi, half

            def causal_job(g, part):
                def job(k):
                    for hd in range(2):
                        exps, hi, half = soft("dil", 2 * g + hd, hd, lambda i: (i + 1) * P)
                        r = k + 16 * part - START[hd]
                        if r in TURN_AT:
                            hi(TURN_AT[r])
                        if r in HALF_AT:
                            half(HALF_AT[r])
                        if r - 1 in QK_AT:
                            exps(QK_AT[r - 1])
                return job

            def mem_job(j, part):
                def parts(n):
                    return soft("mem", 2 * j + n // NBLK, n // NBLK, lambda i: MEM)

                def job(k):
                    r = k + 16 * part
                    if r in MEM_TURN_AT:
                        n = MEM_TURN_AT[r]
                        parts(n)[1](n % NBLK)
                    if r in MEM_HALF_AT:
                        q = MEM_HALF_AT[r]
                        parts(4 * q)[2](q % 2)
                    if r in MEM_QK_AT:
                        n = MEM_QK_AT[r]
                        parts(n)[0](n % NBLK)
                return job

            def store_mix(n, group):
                act.wait_ge(gated, n)
                act.dma_start(mix[bass.ds(group * P, P), :], mixb[:, :]).then_inc(mix_stored, 16)

            def gla(h, part):
                def job(k0):
                    k = k0 + 16 * part
                    if k == 0:
                        act.wait_ge(g_par, 32 * h + 32)
                        act.wait_ge(g_z, h + 1)
                        act.activation(e1[:, :], ps[:, L:L + 2, :].rearrange("p a b -> p (a b)"), ACT.Abs, bias=bgh[:, 0:1]).then_inc(g_abs, 1)
                        act.wait_ge(g_abs, h + 1)
                        act.activation(e1[:, :], e1[:, :], ACT.Exp, scale=-1.0).then_inc(g_exp, 1)
                        act.wait_ge(g_exp, h + 1)
                        act.activation(e1[:, :], e1[:, :], ACT.Ln, bias=1.0).then_inc(g_ln, 1)
                    if k == 5:
                        act.wait_ge(g_scan, h + 1)
                        act.activation(e1[:, :], bcum[:, :], ACT.Exp, scale=1.0 / TAU).then_inc(g_e1, 1)
                        act.wait_ge(g_rest, h + 1)
                        act.activation(e2[:, :], e2[:, :], ACT.Exp, scale=1.0 / TAU).then_inc(g_e3, 1)
                        act.wait_ge(g_qt, h + 1)
                        act.activation(e1[:, :], bcum[:, :], ACT.Exp, scale=-1.0 / TAU).then_inc(g_e2, 1)
                    if k in (10, 11):
                        q = k - 10
                        act.wait_ge(g_kturned, 2 * h + q + 1)
                        act.activation(ks[:, 4 * q:4 * q + 4, :], ps[:, TB, :].rearrange("p (b c) -> p b c", c=P), ACT.Copy).then_inc(g_kcopied, 1)
                    if 13 <= k < 29 and k % 2 == 1:
                        i = (k - 13) // 2
                        act.wait_ge(g_o, 8 * h + i + 1)
                        act.activation(osb[:, i, :], ps[:, OB, 0:DV], ACT.Copy)
                        act.activation(e1[:, 0:DV], ps[:, OB, 0:DV], ACT.Square, accum_out=gst[:, 0, i:i + 1]).then_inc(g_ocopied, 1)
                    if k == 28:
                        act.wait_ge(g_v, h + 1)
                        act.activation(gst[:, 2, :], gst[:, 1, :], ACT.Sqrt).then_inc(g_sqrt, 1)
                    if 32 <= k < 36:
                        q = k - 32
                        act.wait_ge(g_mixo, 4 * h + q + 1)
                        rows = bass.ds((X_GLA + q // 2) * P + h * (2 * P), P)
                        act.dma_start(mix[rows, (q % 2) * HALF:(q % 2 + 1) * HALF], mixo[:, q % 2, :]).then_inc(g_stored[q % 2], 16)
                    if k == 47:
                        for q in range(2):
                            act.wait_ge(g_stored[q], 32 * h + 32)
                return job

            for T in range(2):
                tile(T, T % 2, ev_mk, None, T)
            for T in range(2, 4):
                tile(T, T % 2, ev_mv, None, T - 2)
            for n in range(6, 10):
                act.wait_ge(evac_dve, 4)
                squares(n)
            root(2, 6, 10)
            turn_hi(2, HALF, HALF, 1)

            tile(T_LR, T_LR % 2, ev_lr)
            tile(T_GV0, T_GV0 % 2, ev_copy, None, e2)

            def gla_head(h, last):
                T = T_G + 6 * h
                tile(T, 0, ev_copy, gla_v(2 + 4 * h, 0), e2)
                tile(T + 1, 1, ev_copy, gla_v(4 + 4 * h, 1), gk)
                tile(T + 2, 0, ev_copy, None, gq)
                tile(T + 3, 1, ev_gate, gla(h, 0), ggate[:, 0, :])
                tile(T + 4, 0, ev_gate, gla(h, 1), ggate[:, 1, :])
                tile(T + 5, 1, ev_copy, gla(h, 2), sc[:, 0, :] if last else e2)

            with act.Fori(0, N_GLA - 1) as h:
                gla_head(h, False)
            gla_head(N_GLA - 1, True)

            V0 = 2 + 4 * N_GLA

            def dil_pair(g, T, last):
                tile(T, 0, ev_kd, dil_v(V0 + 2 * g))
                tile(T + 1, 1, ev_qd)
                tile(T + 2, 0, ev_gate, causal_job(g, 0), gate[:, :])
                if last:
                    tile(T + 3, 1, ev_qd, causal_job(g, 1))
                else:
                    tile(T + 3, 1, ev_copy, causal_job(g, 1), sc[:, 0, :])
                store_mix(g + 1, X_DIL + g)

            with act.Fori(0, N_DIL // 2 - 1) as g:
                dil_pair(g, T_D + 4 * g, False)
            dil_pair(N_DIL // 2 - 1, T_D + 4 * (N_DIL // 2 - 1), True)
            tile(T_MQ0 + 1, (T_MQ0 + 1) % 2, ev_gate, mem_job(0, 0), gate[:, :])
            tile(T_MQ0 + 2, T_MQ0 % 2, ev_qd, mem_job(0, 1))
            store_mix(N_DIL // 2 + 1, X_MEM)

            def osplit(c, k):
                u = UNIT_NO[c, k]
                act.wait_ge(raw_landed[u % 2], 16 * (u // 2 + 1))
                if c < CHUNKS - 1:
                    act.wait_ge(unit_used, 4 * T_END + 16 * c + k - 3)
                    dst = w_hi[:, k % 4, :]
                else:
                    dst = hT_hi[:, k, 0:HALF]
                act.activation(dst, w_raw[:, u % 2, :], ACT.Copy).then_inc(hi_done, 1)

            def piece(n):
                hf, k = PIECES[n]
                act.wait_ge(stg_in[n % 4], 16 * (n // 4 + 1))
                act.wait_ge(unit_used, 4 * (T_END - 1) + k // 4 + 1)
                act.activation(hT_hi[:, k, hf * HALF:(hf + 1) * HALF], stg[:, n % 4, :], ACT.Copy).then_inc(m_hi, 1)

            def direct():
                act.wait_ge(gated, N_DIL // 2 + 2)
                for hf in range(2):
                    r = slice(hf * HALF, (hf + 1) * HALF)
                    act.activation(hT_hi[:, KT - 1, r], mixb[:, r], ACT.Copy).then_inc(m_hi, 1)

            def y_squares(c, m):
                act.wait_ge(y_copied, 4 * c + m + 1)
                b = ps[:, 4 * (c % 2) + m, :]
                act.activation(b, b, ACT.Square, accum_out=ssy[:, m, c % 4:c % 4 + 1]).then_inc(y_sq, 1)

            def root(q, lo, hi):
                act.wait_ge(y_sum, q + 1)
                act.activation(yst[:, 1, lo:hi], yst[:, 0, lo:hi], ACT.Sqrt).then_inc(y_sqrt, 1)

            def store(hf, m, c0, c1):
                row = (4 * hf + m) * P
                act.wait_ge(y_out, 8 * hf + 2 * m + c1)
                r = slice(c0 * 1024, c1 * 1024)
                act.dma_start(out[row:row + P, r], y[:, m, r]).then_inc(out_stored, 16)

            mem_job_1 = mem_job(1, 0)

            def last_tile_job(k):
                mem_job_1(k)
                for n in pieces_at(-1, k):
                    piece(n)

            tile(T_MQ0 + 3, (T_MQ0 + 1) % 2, ev_gate, last_tile_job, gate[:, :])
            for c in range(CHUNKS - 1):
                for k in range(KT):
                    for unit_ in splits_at(c, k):
                        osplit(*unit_)
                    for n in pieces_at(c, k):
                        piece(n)
                    if c == 0:
                        mem_job(1, 1)(k)
                        if k == DIRECT_AT:
                            direct()
                    if c == 4:
                        if k == 0:
                            root(0, 0, 4)
                        if k in (5, 7, 9, 11):
                            store(0, (k - 5) // 2, 0, 2)
                for m in range(4):
                    y_squares(c, m)
            for m in range(4):
                y_squares(CHUNKS - 1, m)
                root(1 + m, m, m + 1)
                for c in range(2):
                    store(1, m, c, c + 1)
            act.wait_ge(out_stored, 16 * 12)

        @block.vector
        def _(dve):
            def carry(s, n):
                dve.wait_ge(s, n)
                dve.sem_inc(carried, 1)

            def split(T, j):
                dve.wait_ge(hi_done, 4 * T + j + 1)
                dve.tensor_tensor(w_lo[:, j % 4, :], w_raw[:, j % 2, :], r32(w_hi[:, j % 4, :]), ALU.subtract).then_inc(lo_done, 1)

            def tile(T, par, kind, job=None, arg=None):
                for k in range(KT):
                    if k in (4, 8, 12):
                        split(T + 1, k // 4 - 1)
                    if job:
                        job(k)
                dve.wait_ge(unit_used, 4 * T + 4)
                kind(T, par, arg)
                split(T + 1, 3)

            def inverse_root(v, root, t, out_, chain, c0):
                dve.reciprocal(out_, root).then_inc(chain, 1)
                dve.wait_ge(chain, c0 + 1)
                dve.tensor_tensor(t, out_, v, ALU.mult).then_inc(chain, 1)
                dve.wait_ge(chain, c0 + 2)
                dve.scalar_tensor_tensor(t, t, -0.5, out_, ALU.mult, ALU.mult).then_inc(chain, 1)
                dve.wait_ge(chain, c0 + 3)
                dve.scalar_tensor_tensor(out_, t, 1.5, out_, ALU.add, ALU.mult).then_inc(chain, 1)
                dve.wait_ge(chain, c0 + 4)

            def scale_rows(q, lo, hi):
                dve.wait_ge(x_sq, hi)
                dve.tensor_scalar(st[:, 0, lo:hi], st[:, 0, lo:hi], 1.0 / D, EPS, ALU.mult, ALU.add).then_inc(x_v, 1)
                dve.wait_ge(x_sqrt, q + 1)
                inverse_root(st[:, 0, lo:hi], st[:, 1, lo:hi], st[:, 3, lo:hi], st[:, 2, lo:hi], x_rc, 4 * q)
                for n in range(lo, hi):
                    dve.tensor_scalar(xs[:, n % 7, :], xs[:, n % 7, :], st[:, 2, n:n + 1], None, ALU.mult).then_inc(x_scaled, 1)

            def turn_lo(q, base, width, w):
                for k in range(KT):
                    n = KT * q + k
                    dve.wait_ge(x_hi, n + 1)
                    dve.scalar_tensor_tensor(hT_lo[:, k, base:base + width], ps[:, L + k % 4, 0:width], nwT[:, w, k:k + 1],
                                             r32(hT_hi[:, k, base:base + width]), ALU.mult, ALU.subtract).then_inc(x_lo, 1)

            dve.wait_ge(s_small, 48)
            scale_rows(0, 0, 2)
            turn_lo(0, 512, MEM, 0)
            scale_rows(1, 2, 6)
            for j in range(4):
                split(0, j)
            turn_lo(1, 0, HALF, 1)

            def stacked_lo(T, dst, hi_a, hi_b, par, n, count):
                for r, hi, ready, c, done in ((slice(0, DH), hi_a, keys_a, count, lo_a), (slice(DH, P), hi_b, evac_act, T + 1, evac_dve)):
                    dve.wait_ge(ready, c)
                    dve.tensor_tensor(dst[r, :], proj(par, r.start, r.stop, n), r32(hi[r, :]), ALU.subtract).then_inc(done, 1)

            def ev_mk(T, par, j):
                stacked_lo(T, mkl[:, j, :], mkh[:, 2 * j, :], mkh[:, 2 * j + 1, :], par, MEM, j + 1)

            def ev_mv(T, par, j):
                dve.wait_ge(v_act, j + 1)
                v = mv[:, 2 * j:2 * j + 2, :, :]
                dve.tensor_tensor(v[:, :, :, DH:P], ps[:, TB, 0:MEM].rearrange("p (b h c) -> p h b c", h=2, c=DH),
                                  r32(v[:, :, :, 0:DH]), ALU.subtract).then_inc(v_dve, 1)
                dve.sem_inc(evac_dve, 1)

            def ev_lr(T, par, _):
                dve.tensor_copy(lrT[:, HALF:SEQ], ps[0:RANK, 2 * par + 1, :]).then_inc(evac_dve, 1)

            def ev_copy(T, par, dst):
                dve.tensor_copy(dst[:, HALF:SEQ], ps[:, 2 * par + 1, :]).then_inc(evac_dve, 1)

            def ev_none(T, par, _):
                dve.sem_inc(evac_dve, 1)

            def ev_kd(T, par, count):
                stacked_lo(T, kl, kh[:, 0, :], kh[:, 1, :], par, SEQ, count)

            def ev_qd(T, par, count):
                for hd, r, o, ready, c, done in ((0, slice(0, DH), slice(DH, P), keys_a, count, lo_a),
                                                 (1, slice(DH, P), slice(0, DH), evac_act, T + 1, evac_dve)):
                    dve.wait_ge(ready, c)
                    dve.scalar_tensor_tensor(qs[o, hd, :], proj(par, r.start, r.stop), -DH ** -0.5, r32(qs[r, hd, :]),
                                             ALU.mult, ALU.subtract).then_inc(done, 1)

            def gla_v(first, j):
                def job(k):
                    if k == VALUES_AT + 1:
                        dve.wait_ge(v_turned, first + 2)
                        dve.tensor_copy(gv[:, 4:8, j * P:(j + 1) * P], ps[:, TB, :].rearrange("p (b c) -> p b c", c=P)).then_inc(v_dve, 1)
                return job

            def dil_v(before):
                def job(k):
                    if k in (VALUES_AT, VALUES_AT + 1):
                        q = k - VALUES_AT
                        dve.wait_ge(v_act, before + q + 1)
                        v = vv[:, :, 4 * q:4 * q + 4, :]
                        dve.tensor_tensor(v[:, :, :, DH:P], ps[:, TB, :].rearrange("p (b h c) -> p h b c", h=2, c=DH),
                                          r32(v[:, :, :, 0:DH]), ALU.subtract).then_inc(v_dve, 1)
                return job

            def soft(kind, a, hd, width, pairs):
                s = J[kind]
                causal = kind == "dil"
                groups = GROUPS if causal else [(i, 0, 2) for i in range(NBLK)]
                ng = len(groups)

                def scores(i):
                    w = width(i)
                    if causal:
                        if i >= 2:
                            carry(s["turned"], ng * a + len([g for g in groups if g[0] <= i - 2]))
                        elif hd == 1:
                            carry(s["turned"], ng * a - len([g for g in groups if g[0] > i + NBLK - 2]))
                        carry(s["logits"], NBLK * a + i + 1)
                        if i == 0:
                            carry(tab_landed[hd], pairs)
                        dve.tensor_tensor_reduce(sc[:, i % 2, 0:w], logits(i, w), tab[:, hd, SEQ - w:SEQ], 1.0, 3e38,
                                                 ALU.add, ALU.min, negmax[:, i:i + 1]).then_inc(s["negmax"], 1)
                    else:
                        dve.wait_ge(s["logits"], NBLK * a + i + 1)
                        dve.tensor_reduce(negmax[:, i:i + 1], logits(i, w), AXX, ALU.min).then_inc(s["negmax"], 1)

                def norm(i):
                    w = width(i)
                    dve.wait_ge(s["exps"], NBLK * a + i + 1)
                    dve.reciprocal(rden[:, i:i + 1], den[:, i:i + 1]).then_inc(s["rden"], 1)
                    dve.wait_ge(s["rden"], NBLK * a + i + 1)
                    dve.tensor_scalar(sc[:, i % 2, 0:w], sc[:, i % 2, 0:w], rden[:, i:i + 1], None, ALU.mult).then_inc(s["probs"], 1)

                def lo(n):
                    nb = groups[n][2]
                    dve.wait_ge(s["hi"], ng * a + n + 1)
                    dve.tensor_tensor(pT_lo[:, n % 2, 0:nb * P], ps[:, TB, 0:nb * P], r32(pT_hi[:, n % 2, 0:nb * P]),
                                      ALU.subtract).then_inc(s["lo"], 1)

                def half(q):
                    r = slice(hd * DH, hd * DH + DH)
                    dve.wait_ge(s["ocopy"], 2 * a + q + 1)
                    dve.tensor_tensor(mixb[r, q * HALF:(q + 1) * HALF], ps[0:DH, OB, :], otmp[r, :], ALU.add).then_inc(s["osum"], 1)

                return scores, norm, lo, half

            def causal_job(g, part):
                def job(k):
                    for hd in range(2):
                        scores, norm, lo, half = soft("dil", 2 * g + hd, hd, lambda i: (i + 1) * P, 16 * g + 16)
                        r = k + 16 * part - START[hd]
                        if r - 2 in QK_AT:
                            norm(QK_AT[r - 2])
                        if r in TURN_AT:
                            lo(TURN_AT[r])
                        if r in HALF_AT:
                            if hd == 0 and HALF_AT[r] == 0:
                                dve.wait_ge(mix_stored, 16 * g + 16)
                            half(HALF_AT[r])
                        if r in QK_AT:
                            scores(QK_AT[r])
                return job

            def mem_job(j, part):
                def parts(n):
                    return soft("mem", 2 * j + n // NBLK, n // NBLK, lambda i: MEM, None)

                def job(k):
                    r = k + 16 * part
                    if r in MEM_TURN_AT:
                        n = MEM_TURN_AT[r]
                        parts(n)[2](n % NBLK)
                    if r in MEM_HALF_AT:
                        q = MEM_HALF_AT[r]
                        if q == 0:
                            dve.wait_ge(mix_stored, 16 * (N_DIL // 2 + j) + 16)
                        parts(4 * q)[3](q % 2)
                    if r - 1 in MEM_QK_AT:
                        n = MEM_QK_AT[r - 1]
                        parts(n)[1](n % NBLK)
                    if r in MEM_QK_AT:
                        n = MEM_QK_AT[r]
                        parts(n)[0](n % NBLK)
                return job

            def gla(h, part):
                def job(k0):
                    k = k0 + 16 * part
                    if k == 0:
                        dve.memset(state[:, 0, :], 0.0)
                        dve.wait_ge(g_abs, h + 1)
                        dve.tensor_scalar(e2[:, :], ps[:, L:L + 2, :].rearrange("p a b -> p (a b)"), bgh[:, 0:1], 0.0,
                                          ALU.add, ALU.min).then_inc(g_min, 1)
                        dve.wait_ge(g_min, h + 1)
                        dve.wait_ge(g_ln, h + 1)
                        dve.tensor_tensor(e2[:, :], e2[:, :], e1[:, :], ALU.subtract).then_inc(g_la, 1)
                    if k == 1:
                        dve.wait_ge(g_la, h + 1)
                        for c in range(2 * NBLK):
                            r = slice(c * CHUNK, (c + 1) * CHUNK)
                            scan = dve.tensor_tensor_scan(bcum[:, r], ones[:, :], e2[:, r], 0.0, ALU.mult, ALU.add)
                        scan.then_inc(g_scan, 1)
                    if k == 4:
                        dve.wait_ge(g_scan, h + 1)
                        b = bcum[:, :].rearrange("p (c t) -> p c t", t=CHUNK)
                        dve.tensor_tensor(e2[:, :].rearrange("p (c t) -> p c t", t=CHUNK),
                                          b[:, :, CHUNK - 1:CHUNK].to_broadcast([P, 2 * NBLK, CHUNK]), b, ALU.subtract).then_inc(g_rest, 1)
                    if k == 6:
                        dve.wait_ge(g_e1, h + 1)
                        dve.wait_ge(evac_act, T_G + 6 * h + 3)
                        dve.wait_ge(evac_dve, T_G + 6 * h + 3)
                        dve.scalar_tensor_tensor(gq[:, :], gq[:, :], P ** -0.5, e1[:, :], ALU.mult, ALU.mult)
                        dve.tensor_copy(dec[:, :], e1[:, :].rearrange("p (c t) -> p c t", t=CHUNK)[:, :, CHUNK - 1]).then_inc(g_qt, 1)
                        dve.wait_ge(g_e2, h + 1)
                        dve.tensor_tensor(bcum[:, :], gk[:, :], e1[:, :], ALU.mult).then_inc(g_kt, 1)
                        dve.wait_ge(g_e3, h + 1)
                        dve.tensor_tensor(gk[:, :], gk[:, :], e2[:, :], ALU.mult).then_inc(g_ks, 1)
                    if 12 <= k < 28 and k % 2 == 0:
                        i = (k - 12) // 2
                        if i >= 2:
                            carry(g_o, 8 * h + i - 1)
                        carry(g_a, 8 * h + i + 1)
                        dve.copy_predicated(am[:, i % 2, :], amask[:, :], ps[:, TB, 0:P]).then_inc(g_am, 1)
                        for c in range(2):
                            n = 2 * i + c
                            if n == 2 * NBLK - 1:
                                continue
                            if n >= 3:
                                dve.wait_ge(g_o, 8 * h + (n - 3) // 2 + 1)
                            if n >= 1:
                                dve.wait_ge(g_st, 15 * h + n)
                            dve.wait_ge(g_kv, 15 * h + n + 1)
                            dve.scalar_tensor_tensor(state[:, (n + 1) % 4, :], state[:, n % 4, :], dec[:, n:n + 1],
                                                     ps[:, L + c, 0:DV], ALU.mult, ALU.add).then_inc(g_st, 1)
                    if k == 28:
                        dve.wait_ge(g_ocopied, 8 * h + 8)
                        dve.tensor_scalar(gst[:, 1, :], gst[:, 0, :], 1.0 / DV, EPS, ALU.mult, ALU.add).then_inc(g_v, 1)
                    if k == 29:
                        dve.wait_ge(g_sqrt, h + 1)
                        inverse_root(gst[:, 1, :], gst[:, 2, :], gst[:, 3, :], gst[:, 0, :], g_rc, 4 * h)
                        for i in range(NBLK):
                            last = dve.tensor_scalar(osb[:, i, :], osb[:, i, :], gst[:, 0, i:i + 1], None, ALU.mult)
                        last.then_inc(g_scaled, 1)
                    if 32 <= k < 36:
                        q = k - 32
                        j, t = q // 2, q % 2
                        dve.wait_ge(evac_act, T_G + 6 * h + 5)
                        if j == 1:
                            dve.wait_ge(g_stored[t], 32 * h + 16)
                        dve.wait_ge(g_turned, 4 * h + q + 1)
                        dve.scalar_tensor_tensor(mixo[:, t, :], ps[:, TB, :], nw[:, j:j + 1], ggate[:, j, t * HALF:(t + 1) * HALF],
                                                 ALU.mult, ALU.mult).then_inc(g_mixo, 1)
                    if k == 47:
                        for t in range(2):
                            dve.wait_ge(g_stored[t], 32 * h + 32)
                return job

            for T in range(2):
                tile(T, T % 2, ev_mk, None, T)
            for T in range(2, 4):
                tile(T, T % 2, ev_mv, None, T - 2)
            scale_rows(2, 6, 10)
            turn_lo(2, HALF, HALF, 1)
            tile(T_LR, T_LR % 2, ev_lr)
            tile(T_GV0, T_GV0 % 2, ev_copy, None, e2)

            def gla_head(h, last):
                T = T_G + 6 * h
                tile(T, 0, ev_copy, gla_v(2 + 4 * h, 0), e2)
                tile(T + 1, 1, ev_copy, gla_v(4 + 4 * h, 1), gk)
                tile(T + 2, 0, ev_copy, None, gq)
                tile(T + 3, 1, ev_none, gla(h, 0))
                tile(T + 4, 0, ev_none, gla(h, 1))
                tile(T + 5, 1, ev_copy, gla(h, 2), sc[:, 0, :] if last else e2)

            dve.wait_ge(g_zero, 5)
            with dve.Fori(0, N_GLA - 1) as h:
                gla_head(h, False)
            gla_head(N_GLA - 1, True)

            V0 = 2 + 2 * N_GLA

            def dil_pair(g, T, last):
                tile(T, 0, ev_kd, dil_v(V0 + 2 * g), 2 + 2 * g + 1)
                tile(T + 1, 1, ev_qd, None, 2 + 2 * g + 2)
                tile(T + 2, 0, ev_none, causal_job(g, 0))
                if last:
                    tile(T + 3, 1, ev_qd, causal_job(g, 1), 2 + 2 * g + 3)
                else:
                    tile(T + 3, 1, ev_copy, causal_job(g, 1), sc[:, 0, :])

            with dve.Fori(0, N_DIL // 2 - 1) as g:
                dil_pair(g, T_D + 4 * g, False)
            dil_pair(N_DIL // 2 - 1, T_D + 4 * (N_DIL // 2 - 1), True)
            tile(T_MQ0 + 1, (T_MQ0 + 1) % 2, ev_none, mem_job(0, 0))
            tile(T_MQ0 + 2, T_MQ0 % 2, ev_qd, mem_job(0, 1), 2 + N_DIL + 2)

            def osplit(c, k):
                u = UNIT_NO[c, k]
                dve.wait_ge(hi_done, u + 1)
                hi, lo = (w_hi[:, k % 4, :], w_lo[:, k % 4, :]) if c < CHUNKS - 1 else (hT_hi[:, k, 0:HALF], hT_lo[:, k, 0:HALF])
                dve.tensor_tensor(lo, w_raw[:, u % 2, :], r32(hi), ALU.subtract).then_inc(lo_done, 1)

            def piece(n):
                hf, k = PIECES[n]
                dve.wait_ge(m_hi, piece_no(n))
                r = slice(hf * HALF, (hf + 1) * HALF)
                dve.tensor_tensor(hT_lo[:, k, r], stg[:, n % 4, :], r32(hT_hi[:, k, r]), ALU.subtract).then_inc(m_lo, 1)

            def direct():
                for hf in range(2):
                    dve.wait_ge(m_hi, DIRECT + hf + 1)
                    r = slice(hf * HALF, (hf + 1) * HALF)
                    dve.tensor_tensor(hT_lo[:, KT - 1, r], mixb[:, r], r32(hT_hi[:, KT - 1, r]), ALU.subtract).then_inc(m_lo, 1)

            def y_copy(c, m):
                if c == CHUNKS - 1 or m < 3:
                    dve.wait_ge(y_done, 3 * c + m + 1)
                else:
                    dve.wait_ge(unit_used, 4 * T_END + 16 * (c + 1))
                if c == 4:
                    dve.wait_ge(out_stored, 16 * 4)
                n = c % 4
                dve.tensor_tensor(y[:, m, n * 512:(n + 1) * 512], ps[:, 4 * (c % 2) + m, :], wpost[:, n * 512:(n + 1) * 512],
                                  ALU.mult).then_inc(y_copied, 1)

            def mean(q, lo, hi):
                dve.wait_ge(y_sq, 16 * (q > 0) + 12 + hi)
                dve.tensor_reduce(yst[:, 0, lo:hi], ssy[:, lo:hi, :], AXX, ALU.add).then_inc(y_rc, 1)
                dve.wait_ge(y_rc, 5 * q + 1)
                dve.tensor_scalar(yst[:, 0, lo:hi], yst[:, 0, lo:hi], 1.0 / D, EPS, ALU.mult, ALU.add).then_inc(y_sum, 1)

            def rstd(q, lo, hi):
                dve.wait_ge(y_sqrt, q + 1)
                inverse_root(yst[:, 0, lo:hi], yst[:, 1, lo:hi], yst[:, 3, lo:hi], yst[:, 2, lo:hi], y_rc, 5 * q + 1)

            def add_residual(hf, m):
                for c in range(2):
                    n = 8 * hf + 2 * m + c
                    dve.wait_ge(xr_in[n % 3], 16 * (n // 3 + 1))
                    r = slice(c * 1024, (c + 1) * 1024)
                    dve.scalar_tensor_tensor(y[:, m, r], y[:, m, r], yst[:, 2, m:m + 1], xr[:, n % 3, :], ALU.mult, ALU.add).then_inc(y_out, 1)

            mem_job_1 = mem_job(1, 0)

            def last_tile_job(k):
                mem_job_1(k)
                for n in pieces_at(-1, k):
                    piece(n)

            tile(T_MQ0 + 3, (T_MQ0 + 1) % 2, ev_none, last_tile_job)
            for c in range(CHUNKS - 1):
                for k in range(KT):
                    for unit_ in splits_at(c, k):
                        osplit(*unit_)
                    for n in pieces_at(c, k):
                        piece(n)
                    if c == 0:
                        mem_job(1, 1)(k)
                        if k == DIRECT_AT:
                            direct()
                        if k == KT - 1:
                            dve.wait_ge(wpost_in, 16)
                    if c == 4:
                        if k == 0:
                            mean(0, 0, 4)
                        if k == 1:
                            rstd(0, 0, 4)
                        if k in (2, 4, 6, 8):
                            add_residual(0, (k - 2) // 2)
                for m in range(4):
                    y_copy(c, m)
            for m in range(4):
                y_copy(CHUNKS - 1, m)
                mean(1 + m, m, m + 1)
                rstd(1 + m, m, m + 1)
                add_residual(1, m)

        @block.tensor
        def _(pe):
            def tile(T, par, job=None, cols=SEQ):
                halves = [(0, HALF), (1, HALF)] if cols == SEQ else [(0, cols)]
                base = 0 if cols == SEQ else HALF
                if not isinstance(T, int) or T >= 2:
                    pe.wait_ge(evac_act, T - 1)
                    pe.wait_ge(evac_dve, T - 1)
                for k in range(KT):
                    j = k // 4
                    if k % 4 == 0:
                        pe.wait_ge(lo_done, 4 * T + j + 1)
                    whi = w_hi[:, j, (k % 4) * P:(k % 4 + 1) * P]
                    wlo = w_lo[:, j, (k % 4) * P:(k % 4 + 1) * P]
                    for w, h, first, final in ((whi, hT_hi, True, False), (whi, hT_lo, False, False), (wlo, hT_hi, False, True)):
                        for q, n in halves:
                            mm = pe.matmul(ps[:, 2 * par + q, 0:n], w, h[:, k, base + q * HALF:base + q * HALF + n],
                                           start=(k == 0 and first), stop=(k == KT - 1 and final))
                    if k % 4 == 3:
                        mm.then_inc(unit_used, 1)
                    if job:
                        job(k)

            pe.wait_ge(s_rel, 32)
            pe.wait_ge(s_id, 3)
            for c in range(3):
                n = min(512, TABLE - 512 * c)
                mm = pe.matmul(ps[0:N_DIL, L + c, 0:n], rel_sb[:, :], tab_sb[:, 512 * c:512 * c + n], start=True, stop=True)
            mm.then_inc(s_bias, 1)
            pe.wait_ge(s_biasc, 1)

            def turn(q, tiles):
                for k in range(KT):
                    n = KT * q + k
                    if k == 0:
                        pe.wait_ge(x_scaled, tiles[-1] + 1)
                    if n >= 4:
                        pe.wait_ge(x_lo, n - 3)
                    for b, t in enumerate(tiles):
                        mm = pe.transpose(ps[:, L + k % 4, b * P:(b + 1) * P], xs[:, t % 7, k * P:(k + 1) * P], ident[:, :])
                    mm.then_inc(x_turned, 1)

            def turn_values(src, blocks):
                for b, t in enumerate(blocks):
                    mm = pe.transpose(ps[:, TB, b * P:(b + 1) * P], src[:, t * P:(t + 1) * P], ident[:, :])
                mm.then_inc(v_turned, 1)

            def mem_values(j):
                pe.wait_ge(evac_act, 3 + j)
                pe.wait_ge(x_lo, 2 * KT)
                if j > 0:
                    pe.wait_ge(v_dve, j)
                turn_values(vtm, (0, 1))

            turn(0, range(0, 2))
            turn(1, range(2, 6))
            pe.wait_ge(x_lo, 2 * KT)
            pe.wait_ge(x_sq, 6)
            tile(0, 0, None, MEM)
            tile(1, 1, None, MEM)
            tile(2, 0, None, MEM)
            tile(3, 1, lambda k: mem_values(0) if k == 2 else None, MEM)
            mem_values(1)
            pe.wait_ge(v_dve, 2)
            turn(2, range(6, 10))
            pe.wait_ge(x_lo, 3 * KT)

            def gla_v(T, q):
                def job(k):
                    if k == VALUES_AT:
                        pe.wait_ge(evac_act, T)
                        pe.wait_ge(evac_dve, T)
                        pe.wait_ge(v_dve, 2 + q)
                        turn_values(e2, range(0, 4))
                    if k == VALUES_AT + 1:
                        pe.wait_ge(v_act, 2 + q + 1)
                        turn_values(e2, range(4, 8))
                return job

            NV = 2 + 2 * N_GLA

            def dil_v(T, g):
                def job(k):
                    if k == VALUES_AT:
                        pe.wait_ge(evac_act, T)
                        pe.wait_ge(evac_dve, T)
                        turn_values(sc[:, 0, :], range(0, 4))
                    if k == VALUES_AT + 1:
                        pe.wait_ge(v_dve, NV + 2 * g + 1)
                        turn_values(sc[:, 0, :], range(4, 8))
                return job

            def soft(kind, a, hd, width, keys_hi, keys_lo, values):
                s = J[kind]
                causal = kind == "dil"
                groups = GROUPS if causal else [(i, 0, 2) for i in range(NBLK)]
                ng = len(groups)

                def scores(i):
                    w = width(i)
                    if i >= 2 or (hd == 1 and not causal):
                        pe.wait_ge(s["negmax" if causal else "exps"], NBLK * a + (i - 1 if w <= 512 else i))
                    elif hd == 1:
                        pe.wait_ge(s["negmax"], NBLK * a)
                    out_ = logits(i, w)
                    hi_rows = slice(hd * DH, hd * DH + DH)
                    for c in range(0, w, 512):
                        n = min(512, w - c)
                        pe.matmul(out_[:, c:c + n], qs[:, hd, i * P:(i + 1) * P], keys_hi[:, c:c + n], start=True, stop=False)
                        mm = pe.matmul(out_[:, c:c + n], qs[hi_rows, hd, i * P:(i + 1) * P], keys_lo[hi_rows, c:c + n], start=False, stop=True)
                    mm.then_inc(s["logits"], 1)

                def turned(n):
                    i, jb, nb = groups[n]
                    if jb == 0:
                        pe.wait_ge(s["probs"], NBLK * a + i + 1)
                    if n >= 1 or hd == 1:
                        pe.wait_ge(s["lo"], ng * a + n)
                    for b in range(nb):
                        mm = pe.transpose(ps[:, TB, b * P:(b + 1) * P], sc[:, i % 2, (jb + b) * P:(jb + b + 1) * P], ident[:, :])
                    mm.then_inc(s["turned"], 1)

                def values_(n):
                    i, jb, nb = groups[n]
                    pe.wait_ge(s["lo"], ng * a + n + 1)
                    if i == 4 and jb == 0:
                        pe.wait_ge(s["osum"], 2 * a + 1)
                    if n == 0 and hd == 1:
                        pe.wait_ge(s["osum"], 2 * a)
                    last = i if causal else 1
                    for b in range(nb):
                        for part in (pT_hi, pT_lo):
                            mm = pe.matmul(ps[:, OB, (i % 4) * P:(i % 4 + 1) * P], values[:, jb + b, :], part[:, n % 2, b * P:(b + 1) * P],
                                           start=(jb + b == 0 and part is pT_hi), stop=(jb + b == last and part is pT_lo))
                    if i % 4 == 3 and jb + nb - 1 == last:
                        mm.then_inc(s["half"], 1)

                return scores, turned, values_

            def causal_job(g, part):
                def job(k):
                    if k == START[0] and part == 0:
                        pe.wait_ge(lo_a, 2 + 2 * g + 2)
                        pe.wait_ge(v_dve, NV + 2 * g + 2)
                    for hd in range(2):
                        scores, turned, values_ = soft("dil", 2 * g + hd, hd, lambda i: (i + 1) * P, kh[:, hd, :], kl[:, :], vv[:, hd, :, :])
                        r = k + 16 * part - START[hd]
                        if r in TURN_AT:
                            turned(TURN_AT[r])
                        if r in USE_AT:
                            values_(USE_AT[r])
                        if r in QK_AT:
                            if r == 0 and hd == 1:
                                pe.wait_ge(evac_dve, T_D + 4 * g + 2)
                            scores(QK_AT[r])
                return job

            def mem_job(j, part):
                def parts(n):
                    hd = n // NBLK
                    return soft("mem", 2 * j + hd, hd, lambda i: MEM, mkh[:, 2 * j + hd, :], mkl[:, j, :], mv[:, 2 * j + hd, :, :])

                def job(k):
                    r = k + 16 * part
                    if r == 0:
                        pe.wait_ge(evac_dve, T_MQ0 + 2 * j + 1)
                        pe.wait_ge(J["dil" if j == 0 else "mem"]["osum"], 2 * N_DIL if j == 0 else 4)
                    if r in MEM_TURN_AT:
                        n = MEM_TURN_AT[r]
                        parts(n)[1](n % NBLK)
                    if r in MEM_USE_AT:
                        n = MEM_USE_AT[r]
                        parts(n)[2](n % NBLK)
                    if r in MEM_QK_AT:
                        n = MEM_QK_AT[r]
                        parts(n)[0](n % NBLK)
                return job

            def gla(h, part):
                def job(k0):
                    k = k0 + 16 * part
                    if k == 0:
                        pe.wait_ge(g_par, 32 * h + 32)
                        for q in range(2):
                            mm = pe.matmul(ps[:, L + q, :], w2h[:, :], lrT[:, q * HALF:(q + 1) * HALF], start=True, stop=True)
                        mm.then_inc(g_z, 1)
                    if k in (10, 11):
                        q = k - 10
                        if q == 0:
                            pe.wait_ge(g_ks, h + 1)
                            pe.wait_ge(v_dve, 2 + 2 * h + 2)
                        else:
                            pe.wait_ge(g_kcopied, 2 * h + 1)
                        for b in range(4):
                            t = 4 * q + b
                            mm = pe.transpose(ps[:, TB, b * P:(b + 1) * P], gk[:, t * P:(t + 1) * P], ident[:, :])
                        mm.then_inc(g_kturned, 1)
                    if 12 <= k < 28 and k % 2 == 0:
                        i = (k - 12) // 2
                        blk = slice(i * P, (i + 1) * P)
                        if i == 0:
                            pe.wait_ge(g_kcopied, 2 * h + 2)
                            pe.wait_ge(g_kt, h + 1)
                            pe.wait_ge(g_min, h + 1)
                        else:
                            pe.wait_ge(g_am, 8 * h + i)
                            pe.wait_ge(g_st, 15 * h + 2 * i)
                        pe.matmul(ps[:, TB, 0:P], bcum[:, blk], gq[:, blk], start=True, stop=True).then_inc(g_a, 1)
                        for c in range(2):
                            if 2 * i + c == 2 * NBLK - 1:
                                continue
                            r = slice(c * CHUNK, (c + 1) * CHUNK)
                            pe.matmul(ps[:, L + c, 0:DV], ks[r, i, :], gv[r, i, :], start=True, stop=True).then_inc(g_kv, 1)
                    if 13 <= k < 29 and k % 2 == 1:
                        i = (k - 13) // 2
                        pe.wait_ge(g_am, 8 * h + i + 1)
                        pe.wait_ge(g_st, 15 * h + min(2 * i + 1, 15))
                        if i >= 1:
                            pe.wait_ge(g_ocopied, 8 * h + i)
                        pe.matmul(ps[:, OB, 0:DV], am[:, i % 2, :], gv[:, i, :], start=True, stop=False)
                        for c in range(2):
                            t = i * P + c * CHUNK
                            mm = pe.matmul(ps[c * CHUNK:(c + 1) * CHUNK, OB, 0:DV], gq[:, t:t + CHUNK], state[:, (2 * i + c) % 4, :],
                                           start=False, stop=True)
                        mm.then_inc(g_o, 1)
                    if 32 <= k < 36:
                        q = k - 32
                        j, t = q // 2, q % 2
                        if q == 0:
                            pe.wait_ge(g_scaled, h + 1)
                        else:
                            pe.wait_ge(g_mixo, 4 * h + q)
                        for b in range(4):
                            mm = pe.transpose(ps[:, TB, b * P:(b + 1) * P], osb[:, 4 * t + b, j * P:(j + 1) * P], ident[:, :])
                        mm.then_inc(g_turned, 1)
                return job

            pe.wait_ge(x_sq, 10)
            tile(T_LR, T_LR % 2)
            tile(T_GV0, T_GV0 % 2)

            def gla_head(h):
                T = T_G + 6 * h
                tile(T, 0, gla_v(T, 2 * h))
                tile(T + 1, 1, gla_v(T + 1, 2 * h + 1))
                tile(T + 2, 0)
                tile(T + 3, 1, gla(h, 0))
                tile(T + 4, 0, gla(h, 1))
                tile(T + 5, 1, gla(h, 2))

            with pe.Fori(0, N_GLA) as h:
                gla_head(h)

            def dil_pair(g):
                T = T_D + 4 * g
                tile(T, 0, dil_v(T, g))
                tile(T + 1, 1)
                tile(T + 2, 0, causal_job(g, 0))
                tile(T + 3, 1, causal_job(g, 1))

            with pe.Fori(0, N_DIL // 2) as g:
                dil_pair(g)
            tile(T_MQ0 + 1, (T_MQ0 + 1) % 2, mem_job(0, 0))
            tile(T_MQ0 + 2, T_MQ0 % 2, mem_job(0, 1))
            tile(T_MQ0 + 3, (T_MQ0 + 1) % 2, mem_job(1, 0))

            def bank_free(c, m):
                if c == 0 and m == 0:
                    pe.wait_ge(evac_act, T_END)
                    pe.wait_ge(evac_dve, T_END)
                if c == 1 and m == 0:
                    pe.wait_ge(J["mem"]["osum"], 8)
                if c >= 2:
                    pe.wait_ge(y_sq, 4 * (c - 2) + m + 1)

            def mix_ready(hf, k):
                pe.wait_ge(m_lo, piece_no(DIRECT * hf + k) if k < KT - 1 else DIRECT + 1 + hf)

            def products(c, m, k, whi, wlo):
                hf = c // 4
                t = slice(hf * HALF + m * P, hf * HALF + (m + 1) * P)
                bank = ps[:, 4 * (c % 2) + m, :]
                pe.matmul(bank, hT_hi[:, k, t], whi, start=(k == 0), stop=False)
                pe.matmul(bank, hT_hi[:, k, t], wlo, start=False, stop=False)
                return pe.matmul(bank, hT_lo[:, k, t], whi, start=False, stop=(k == KT - 1))

            for c in range(CHUNKS - 1):
                for k in range(KT):
                    pe.wait_ge(lo_done, UNIT_NO[c, k] + 1)
                    mix_ready(c // 4, k)
                    for m in range(4):
                        if k == 0:
                            bank_free(c, m)
                        mm = products(c, m, k, w_hi[:, k % 4, :], w_lo[:, k % 4, :])
                        if m < 3 and k == KT - 1:
                            mm.then_inc(y_done, 1)
                    mm.then_inc(unit_used, 1)
                    if c == 0:
                        mem_job(1, 1)(k)
            for m in range(4):
                bank_free(CHUNKS - 1, m)
                for k in range(KT):
                    if m == 0:
                        pe.wait_ge(lo_done, UNIT_NO[CHUNKS - 1, k] + 1)
                    mm = products(CHUNKS - 1, m, k, hT_hi[:, k, 0:HALF], hT_lo[:, k, 0:HALF])
                mm.then_inc(y_done, 1)


_INS = ['x', 'mem', 'norm_pre_w', 'w_in', 'rel_bias', 'w_gla_gate2', 'b_gla_gate', 'gla_norm_w',
        'mem_norm_w', 'w_mem_kv', 'w_out', 'norm_post_w']


def kernel(**inputs):
    import numpy as _np
    import concourse.bacc as _bacc
    from concourse import mybir as _mybir
    from concourse.bass_utils import run_bass_kernel_spmd as _run

    nc = _bacc.Bacc("TRN2", target_bir_lowering=False, num_devices=1, dynamic_dma_scratch_size=1024)
    arrays, args = {}, []
    for name in _INS:
        a = _np.ascontiguousarray(inputs[name])
        arrays[f"in_{name}_dram"] = a
        args.append(nc.dram_tensor(f"in_{name}_dram", a.shape, _mybir.dt.from_np(a.dtype), kind="ExternalInput").ap())
    arrays["dist_table_dram"] = distance_table()
    f32 = _mybir.dt.float32
    args.append(nc.dram_tensor("dist_table_dram", (BUCKETS + 1, TABLE), f32, kind="ExternalInput").ap())
    args.append(nc.dram_tensor("bias_rows", (N_DIL, TABLE), f32, kind="Internal").ap())
    args.append(nc.dram_tensor("bias_tables", (N_DIL, P * TABLE), f32, kind="Internal").ap())
    args.append(nc.dram_tensor("mix", (D, SEQ), f32, kind="Internal").ap())
    args.append(nc.dram_tensor("out_dram", (1, SEQ, D), f32, kind="ExternalOutput").ap())
    with nc.allow_non_contiguous_dma(reason="norm weights and gate biases, one element a partition"):
        build(nc, *args)
    r = _run(nc, [arrays], core_ids=[0])
    return r.results[0]["out_dram"]
```

```python
from contextlib import ExitStack

import numpy as np

import concourse.bass as bass
from concourse import mybir

F32 = mybir.dt.float32
F32R = mybir.dt.float32r
I32 = mybir.dt.int32
ALU = mybir.AluOpType
ACT = mybir.ActivationFunctionType
AXX = mybir.AxisListType.X

P = 128
D = 2048
KT = D // P
SEQ = 1024
HALF = 512
NBLK = SEQ // P
ROWS = 2 + NBLK
MEM_TILE_AFTER = {2: 0, 4: 1, 6: 2, 8: 3}
MEM_VALUES_AT = 4
SPLITS_AFTER = {n: ((n // 2, n % 2 * 2), (n // 2, n % 2 * 2 + 1)) for n in range(ROWS)}
DH = 64
N_DIL, N_GLA, N_MEM = 12, 4, 4
DV = 256
MEM = 256
CHUNK = 64
TAU = 16.0
RANK = 16
BUCKETS = 32
EPS = 1e-6
PATTERNS = ((128, 1), (512, 4), (2048, 16))
NEG = 1e30

C_DQ = 0
C_DK = C_DQ + N_DIL * DH
C_DV = C_DK + N_DIL * DH
C_GQ = C_DV + N_DIL * DH
C_GK = C_GQ + N_GLA * P
C_GV = C_GK + N_GLA * P
C_LR = C_GV + N_GLA * DV
C_MQ = C_LR + RANK
C_GATE = C_MQ + N_MEM * DH
X_DIL, X_GLA, X_MEM = 0, N_DIL // 2, N_DIL // 2 + 2 * N_GLA

T_LR = 4
LR_LO = 32
T_GV0 = T_LR + 1
T_G = T_GV0 + 1
T_DV0 = T_G + 6 * N_GLA - 1
T_D = T_DV0 + 1
T_MQ0 = T_D + 4 * (N_DIL // 2) - 1
T_END = T_MQ0 + 4

TABLE = SEQ + P
GROUPS = [(i, j, min(4, i + 1 - j)) for i in range(NBLK) for j in range(0, i + 1, 4)]
NG = len(GROUPS)
START = (1, 15)
QK_AT = {0: 0, 1: 1, 2: 2, 4: 3, 5: 4, 7: 5, 9: 6, 11: 7}
TURN_AT = {n + (3 if n < 3 else 4): n for n in range(NG)}
USE_AT = {r + 1: n for r, n in TURN_AT.items() if GROUPS[n][0] % 2}
HALF_AT = {max(r for r, n in USE_AT.items() if GROUPS[n][0] == 4 * q + 3): q for q in range(2)}
VALUES_AT = 5
MEM_START = 1
MEM_QK_AT = {MEM_START + 3 * n // 2: n for n in range(2 * NBLK)}
MEM_TURN_AT = {r + 3: n for r, n in MEM_QK_AT.items()}
MEM_USE_AT = {r + 4: n for r, n in MEM_QK_AT.items() if n % 2}
MEM_HALF_AT = {r: n // 4 for r, n in MEM_USE_AT.items() if n % 4 == 3}

CHUNKS = 8
LAST = CHUNKS - 1
BLOCKS = (2, 3, 0, 1)


def splits_at(c, k):
    now = [(c + (k + 4) // KT, (k + 4) % KT)]
    if now[0][0] >= LAST:
        now = []
    if LAST - 3 <= c < LAST and k % 3 == 0:
        early = 6 * (c - LAST + 3) + k // 3
        if early < KT:
            now.append((LAST, early))
    return now


UNITS = [(0, k) for k in range(4)] + [u for c in range(LAST) for k in range(KT) for u in splits_at(c, k)]
UNIT_NO = {u: 4 * T_END + i for i, u in enumerate(UNITS)}


FOUR_FROM = 4 * T_END + 2 * KT


def raw_slot(u):
    if u < FOUR_FROM:
        return u % 2, u // 2 + 1, u - 2
    j, i = (u - FOUR_FROM) % 4, (u - FOUR_FROM) // 4
    if i > 0:
        return j, (FOUR_FROM // 2 if j < 2 else 0) + i + 1, u - 4
    return (j, FOUR_FROM // 2 + 1, u - 2) if j < 2 else (j, 1, None)


PIECES = [(0, k) for k in range(KT - 1)] + [(1, k) for k in range(KT - 1)]
DIRECT = KT - 1


def piece_no(n):
    return n + 1 if n < DIRECT else n + 3


def pieces_at(c, k):
    if c == -1:
        return [k // 3 - 2] if k >= 6 and k % 3 == 0 else []
    if c == 0:
        return [k + 4] if k + 4 < DIRECT else []
    return [DIRECT + k] if c == 1 and k < KT - 1 else []


PAIR_SILU_AT = 14
SILU_AT = 10
DIRECT_AT = 13


def t5_bucket(dist):
    half = BUCKETS // 2
    n = np.maximum(dist, 1).astype(np.float32)
    large = half + (np.log(n / np.float32(half)) / np.float32(np.log(2048 / half)) * np.float32(half)).astype(np.int32)
    return np.where(dist < half, dist, np.minimum(large, BUCKETS - 1))


def distance_table():
    dist = SEQ - 1 - np.arange(TABLE)
    count = np.zeros(TABLE, np.float32)
    for window, dil in PATTERNS:
        count += (dist >= 0) & (dist <= window) & (dist % dil == 0)
    out = np.zeros((BUCKETS + 1, TABLE), np.float32)
    out[t5_bucket(np.maximum(dist, 0)), np.arange(TABLE)] = -1.0
    out[BUCKETS] = np.where(count > 0, -np.log(np.maximum(count, 1)), NEG)
    return out


def build(nc, x, mem, norm_pre_w, w_in, rel_bias, w_gla_gate2, b_gla_gate, gla_norm_w, mem_norm_w,
          w_mem_kv, w_out, norm_post_w, dist_table, bias_rows, bias_tables, mix, out):
    x, mem, out = x[0], mem[0], out[0]
    w_in, w_mem_kv, w_out, w_gate2 = w_in[0], w_mem_kv[0], w_out[0], w_gla_gate2[0]

    with ExitStack() as ctx:
        def sb(name, shape, dt=F32, stack=ctx):
            return stack.enter_context(nc.sbuf_tensor(name, shape, dt))

        def sem(name):
            return ctx.enter_context(nc.semaphore(name))

        with ExitStack() as ph:
            tab_sb = sb("tab_sb", [BUCKETS + 1, TABLE], F32, ph)
            brow = sb("brow", [N_DIL, TABLE], F32, ph)
        hT_hi = sb("hT_hi", [P, KT, SEQ], F32R)
        hT_lo = sb("hT_lo", [P, KT, SEQ], F32R)
        w_raw = sb("w_raw", [P, 2, 512])
        w_hi = sb("w_hi", [P, 4, 512], F32R)
        w_lo = sb("w_lo", [P, 4, 512], F32R)
        mkh = sb("mkh", [P, N_MEM, MEM], F32R)
        mkl = sb("mkl", [P, N_MEM // 2, MEM], F32R)
        with ExitStack() as ph:
            pre_a = sb("pre_a", [P, D // 2], F32, ph)
        mv = sb("mv", [P, N_MEM, MEM // P, P], F32R)
        ident = sb("ident", [P, P])
        nw = sb("nw", [P, 2])
        negmax = sb("negmax", [P, NBLK])
        den = sb("den", [P, NBLK])
        rden = sb("rden", [P, NBLK])
        with ExitStack() as ph:
            memT_hi = sb("memT_hi", [P, KT, MEM], F32R, ph)
            memT_lo = sb("memT_lo", [P, KT, MEM], F32R, ph)
            vtm = sb("vtm", [P, 2, MEM], F32, ph)
            xs = sb("xs", [P, 3, D], F32, ph)
            pre_b = sb("pre_b", [P, D // 2], F32, ph)
            nwT = sb("nwT", [P, KT], F32, ph)
            ssx = sb("ssx", [P, ROWS, 2], F32, ph)
            st = sb("st", [P, 4, ROWS], F32, ph)
            rel_sb = sb("rel_sb", [BUCKETS + 1, N_DIL], F32, ph)
        with ExitStack() as ph:
            kh = sb("kh", [P, 2, SEQ], F32R, ph)
            kl = sb("kl", [P, SEQ], F32R, ph)
            vv = sb("vv", [P, 2, NBLK, P], F32R, ph)
            tab = sb("tab", [P, SEQ], F32, ph)
            qs = sb("qs", [P, 2, SEQ], F32R, ph)
            pT_hi = sb("pT_hi", [P, NBLK, 2, P], F32R, ph)
            pT_lo = sb("pT_lo", [P, NBLK, 2, P], F32R, ph)
            sc = sb("sc", [P, 2, SEQ], F32, ph)
            gate = sb("gate", [P, SEQ], F32, ph)
            mixb = sb("mixb", [P, SEQ], F32, ph)
        with ExitStack() as ph:
            ggate = sb("ggate", [P, 2, SEQ], F32, ph)
            gq = sb("gq", [P, SEQ], F32, ph)
            gk = sb("gk", [P, SEQ], F32, ph)
            bcum = sb("bcum", [P, SEQ], F32, ph)
            e1 = sb("e1", [P, SEQ], F32, ph)
            e2 = sb("e2", [P, SEQ], F32, ph)
            ks = sb("ks", [P, NBLK, P], F32, ph)
            gv = sb("gv", [P, NBLK, DV], F32, ph)
            am = sb("am", [P, 2, P], F32, ph)
            state = sb("state", [P, 4, DV], F32, ph)
            osb = sb("osb", [P, NBLK, DV], F32, ph)
            mixo = sb("mixo", [P, 2, HALF], F32, ph)
            lrT = sb("lrT", [RANK, SEQ], F32, ph)
            w2h = sb("w2h", [RANK, P], F32, ph)
            bgh = sb("bgh", [P, 1], F32, ph)
            ones = sb("ones", [P, CHUNK], F32, ph)
            amask = sb("amask", [P, P], I32, ph)
            dec = sb("dec", [P, 2 * NBLK], F32, ph)
            gst = sb("gst", [P, 4, NBLK], F32, ph)
        with ExitStack() as ph:
            stg = sb("stg", [P, 4, HALF], F32, ph)
            wpost = sb("wpost", [P, D], F32, ph)
            xr = sb("xr", [P, 2, D // 2], F32, ph)
            y = sb("y", [P, 4, D], F32, ph)
            ssy = sb("ssy", [P, 4, 4], F32, ph)
            yst = sb("yst", [P, 4, 4], F32, ph)
            w_raw2 = sb("w_raw2", [P, 2, 512], F32, ph)
            xr2 = sb("xr2", [P, D // 2], F32, ph)

        ps = ctx.enter_context(nc.psum_tensor("ps", [P, 8, 512], F32))
        L, TB, OB = 4, 6, 7

        def sems(*names):
            return [sem(n) for n in names]

        raw_landed = sems("raw_landed0", "raw_landed1", "raw_landed2", "raw_landed3")
        hi_done, lo_done, unit_used = sems("hi_done", "lo_done", "unit_used")
        evac_act, evac_dve = sems("evac_act", "evac_dve")
        s_id, s_small, s_pre, s_rel = sems("s_id", "s_small", "s_pre", "s_rel")
        s_bias, s_biasc, s_biasw, s_rep = sems("s_bias", "s_biasc", "s_biasw", "s_rep")
        x_in = sems("x_in0", "x_in1", "x_in2")
        x_sq, x_v, x_sqrt, x_rc = sems("x_sq", "x_v", "x_sqrt", "x_rc")
        x_warm = sem("x_warm")
        x_scaled, x_weighted, x_scaled_b = sems("x_scaled", "x_weighted", "x_scaled_b")
        x_turned, x_hi, x_lo = sems("x_turned", "x_hi", "x_lo")
        v_turned, v_act, v_dve = sems("v_turned", "v_act", "v_dve")
        keys_a, lo_a = sems("keys_a", "lo_a")
        carried = sem("carried")
        J = {kind: {n: sem(f"{kind}_{n}") for n in (
            "logits", "negmax", "exps", "rden", "probs", "turned", "hi", "lo", "half", "ocopy", "osum")}
            for kind in ("dil", "mem")}
        tab_landed = sems("tab_landed0", "tab_landed1")
        silu_done, gated, mix_stored = sems("silu_done", "gated", "mix_stored")
        g_par, g_z, g_abs, g_exp, g_min, g_ln, g_la, g_scan, g_rest = sems(
            "g_par", "g_z", "g_abs", "g_exp", "g_min", "g_ln", "g_la", "g_scan", "g_rest")
        g_e1, g_qt, g_e2, g_kt, g_e3, g_ks = sems("g_e1", "g_qt", "g_e2", "g_kt", "g_e3", "g_ks")
        g_kturned, g_kcopied, g_a, g_am, g_kv, g_st = sems("g_kturned", "g_kcopied", "g_a", "g_am", "g_kv", "g_st")
        g_o, g_ocopied, g_v, g_sqrt, g_rc, g_scaled = sems("g_o", "g_ocopied", "g_v", "g_sqrt", "g_rc", "g_scaled")
        g_turned, g_silu, g_mixo = sems("g_turned", "g_silu", "g_mixo")
        g_stored = sems("g_stored0", "g_stored1")
        g_zero = sem("g_zero")
        stg_in = sems("stg_in0", "stg_in1", "stg_in2", "stg_in3")
        m_hi, m_lo = sems("m_hi", "m_lo")
        y_done, y_copied, y_sq = sems("y_done", "y_copied", "y_sq")
        y_sum, y_sqrt, y_rc, y_out, out_stored = sems("y_sum", "y_sqrt", "y_rc", "y_out", "out_stored")
        xr_in = sems("xr_in0", "xr_in1", "xr_in2")
        wpost_in = sem("wpost_in")

        def raw(u):
            j = raw_slot(u)[0]
            return w_raw[:, j, :] if j < 2 else w_raw2[:, j - 2, :]

        def lr_cols(w, c, n=P):
            return w.rearrange("p (k c) -> p k c", c=n)[:, :, c:c + RANK]

        def xr_slot(n):
            return xr[:, n % 3, :] if n % 3 < 2 else xr2[:, :]

        def proj(par, a=0, b=P, n=SEQ):
            if n == MEM:
                return ps[a:b, par, 0:n]
            return ps[a:b, 2 * par:2 * par + 2, :].rearrange("p a b -> p (a b)")[:, 0:n]

        def place(kind, i, jb):
            if kind == "mem":
                return 2 * (i // 2 % 4) + jb
            return jb + (4 if i in (2, 3) else 0)

        def logits(i, w):
            bank = i % 2 if w <= 512 else 0
            return ps[:, L:L + 2, :].rearrange("p a b -> p (a b)")[:, bank * 512:bank * 512 + w]

        def r32(ap):
            return ap.bitcast(F32)

        block = ctx.enter_context(nc.Block())

        @block.sync
        def _(sp):
            def unit(T, j, src):
                if not (isinstance(T, int) and 4 * T + j < 2):
                    sp.wait_ge(lo_done, 4 * T + j - 1)
                sp.dma_start(w_raw[:, j % 2, :].rearrange("p (k c) -> p k c", c=src.shape[-1]), src).then_inc(raw_landed[j % 2], 16)

            def tile(T, w, col):
                v = w.rearrange("(k p) c -> p k c", p=P)
                for j in range(4):
                    unit(T, j, v[:, 4 * j:4 * j + 4, bass.ds(col, P)])

            sp.dma_start(tab_sb[:, :], dist_table).then_inc(s_rel, 16)
            sp.wait_ge(s_id, 2)
            sp.dma_start(rel_sb[0:BUCKETS, :], rel_bias).then_inc(s_rel, 16)
            sp.dma_start(nwT[:, :], mem_norm_w.rearrange("a (k p) -> p (a k)", p=P)).then_inc(s_small, 16)
            sp.dma_start(nw[:, :], gla_norm_w.rearrange("a (k p) -> p (a k)", p=P)).then_inc(s_small, 16)
            for c, half in enumerate((pre_a, pre_b)):
                sp.dma_start(half[:, :], norm_pre_w[0:1, c * 1024:(c + 1) * 1024].to_broadcast([P, D // 2])).then_inc(s_pre, 16)
            for T in range(4):
                tile(T, w_mem_kv, T * P)
            for j in range(4):
                sp.wait_ge(lo_done, 4 * T_LR + j - 1)
                sp.dma_start(lr_cols(w_raw[:, j % 2, 0:4 * RANK], 0, RANK),
                             w_in.rearrange("(k p) c -> p k c", p=P)[:, 4 * j:4 * j + 4, C_LR:C_LR + RANK]).then_inc(raw_landed[j % 2], 16)
            tile(T_GV0, w_in, C_GV)
            sp.wait_ge(s_biasw, 16)
            for h in range(N_DIL):
                sp.dma_start(bias_tables[h].rearrange("(p n) -> p n", n=TABLE),
                             bias_rows[h:h + 1, :].to_broadcast([P, TABLE])).then_inc(s_rep, 16)

            def gla_params(h):
                sp.dma_start(w2h[:, :], w_gate2[:, bass.ds(h * P, P)]).then_inc(g_par, 16)
                sp.dma_start(bgh[:, :], b_gla_gate[0:1, bass.ds(h * P, P)].rearrange("a p -> p a")).then_inc(g_par, 16)

            def gla_tiles(h, T):
                tile(T, w_in, C_GV + P + h * DV)
                tile(T + 1, w_in, C_GK + h * P)
                tile(T + 2, w_in, C_GQ + h * P)
                tile(T + 3, w_in, C_GATE + X_GLA * P + h * (2 * P))
                tile(T + 4, w_in, C_GATE + (X_GLA + 1) * P + h * (2 * P))

            sp.wait_ge(x_turned, 4 * ROWS)
            gla_params(0)
            with sp.Fori(0, N_GLA - 1) as h:
                gla_tiles(h, T_G + 6 * h)
                sp.wait_ge(g_min, h + 1)
                gla_params(h + 1)
                tile(T_G + 6 * h + 5, w_in, C_GV + DV + h * DV)
            gla_tiles(N_GLA - 1, T_G + 6 * (N_GLA - 1))
            tile(T_DV0, w_in, C_DV)

            def table(g, hd):
                src = bias_tables[bass.ds(2 * g + hd, 1), P - 1:P - 1 + P * (TABLE - 1)]
                src = src.rearrange("a (p n) -> (a p) n", n=TABLE - 1)[:, 0:SEQ]
                sp.dma_start(tab[:, :], src).then_inc(tab_landed[hd], 16)

            tile(T_D, w_in, C_DK)
            sp.wait_ge(s_rep, 16 * N_DIL)
            sp.wait_ge(g_mixo, 4 * N_GLA)
            table(0, 0)
            with sp.Fori(0, N_DIL // 2 - 1) as g:
                T = T_D + 4 * g
                tile(T + 1, w_in, C_DQ + g * P)
                tile(T + 2, w_in, C_GATE + X_DIL * P + g * P)
                tile(T + 3, w_in, C_DV + P + g * P)
                sp.wait_ge(J["dil"]["negmax"], 2 * NBLK * g + NBLK)
                table(g, 1)
                tile(T + 4, w_in, C_DK + P + g * P)
                sp.wait_ge(J["dil"]["negmax"], 2 * NBLK * g + 2 * NBLK)
                table(g + 1, 0)
            gl = N_DIL // 2 - 1
            tile(T_D + 4 * gl + 1, w_in, C_DQ + gl * P)
            tile(T_D + 4 * gl + 2, w_in, C_GATE + (X_DIL + gl) * P)
            for j in range(2):
                tile(T_MQ0 + 2 * j, w_in, C_MQ + j * P)
                if j == 0:
                    sp.wait_ge(J["dil"]["negmax"], 2 * NBLK * gl + NBLK)
                    table(gl, 1)
                tile(T_MQ0 + 2 * j + 1, w_in, C_GATE + (X_MEM + j) * P)

            def piece(n):
                hf, k = PIECES[n]
                if n >= 4:
                    sp.wait_ge(m_lo, piece_no(n - 4))
                if n < KT - 2:
                    sp.wait_ge(mix_stored, 16 * (min(n, N_DIL // 2 - 1) + 2))
                else:
                    sp.wait_ge(mix_stored, 16 * (N_DIL // 2 + 2))
                sp.dma_start(stg[:, n % 4, :], mix[k * P:(k + 1) * P, hf * HALF:(hf + 1) * HALF]).then_inc(stg_in[n % 4], 16)

            def out_unit(c, k):
                u = UNIT_NO[c, k]
                slot, _, before = raw_slot(u)
                if before is not None:
                    sp.wait_ge(lo_done, before + 1)
                else:
                    sp.wait_ge(m_lo, DIRECT + 2)
                sp.dma_start(raw(u), w_out[k * P:(k + 1) * P, c % 4 * 512:(c % 4 + 1) * 512]).then_inc(raw_landed[slot], 16)

            def residual(n):
                if n >= 3:
                    sp.wait_ge(y_out, n - 2)
                row = (n // 8 * 4 + BLOCKS[n % 8 // 2]) * P
                sp.dma_start(xr_slot(n), x[row:row + P, n % 2 * 1024:(n % 2 + 1) * 1024]).then_inc(xr_in[n % 3], 16)

            for q in range(2):
                sp.wait_ge(g_stored[q], 32 * N_GLA)
            sp.wait_ge(mix_stored, 16 * (N_DIL // 2 + 1))
            for k in range(KT):
                if k in (4, 8, 12):
                    out_unit(0, k // 4 - 1)
                for n in pieces_at(-1, k):
                    piece(n)
            out_unit(0, 3)
            for c in range(CHUNKS):
                for k in range(KT):
                    for unit_ in splits_at(c, k):
                        out_unit(*unit_)
                    for n in pieces_at(c, k):
                        piece(n)
                    if c == 0 and k == KT // 2:
                        sp.dma_start(wpost[:, :], norm_post_w[0:1, :].to_broadcast([P, D])).then_inc(wpost_in, 16)
                    if c == 3 and k >= KT - 3:
                        residual(k - (KT - 3))
                    if c == 4 and k >= 5 and k - 2 < 8:
                        residual(k - 2)
            for n in range(8, 16):
                residual(n)

        @block.gpsimd
        def _(pool):
            def split(T, j):
                pool.wait_ge(hi_done, 4 * T + j + 1)
                if isinstance(T, int) and T == T_LR:
                    pool.tensor_tensor(lr_cols(w_hi[:, j, :], LR_LO), lr_cols(w_raw[:, j % 2, 0:4 * RANK], 0, RANK),
                                       r32(lr_cols(w_hi[:, j, :], 0)), ALU.subtract).then_inc(lo_done, 1)
                    return
                pool.tensor_tensor(w_lo[:, j % 4, :], w_raw[:, j % 2, :], r32(w_hi[:, j % 4, :]), ALU.subtract).then_inc(lo_done, 1)

            def tiles(T, n):
                for i in range(n):
                    for j in range(4):
                        split(T + i + 1, j)

            pool.memset(ident[:, :], 0.0).then_inc(s_id, 1)
            pool.memset(rel_sb[:, :], 1.0).then_inc(s_id, 1)
            pool.wait_ge(s_id, 2)
            pool.affine_select(out=ident[:, :], in_=ident[:, :], compare_op=ALU.not_equal, fill=1.0, base=0,
                               pattern=[[-1, P]], channel_multiplier=1).then_inc(s_id, 1)
            pool.sem_inc(mix_stored, 16)
            pool.wait_ge(s_pre, 32)
            for n in range(ROWS):
                if n + 2 < ROWS:
                    pool.wait_ge(x_sq, 2 * (n + 2) + 2)
                    xb = xs[:, (n + 2) % 3, 1024:2048]
                    pool.tensor_tensor(xb, xb, pre_b[:, :], ALU.mult).then_inc(x_weighted, 1)
                for unit in SPLITS_AFTER[n]:
                    split(*unit)
            pool.wait_ge(x_turned, 4 * ROWS)
            pool.memset(amask[:, :], 1).then_inc(g_zero, 1)
            pool.memset(am[:, :, :], 0.0).then_inc(g_zero, 1)
            pool.memset(ones[:, :], 1.0).then_inc(g_zero, 1)
            pool.wait_ge(g_zero, 3)
            pool.affine_select(out=amask[:, :], in_=amask[:, :], compare_op=ALU.is_ge, fill=0.0, base=0,
                               pattern=[[1, P]], channel_multiplier=-1).then_inc(g_zero, 1)
            pool.wait_ge(g_zero, 4)
            pool.affine_select(out=amask[:, CHUNK:P], in_=amask[:, CHUNK:P], compare_op=ALU.is_ge, fill=0.0,
                               base=-CHUNK, pattern=[[0, CHUNK]], channel_multiplier=1).then_inc(g_zero, 1)

            def gate_pair(kind, g, n):
                pool.wait_ge(J[kind]["osum"], 4 * g + 4)
                pool.wait_ge(silu_done, n + 1)
                pool.tensor_tensor(mixb[:, :], mixb[:, :], gate[:, :], ALU.mult).then_inc(gated, 1)

            tiles(T_LR, 2)
            with pool.Fori(0, 6 * N_GLA) as n:
                tiles(T_G + n, 1)
            with pool.Fori(0, N_DIL // 2) as g:
                tiles(T_D + 4 * g, 4)
                gate_pair("dil", g, g)
            tiles(T_MQ0 + 1, 2)
            gate_pair("mem", 0, N_DIL // 2)
            tiles(T_END - 1, 1)
            gate_pair("mem", 1, N_DIL // 2 + 1)

        @block.scalar
        def _(act):
            def split(T, j):
                act.wait_ge(raw_landed[j % 2], 16 * (2 * T + j // 2 + 1))
                if not isinstance(T, int) or T > 0:
                    act.wait_ge(unit_used, 4 * T + j - 3)
                if isinstance(T, int) and T == T_LR:
                    act.activation(lr_cols(w_hi[:, j, :], 0), lr_cols(w_raw[:, j % 2, 0:4 * RANK], 0, RANK), ACT.Copy).then_inc(hi_done, 1)
                    return
                act.activation(w_hi[:, j % 4, :], w_raw[:, j % 2, :], ACT.Copy).then_inc(hi_done, 1)

            def tile(T, par, kind, job=None, arg=None):
                for k in range(KT):
                    if k in (4, 8, 12):
                        split(T + 1, k // 4 - 1)
                    if job:
                        job(k)
                act.wait_ge(unit_used, 4 * T + 4)
                kind(T, par, arg)
                split(T + 1, 3)

            def load(n):
                src = mem[n * P:(n + 1) * P, :] if n < 2 else x[(n - 2) * P:(n - 1) * P, :]
                act.dma_start(xs[:, n % 3, :], src).then_inc(x_in[n % 3], 16)

            def squares(n):
                act.wait_ge(x_in[n % 3], 16 * (n // 3 + 1))
                for c in range(2):
                    if n + c > 0:
                        act.wait_ge(x_sq, 2 * n + c)
                    act.activation(ps[:, 2:4, :].rearrange("p a b -> p (a b)"), xs[:, n % 3, c * 1024:(c + 1) * 1024],
                                   ACT.Square, accum_out=ssx[:, n, c:c + 1]).then_inc(x_sq, 1)

            def root(n):
                act.wait_ge(x_v, n + 1)
                act.activation(st[:, 1, n:n + 1], st[:, 0, n:n + 1], ACT.Sqrt).then_inc(x_sqrt, 1)

            def turn_hi(n):
                for q in range(4):
                    act.wait_ge(x_turned, 4 * n + q + 1)
                    if n < 2:
                        for k in range(4 * q, 4 * q + 4):
                            ins = act.activation(memT_hi[:, k, n * P:(n + 1) * P], ps[:, L + q, (k % 4) * P:(k % 4 + 1) * P], ACT.Copy,
                                                 scale=nwT[:, k:k + 1])
                    else:
                        ins = act.activation(hT_hi[:, 4 * q:4 * q + 4, (n - 2) * P:(n - 1) * P],
                                             ps[:, L + q, :].rearrange("p (k c) -> p k c", c=P), ACT.Copy)
                    ins.then_inc(x_hi, 1)

            load(0)
            act.wait_ge(s_id, 3)
            act.activation(st[:, 1, 0:1], ident[:, 0:1], ACT.Sqrt).then_inc(x_warm, 1)
            load(1)
            load(2)
            act.wait_ge(x_warm, 1)
            squares(0)
            root(0)
            act.wait_ge(s_bias, 1)
            act.activation(brow[:, :], ps[0:N_DIL, L:L + 3, :].rearrange("p a b -> p (a b)")[:, 0:TABLE], ACT.Copy).then_inc(s_biasc, 1)
            act.wait_ge(s_biasc, 1)
            act.dma_start(bias_rows, brow[:, :]).then_inc(s_biasw, 16)
            squares(1)
            root(1)
            act.wait_ge(s_small, 32)

            def stacked_hi(dst_a, dst_b, par, n):
                for dst, r, ready in ((dst_a, slice(0, DH), keys_a), (dst_b, slice(DH, P), evac_act)):
                    act.activation(dst[0:DH, :], proj(par, r.start, r.stop, n), ACT.Copy)
                    act.activation(dst[DH:P, :], proj(par, r.start, r.stop, n), ACT.Copy).then_inc(ready, 1)

            def ev_mk(T, par, j):
                stacked_hi(mkh[:, 2 * j, :], mkh[:, 2 * j + 1, :], par, MEM)

            def ev_mv(T, par, j):
                act.activation(vtm[:, j, :], proj(par, 0, P, MEM), ACT.Copy).then_inc(evac_act, 1)

            def mem_values(j):
                act.wait_ge(v_turned, j + 1)
                act.activation(mv[:, 2 * j:2 * j + 2, :, 0:DH],
                               ps[:, TB, 0:MEM].rearrange("p (b h c) -> p h b c", h=2, c=DH), ACT.Copy).then_inc(v_act, 1)

            def ev_lr(T, par, _):
                act.activation(lrT[:, :], proj(par, 0, RANK), ACT.Copy).then_inc(evac_act, 1)

            def ev_copy(T, par, dst):
                act.activation(dst[:, 0:HALF], ps[:, 2 * par, :], ACT.Copy).then_inc(evac_act, 1)

            def silu(T):
                act.wait_ge(evac_act, T + 1)
                act.wait_ge(evac_dve, T + 1)
                act.activation(gate[:, :], gate[:, :], ACT.Silu).then_inc(silu_done, 1)

            def ev_kd(T, par, _):
                stacked_hi(kh[:, 0, :], kh[:, 1, :], par, SEQ)

            def ev_qd(T, par, _):
                for hd, r, ready in ((0, slice(0, DH), keys_a), (1, slice(DH, P), evac_act)):
                    act.activation(qs[r, hd, :], proj(par, r.start, r.stop), ACT.Copy, scale=-DH ** -0.5).then_inc(ready, 1)

            def gla_v(first, j):
                def job(k):
                    if k == VALUES_AT + 1:
                        act.wait_ge(v_turned, first + 1)
                        act.activation(gv[:, 0:4, j * P:(j + 1) * P], ps[:, TB, :].rearrange("p (b c) -> p b c", c=P), ACT.Copy).then_inc(v_act, 1)
                return job

            def dil_v(first):
                def job(k):
                    if k in (VALUES_AT, VALUES_AT + 1):
                        q = k - VALUES_AT
                        act.wait_ge(v_turned, first + q + 1)
                        act.activation(vv[:, :, 4 * q:4 * q + 4, 0:DH],
                                       ps[:, TB, :].rearrange("p (b h c) -> p h b c", h=2, c=DH), ACT.Copy).then_inc(v_act, 1)
                return job

            def soft(kind, a, hd, width):
                s = J[kind]
                causal = kind == "dil"
                ng = NG if causal else NBLK
                groups = GROUPS if causal else [(i, 0, 2) for i in range(NBLK)]

                def exps(i):
                    w = width(i)
                    act.wait_ge(s["negmax"], NBLK * a + i + 1)
                    src = sc[:, i % 2, 0:w] if causal else logits(i, w)
                    act.activation(sc[:, i % 2, 0:w], src, ACT.Exp, bias=negmax[:, i:i + 1], scale=-1.0,
                                   accum_out=den[:, i:i + 1]).then_inc(s["exps"], 1)

                def hi(n):
                    i, j, nb = groups[n]
                    act.wait_ge(s["turned"], ng * a + n + 1)
                    b = place(kind, i, j)
                    act.activation(pT_hi[:, b:b + nb, i % 2, :], ps[:, TB, 0:nb * P].rearrange("p (b c) -> p b c", c=P),
                                   ACT.Copy).then_inc(s["hi"], 1)

                def half(q):
                    r = slice(hd * DH, hd * DH + DH)
                    act.wait_ge(s["half"], 2 * a + q + 1)
                    act.activation(mixb[r, q * HALF:(q + 1) * HALF], ps[DH:P, OB, :], ACT.Copy).then_inc(s["ocopy"], 1)

                return exps, hi, half

            def causal_job(g, part):
                def job(k):
                    for hd in range(2):
                        exps, hi, half = soft("dil", 2 * g + hd, hd, lambda i: (i + 1) * P)
                        r = k + 16 * part - START[hd]
                        if r in TURN_AT:
                            hi(TURN_AT[r])
                        if r in HALF_AT:
                            if hd == 0 and HALF_AT[r] == 0:
                                act.wait_ge(mix_stored, 16 * g + 16)
                            half(HALF_AT[r])
                        if r - 1 in QK_AT:
                            exps(QK_AT[r - 1])
                    if part == 1 and k == PAIR_SILU_AT:
                        silu(T_D + 4 * g + 2)
                return job

            def mem_job(j, part):
                def parts(n):
                    return soft("mem", 2 * j + n // NBLK, n // NBLK, lambda i: MEM)

                def job(k):
                    r = k + 16 * part
                    if r in MEM_TURN_AT:
                        n = MEM_TURN_AT[r]
                        parts(n)[1](n % NBLK)
                    if r in MEM_HALF_AT:
                        q = MEM_HALF_AT[r]
                        if q == 0:
                            act.wait_ge(mix_stored, 16 * (N_DIL // 2 + j) + 16)
                        parts(4 * q)[2](q % 2)
                    if r in MEM_QK_AT:
                        n = MEM_QK_AT[r]
                        parts(n)[0](n % NBLK)
                    if j == 0 and r == KT + PAIR_SILU_AT:
                        silu(T_MQ0 + 1)
                return job

            def store_mix(n, group):
                act.wait_ge(gated, n)
                act.dma_start(mix[bass.ds(group * P, P), :], mixb[:, :]).then_inc(mix_stored, 16)

            def gla(h, part):
                def job(k0):
                    k = k0 + 16 * part
                    if k == -4:
                        act.wait_ge(g_par, 32 * h + 32)
                        act.wait_ge(g_z, h + 1)
                        act.activation(e1[:, :], ps[:, L:L + 2, :].rearrange("p a b -> p (a b)"), ACT.Abs, bias=bgh[:, 0:1]).then_inc(g_abs, 1)
                        act.wait_ge(g_abs, h + 1)
                        act.activation(e1[:, :], e1[:, :], ACT.Exp, scale=-1.0).then_inc(g_exp, 1)
                        act.wait_ge(g_exp, h + 1)
                        act.activation(e1[:, :], e1[:, :], ACT.Ln, bias=1.0).then_inc(g_ln, 1)
                    if k == 1:
                        act.wait_ge(g_scan, h + 1)
                        act.activation(e1[:, :], bcum[:, :], ACT.Exp, scale=1.0 / TAU).then_inc(g_e1, 1)
                        act.wait_ge(g_rest, h + 1)
                        act.activation(e2[:, :], e2[:, :], ACT.Exp, scale=1.0 / TAU).then_inc(g_e3, 1)
                        act.wait_ge(g_qt, h + 1)
                        act.activation(e1[:, :], bcum[:, :], ACT.Exp, scale=-1.0 / TAU).then_inc(g_e2, 1)
                    if k in (8, 9):
                        q = k - 8
                        act.wait_ge(g_kturned, 2 * h + q + 1)
                        act.activation(ks[:, 4 * q:4 * q + 4, :], ps[:, TB, :].rearrange("p (b c) -> p b c", c=P), ACT.Copy).then_inc(g_kcopied, 1)
                    if 13 <= k < 29 and k % 2 == 1:
                        i = (k - 13) // 2
                        act.wait_ge(g_o, 8 * h + i + 1)
                        act.activation(osb[:, i, :], ps[:, OB, 0:DV], ACT.Copy)
                        act.activation(e1[:, 0:DV], ps[:, OB, 0:DV], ACT.Square, accum_out=gst[:, 0, i:i + 1]).then_inc(g_ocopied, 1)
                    if k == 28:
                        act.wait_ge(g_v, h + 1)
                        act.activation(gst[:, 2, :], gst[:, 1, :], ACT.Sqrt).then_inc(g_sqrt, 1)
                    if k == 32:
                        act.wait_ge(evac_act, T_G + 6 * h + 5)
                        act.wait_ge(evac_dve, T_G + 6 * h + 5)
                        act.activation(ggate[:, :, :], ggate[:, :, :], ACT.Silu).then_inc(g_silu, 1)
                    if 35 <= k < 39:
                        q = k - 35
                        act.wait_ge(g_mixo, 4 * h + q + 1)
                        rows = bass.ds((X_GLA + q // 2) * P + h * (2 * P), P)
                        act.dma_start(mix[rows, (q % 2) * HALF:(q % 2 + 1) * HALF], mixo[:, q % 2, :]).then_inc(g_stored[q % 2], 16)
                    if k == 47:
                        for q in range(2):
                            act.wait_ge(g_stored[q], 32 * h + 32)
                return job

            def mem_tile(T):
                act.wait_ge(unit_used, 4 * T + 4)
                (ev_mk if T < 2 else ev_mv)(T, T % 2, T % 2)

            for n in range(ROWS):
                if n == 2:
                    act.wait_ge(s_biasw, 16)
                turn_hi(n)
                if n + 3 < ROWS:
                    load(n + 3)
                if n + 2 < ROWS:
                    squares(n + 2)
                    root(n + 2)
                if n in MEM_TILE_AFTER:
                    mem_tile(MEM_TILE_AFTER[n])
                for unit in SPLITS_AFTER[n]:
                    split(*unit)
            mem_values(0)
            tile(T_LR, T_LR % 2, ev_lr, lambda k: mem_values(1) if k == MEM_VALUES_AT else None)
            tile(T_GV0, T_GV0 % 2, ev_copy, None, e2)

            def gla_head(h, last):
                T = T_G + 6 * h
                tile(T, 0, ev_copy, gla_v(2 + 4 * h, 0), e2)
                tile(T + 1, 1, ev_copy, gla_v(4 + 4 * h, 1), gk)
                tile(T + 2, 0, ev_copy, gla(h, -1), gq)
                tile(T + 3, 1, ev_copy, gla(h, 0), ggate[:, 0, :])
                tile(T + 4, 0, ev_copy, gla(h, 1), ggate[:, 1, :])
                tile(T + 5, 1, ev_copy, gla(h, 2), sc[:, 0, :] if last else e2)

            with act.Fori(0, N_GLA - 1) as h:
                gla_head(h, False)
            gla_head(N_GLA - 1, True)

            V0 = 2 + 4 * N_GLA

            def dil_pair(g, T, last):
                tile(T, 0, ev_kd, dil_v(V0 + 2 * g))
                tile(T + 1, 1, ev_qd)
                tile(T + 2, 0, ev_copy, causal_job(g, 0), gate)
                if last:
                    tile(T + 3, 1, ev_qd, causal_job(g, 1))
                else:
                    tile(T + 3, 1, ev_copy, causal_job(g, 1), sc[:, 0, :])
                store_mix(g + 1, X_DIL + g)

            with act.Fori(0, N_DIL // 2 - 1) as g:
                dil_pair(g, T_D + 4 * g, False)
            dil_pair(N_DIL // 2 - 1, T_D + 4 * (N_DIL // 2 - 1), True)
            tile(T_MQ0 + 1, (T_MQ0 + 1) % 2, ev_copy, mem_job(0, 0), gate)
            tile(T_MQ0 + 2, T_MQ0 % 2, ev_qd, mem_job(0, 1))
            store_mix(N_DIL // 2 + 1, X_MEM)

            def osplit(c, k):
                u = UNIT_NO[c, k]
                slot, landed, _ = raw_slot(u)
                act.wait_ge(raw_landed[slot], 16 * landed)
                if c < LAST:
                    act.wait_ge(unit_used, 4 * T_END + 16 * c + k - 3)
                    dst = w_hi[:, k % 4, :]
                else:
                    dst = hT_hi[:, k, 0:HALF]
                act.activation(dst, raw(u), ACT.Copy).then_inc(hi_done, 1)

            def piece(n):
                hf, k = PIECES[n]
                act.wait_ge(stg_in[n % 4], 16 * (n // 4 + 1))
                act.wait_ge(unit_used, 4 * (T_END - 1) + k // 4 + 1)
                act.activation(hT_hi[:, k, hf * HALF:(hf + 1) * HALF], stg[:, n % 4, :], ACT.Copy).then_inc(m_hi, 1)

            def direct():
                act.wait_ge(gated, N_DIL // 2 + 2)
                for hf in range(2):
                    r = slice(hf * HALF, (hf + 1) * HALF)
                    act.activation(hT_hi[:, KT - 1, r], mixb[:, r], ACT.Copy).then_inc(m_hi, 1)

            def y_squares(c, m):
                act.wait_ge(y_copied, 4 * c + BLOCKS.index(m) + 1)
                b = ps[:, 4 * (c % 2) + m, :]
                act.activation(b, b, ACT.Square, accum_out=ssy[:, m, c % 4:c % 4 + 1]).then_inc(y_sq, 1)

            def root(q, lo, hi):
                act.wait_ge(y_sum, q + 1)
                act.activation(yst[:, 1, lo:hi], yst[:, 0, lo:hi], ACT.Sqrt).then_inc(y_sqrt, 1)

            def store(hf, m, c0, c1):
                row = (4 * hf + m) * P
                act.wait_ge(y_out, 8 * hf + 2 * BLOCKS.index(m) + c1)
                r = slice(c0 * 1024, c1 * 1024)
                act.dma_start(out[row:row + P, r], y[:, m, r]).then_inc(out_stored, 16)

            mem_job_1 = mem_job(1, 0)

            def last_tile_job(k):
                mem_job_1(k)
                for n in pieces_at(-1, k):
                    piece(n)

            tile(T_MQ0 + 3, (T_MQ0 + 1) % 2, ev_copy, last_tile_job, gate)
            for c in range(LAST):
                for k in range(KT):
                    for unit_ in splits_at(c, k):
                        osplit(*unit_)
                    for n in pieces_at(c, k):
                        piece(n)
                    if c == 0:
                        mem_job(1, 1)(k)
                        if k == SILU_AT:
                            silu(T_END - 1)
                        if k == DIRECT_AT:
                            direct()
                    if c == 4:
                        if k == 0:
                            root(0, 0, 4)
                        if k in (5, 7, 9, 11):
                            store(0, BLOCKS[(k - 5) // 2], 0, 2)
                for m in BLOCKS:
                    y_squares(c, m)
            for m in BLOCKS:
                y_squares(LAST, m)
                root(1 + BLOCKS.index(m), m, m + 1)
                for c in range(2):
                    store(1, m, c, c + 1)
            act.wait_ge(out_stored, 16 * 12)

        @block.vector
        def _(dve):
            def carry(s, n):
                dve.wait_ge(s, n)
                dve.sem_inc(carried, 1)

            def tile(T, par, kind, job=None, arg=None):
                for k in range(KT):
                    if job:
                        job(k)
                dve.wait_ge(unit_used, 4 * T + 4)
                kind(T, par, arg)

            def inverse_root(v, root, t, out_, chain, c0):
                dve.reciprocal(out_, root).then_inc(chain, 1)
                dve.wait_ge(chain, c0 + 1)
                dve.tensor_tensor(t, out_, v, ALU.mult).then_inc(chain, 1)
                dve.wait_ge(chain, c0 + 2)
                dve.scalar_tensor_tensor(t, t, -0.5, out_, ALU.mult, ALU.mult).then_inc(chain, 1)
                dve.wait_ge(chain, c0 + 3)
                dve.scalar_tensor_tensor(out_, t, 1.5, out_, ALU.add, ALU.mult).then_inc(chain, 1)
                dve.wait_ge(chain, c0 + 4)

            def row_scale(n):
                dve.wait_ge(x_sq, 2 * n + 2)
                dve.tensor_tensor(st[:, 0, n:n + 1], ssx[:, n, 0:1], ssx[:, n, 1:2], ALU.add).then_inc(x_rc, 1)
                dve.wait_ge(x_rc, 5 * n + 1)
                dve.tensor_scalar(st[:, 0, n:n + 1], st[:, 0, n:n + 1], 1.0 / D, EPS, ALU.mult, ALU.add).then_inc(x_v, 1)
                dve.wait_ge(x_sqrt, n + 1)
                inverse_root(st[:, 0, n:n + 1], st[:, 1, n:n + 1], st[:, 3, n:n + 1], st[:, 2, n:n + 1], x_rc, 5 * n + 1)
                if n < 2:
                    dve.tensor_scalar(xs[:, n % 3, :], xs[:, n % 3, :], st[:, 2, n:n + 1], None, ALU.mult).then_inc(x_scaled, 1)
                else:
                    dve.wait_ge(s_pre, 32)
                    xa, xb = xs[:, n % 3, 0:1024], xs[:, n % 3, 1024:2048]
                    dve.scalar_tensor_tensor(xa, xa, st[:, 2, n:n + 1], pre_a[:, :], ALU.mult, ALU.mult).then_inc(x_scaled, 1)
                    dve.wait_ge(x_weighted, n - 1)
                    dve.tensor_scalar(xb, xb, st[:, 2, n:n + 1], None, ALU.mult).then_inc(x_scaled_b, 1)

            def turn_lo(n):
                for q in range(4):
                    dve.wait_ge(x_hi, 4 * n + q + 1)
                    if n < 2:
                        r = slice(n * P, (n + 1) * P)
                        for k in range(4 * q, 4 * q + 4):
                            ins = dve.scalar_tensor_tensor(memT_lo[:, k, r], ps[:, L + q, (k % 4) * P:(k % 4 + 1) * P], nwT[:, k:k + 1],
                                                           r32(memT_hi[:, k, r]), ALU.mult, ALU.subtract)
                    else:
                        r, kk = slice((n - 2) * P, (n - 1) * P), slice(4 * q, 4 * q + 4)
                        ins = dve.tensor_tensor(hT_lo[:, kk, r], ps[:, L + q, :].rearrange("p (k c) -> p k c", c=P),
                                                r32(hT_hi[:, kk, r]), ALU.subtract)
                    ins.then_inc(x_lo, 1)

            row_scale(0)
            row_scale(1)
            dve.wait_ge(s_small, 32)

            def stacked_lo(T, dst, hi_a, hi_b, par, n, count):
                for r, hi, ready, c, done in ((slice(0, DH), hi_a, keys_a, count, lo_a), (slice(DH, P), hi_b, evac_act, T + 1, evac_dve)):
                    dve.wait_ge(ready, c)
                    dve.tensor_tensor(dst[r, :], proj(par, r.start, r.stop, n), r32(hi[r, :]), ALU.subtract).then_inc(done, 1)

            def ev_mk(T, par, j):
                stacked_lo(T, mkl[:, j, :], mkh[:, 2 * j, :], mkh[:, 2 * j + 1, :], par, MEM, j + 1)

            def mem_values(j):
                dve.wait_ge(v_act, j + 1)
                v = mv[:, 2 * j:2 * j + 2, :, :]
                dve.tensor_tensor(v[:, :, :, DH:P], ps[:, TB, 0:MEM].rearrange("p (b h c) -> p h b c", h=2, c=DH),
                                  r32(v[:, :, :, 0:DH]), ALU.subtract).then_inc(v_dve, 1)

            def ev_lr(T, par, _):
                dve.wait_ge(evac_act, T + 1)
                dve.tensor_tensor(lrT[:, :], proj(par, LR_LO, LR_LO + RANK), lrT[:, :], ALU.add).then_inc(evac_dve, 1)

            def ev_copy(T, par, dst):
                dve.tensor_copy(dst[:, HALF:SEQ], ps[:, 2 * par + 1, :]).then_inc(evac_dve, 1)

            def ev_none(T, par, _):
                dve.sem_inc(evac_dve, 1)

            def ev_kd(T, par, count):
                stacked_lo(T, kl, kh[:, 0, :], kh[:, 1, :], par, SEQ, count)

            def ev_qd(T, par, count):
                for hd, r, o, ready, c, done in ((0, slice(0, DH), slice(DH, P), keys_a, count, lo_a),
                                                 (1, slice(DH, P), slice(0, DH), evac_act, T + 1, evac_dve)):
                    dve.wait_ge(ready, c)
                    dve.scalar_tensor_tensor(qs[o, hd, :], proj(par, r.start, r.stop), -DH ** -0.5, r32(qs[r, hd, :]),
                                             ALU.mult, ALU.subtract).then_inc(done, 1)

            def gla_v(first, j):
                def job(k):
                    if k == VALUES_AT + 1:
                        dve.wait_ge(v_turned, first + 2)
                        dve.tensor_copy(gv[:, 4:8, j * P:(j + 1) * P], ps[:, TB, :].rearrange("p (b c) -> p b c", c=P)).then_inc(v_dve, 1)
                return job

            def dil_v(before):
                def job(k):
                    if k in (VALUES_AT, VALUES_AT + 1):
                        q = k - VALUES_AT
                        dve.wait_ge(v_act, before + q + 1)
                        v = vv[:, :, 4 * q:4 * q + 4, :]
                        dve.tensor_tensor(v[:, :, :, DH:P], ps[:, TB, :].rearrange("p (b h c) -> p h b c", h=2, c=DH),
                                          r32(v[:, :, :, 0:DH]), ALU.subtract).then_inc(v_dve, 1)
                return job

            def soft(kind, a, hd, width, landed):
                s = J[kind]
                causal = kind == "dil"
                groups = GROUPS if causal else [(i, 0, 2) for i in range(NBLK)]
                ng = len(groups)

                def scores(i):
                    w = width(i)
                    if causal:
                        if i >= 2:
                            carry(s["turned"], ng * a + len([g for g in groups if g[0] <= i - 2]))
                        elif hd == 1:
                            carry(s["turned"], ng * a - len([g for g in groups if g[0] > i + NBLK - 2]))
                        carry(s["logits"], NBLK * a + i + 1)
                        if i == 0:
                            carry(tab_landed[hd], landed)
                        dve.tensor_tensor_reduce(sc[:, i % 2, 0:w], logits(i, w), tab[:, SEQ - w:SEQ], 1.0, 3e38,
                                                 ALU.add, ALU.min, negmax[:, i:i + 1]).then_inc(s["negmax"], 1)
                    else:
                        dve.wait_ge(s["logits"], NBLK * a + i + 1)
                        dve.tensor_reduce(negmax[:, i:i + 1], logits(i, w), AXX, ALU.min).then_inc(s["negmax"], 1)

                def norm(i):
                    w = width(i)
                    dve.wait_ge(s["exps"], NBLK * a + i + 1)
                    dve.reciprocal(rden[:, i:i + 1], den[:, i:i + 1]).then_inc(s["rden"], 1)
                    dve.wait_ge(s["rden"], NBLK * a + i + 1)
                    dve.tensor_scalar(sc[:, i % 2, 0:w], sc[:, i % 2, 0:w], rden[:, i:i + 1], None, ALU.mult).then_inc(s["probs"], 1)

                def lo(n):
                    i, jb, nb = groups[n]
                    b = place(kind, i, jb)
                    dve.wait_ge(s["hi"], ng * a + n + 1)
                    dve.tensor_tensor(pT_lo[:, b:b + nb, i % 2, :], ps[:, TB, 0:nb * P].rearrange("p (b c) -> p b c", c=P),
                                      r32(pT_hi[:, b:b + nb, i % 2, :]), ALU.subtract).then_inc(s["lo"], 1)

                def half(q):
                    r = slice(hd * DH, hd * DH + DH)
                    dve.wait_ge(s["ocopy"], 2 * a + q + 1)
                    dve.tensor_tensor(mixb[r, q * HALF:(q + 1) * HALF], ps[0:DH, OB, :], mixb[r, q * HALF:(q + 1) * HALF], ALU.add).then_inc(s["osum"], 1)

                return scores, norm, lo, half

            def causal_job(g, part):
                def job(k):
                    for hd in range(2):
                        scores, norm, lo, half = soft("dil", 2 * g + hd, hd, lambda i: (i + 1) * P, 16 * g + 16)
                        r = k + 16 * part - START[hd]
                        if r - 2 in QK_AT:
                            norm(QK_AT[r - 2])
                        if r in TURN_AT:
                            lo(TURN_AT[r])
                        if r in HALF_AT:
                            half(HALF_AT[r])
                        if r in QK_AT:
                            scores(QK_AT[r])
                return job

            def mem_job(j, part):
                def parts(n):
                    return soft("mem", 2 * j + n // NBLK, n // NBLK, lambda i: MEM, None)

                def job(k):
                    r = k + 16 * part
                    if r - 1 in MEM_QK_AT:
                        n = MEM_QK_AT[r - 1]
                        parts(n)[1](n % NBLK)
                    if r in MEM_TURN_AT:
                        n = MEM_TURN_AT[r]
                        parts(n)[2](n % NBLK)
                    if r in MEM_HALF_AT:
                        q = MEM_HALF_AT[r]
                        parts(4 * q)[3](q % 2)
                    if r in MEM_QK_AT:
                        n = MEM_QK_AT[r]
                        parts(n)[0](n % NBLK)
                return job

            def gla(h, part):
                def job(k0):
                    k = k0 + 16 * part
                    if k == -4:
                        dve.memset(state[:, 0, :], 0.0)
                        dve.wait_ge(g_abs, h + 1)
                        dve.tensor_scalar(e2[:, :], ps[:, L:L + 2, :].rearrange("p a b -> p (a b)"), bgh[:, 0:1], 0.0,
                                          ALU.add, ALU.min).then_inc(g_min, 1)
                        dve.wait_ge(g_min, h + 1)
                        dve.wait_ge(g_ln, h + 1)
                        dve.tensor_tensor(e2[:, :], e2[:, :], e1[:, :], ALU.subtract).then_inc(g_la, 1)
                    if k == -3:
                        dve.wait_ge(g_la, h + 1)
                        for c in range(2 * NBLK):
                            r = slice(c * CHUNK, (c + 1) * CHUNK)
                            scan = dve.tensor_tensor_scan(bcum[:, r], ones[:, :], e2[:, r], 0.0, ALU.mult, ALU.add)
                        scan.then_inc(g_scan, 1)
                    if k == 0:
                        dve.wait_ge(g_scan, h + 1)
                        b = bcum[:, :].rearrange("p (c t) -> p c t", t=CHUNK)
                        dve.tensor_tensor(e2[:, :].rearrange("p (c t) -> p c t", t=CHUNK),
                                          b[:, :, CHUNK - 1:CHUNK].to_broadcast([P, 2 * NBLK, CHUNK]), b, ALU.subtract).then_inc(g_rest, 1)
                    if k == 2:
                        dve.wait_ge(g_e1, h + 1)
                        dve.wait_ge(evac_act, T_G + 6 * h + 3)
                        dve.wait_ge(evac_dve, T_G + 6 * h + 3)
                        dve.scalar_tensor_tensor(gq[:, :], gq[:, :], P ** -0.5, e1[:, :], ALU.mult, ALU.mult)
                        dve.tensor_copy(dec[:, :], e1[:, :].rearrange("p (c t) -> p c t", t=CHUNK)[:, :, CHUNK - 1]).then_inc(g_qt, 1)
                        dve.wait_ge(g_e2, h + 1)
                        dve.tensor_tensor(bcum[:, :], gk[:, :], e1[:, :], ALU.mult).then_inc(g_kt, 1)
                        dve.wait_ge(g_e3, h + 1)
                        dve.tensor_tensor(gk[:, :], gk[:, :], e2[:, :], ALU.mult).then_inc(g_ks, 1)
                    if 12 <= k < 28 and k % 2 == 0:
                        i = (k - 12) // 2
                        if i >= 2:
                            carry(g_o, 8 * h + i - 1)
                        carry(g_a, 8 * h + i + 1)
                        dve.copy_predicated(am[:, i % 2, :], amask[:, :], ps[:, TB, 0:P]).then_inc(g_am, 1)
                        for c in range(2):
                            n = 2 * i + c
                            if n == 2 * NBLK - 1:
                                continue
                            if n >= 3:
                                dve.wait_ge(g_o, 8 * h + (n - 3) // 2 + 1)
                            if n >= 1:
                                dve.wait_ge(g_st, 15 * h + n)
                            dve.wait_ge(g_kv, 15 * h + n + 1)
                            dve.scalar_tensor_tensor(state[:, (n + 1) % 4, :], state[:, n % 4, :], dec[:, n:n + 1],
                                                     ps[:, L + c, 0:DV], ALU.mult, ALU.add).then_inc(g_st, 1)
                    if k == 28:
                        dve.wait_ge(g_ocopied, 8 * h + 8)
                        dve.tensor_scalar(gst[:, 1, :], gst[:, 0, :], 1.0 / DV, EPS, ALU.mult, ALU.add).then_inc(g_v, 1)
                    if k == 29:
                        dve.wait_ge(g_sqrt, h + 1)
                        inverse_root(gst[:, 1, :], gst[:, 2, :], gst[:, 3, :], gst[:, 0, :], g_rc, 4 * h)
                        for i in range(NBLK):
                            last = dve.tensor_scalar(osb[:, i, :], osb[:, i, :], gst[:, 0, i:i + 1], None, ALU.mult)
                        last.then_inc(g_scaled, 1)
                    if 35 <= k < 39:
                        q = k - 35
                        j, t = q // 2, q % 2
                        dve.wait_ge(g_silu, h + 1)
                        if j == 1:
                            dve.wait_ge(g_stored[t], 32 * h + 16)
                        dve.wait_ge(g_turned, 4 * h + q + 1)
                        dve.scalar_tensor_tensor(mixo[:, t, :], ps[:, TB, :], nw[:, j:j + 1], ggate[:, j, t * HALF:(t + 1) * HALF],
                                                 ALU.mult, ALU.mult).then_inc(g_mixo, 1)
                    if k == 47:
                        for t in range(2):
                            dve.wait_ge(g_stored[t], 32 * h + 32)
                return job

            def mem_tile(T):
                dve.wait_ge(unit_used, 4 * T + 4)
                (ev_mk if T < 2 else ev_none)(T, T % 2, T % 2)

            for n in range(ROWS):
                turn_lo(n)
                if n + 2 < ROWS:
                    row_scale(n + 2)
                if n in MEM_TILE_AFTER:
                    mem_tile(MEM_TILE_AFTER[n])
            mem_values(0)
            tile(T_LR, T_LR % 2, ev_lr, lambda k: mem_values(1) if k == MEM_VALUES_AT else None)
            tile(T_GV0, T_GV0 % 2, ev_copy, None, e2)

            def gla_head(h, last):
                T = T_G + 6 * h
                tile(T, 0, ev_copy, gla_v(2 + 4 * h, 0), e2)
                tile(T + 1, 1, ev_copy, gla_v(4 + 4 * h, 1), gk)
                tile(T + 2, 0, ev_copy, gla(h, -1), gq)
                tile(T + 3, 1, ev_copy, gla(h, 0), ggate[:, 0, :])
                tile(T + 4, 0, ev_copy, gla(h, 1), ggate[:, 1, :])
                tile(T + 5, 1, ev_copy, gla(h, 2), sc[:, 0, :] if last else e2)

            dve.wait_ge(g_zero, 5)
            with dve.Fori(0, N_GLA - 1) as h:
                gla_head(h, False)
            gla_head(N_GLA - 1, True)

            V0 = 2 + 2 * N_GLA

            def dil_pair(g, T, last):
                tile(T, 0, ev_kd, dil_v(V0 + 2 * g), 2 + 2 * g + 1)
                tile(T + 1, 1, ev_qd, None, 2 + 2 * g + 2)
                tile(T + 2, 0, ev_copy, causal_job(g, 0), gate)
                if last:
                    tile(T + 3, 1, ev_qd, causal_job(g, 1), 2 + 2 * g + 3)
                else:
                    tile(T + 3, 1, ev_copy, causal_job(g, 1), sc[:, 0, :])

            with dve.Fori(0, N_DIL // 2 - 1) as g:
                dil_pair(g, T_D + 4 * g, False)
            dil_pair(N_DIL // 2 - 1, T_D + 4 * (N_DIL // 2 - 1), True)
            tile(T_MQ0 + 1, (T_MQ0 + 1) % 2, ev_copy, mem_job(0, 0), gate)
            tile(T_MQ0 + 2, T_MQ0 % 2, ev_qd, mem_job(0, 1), 2 + N_DIL + 2)

            def osplit(c, k):
                u = UNIT_NO[c, k]
                dve.wait_ge(hi_done, u + 1)
                hi, lo = (w_hi[:, k % 4, :], w_lo[:, k % 4, :]) if c < LAST else (hT_hi[:, k, 0:HALF], hT_lo[:, k, 0:HALF])
                dve.tensor_tensor(lo, raw(u), r32(hi), ALU.subtract).then_inc(lo_done, 1)

            def piece(n):
                hf, k = PIECES[n]
                dve.wait_ge(m_hi, piece_no(n))
                r = slice(hf * HALF, (hf + 1) * HALF)
                dve.tensor_tensor(hT_lo[:, k, r], stg[:, n % 4, :], r32(hT_hi[:, k, r]), ALU.subtract).then_inc(m_lo, 1)

            def direct():
                for hf in range(2):
                    dve.wait_ge(m_hi, DIRECT + hf + 1)
                    r = slice(hf * HALF, (hf + 1) * HALF)
                    dve.tensor_tensor(hT_lo[:, KT - 1, r], mixb[:, r], r32(hT_hi[:, KT - 1, r]), ALU.subtract).then_inc(m_lo, 1)

            def y_copy(c, m):
                if c == LAST or m != BLOCKS[3]:
                    dve.wait_ge(y_done, 3 * c + BLOCKS.index(m) + 1)
                else:
                    dve.wait_ge(unit_used, 4 * T_END + 16 * (c + 1))
                if c == 4:
                    dve.wait_ge(out_stored, 16 * 4)
                n = c % 4
                dve.tensor_tensor(y[:, m, n * 512:(n + 1) * 512], ps[:, 4 * (c % 2) + m, :], wpost[:, n * 512:(n + 1) * 512],
                                  ALU.mult).then_inc(y_copied, 1)

            def mean(q, lo, hi):
                dve.wait_ge(y_sq, 16 if q == 0 else 28 + q)
                dve.tensor_reduce(yst[:, 0, lo:hi], ssy[:, lo:hi, :], AXX, ALU.add).then_inc(y_rc, 1)
                dve.wait_ge(y_rc, 5 * q + 1)
                dve.tensor_scalar(yst[:, 0, lo:hi], yst[:, 0, lo:hi], 1.0 / D, EPS, ALU.mult, ALU.add).then_inc(y_sum, 1)

            def rstd(q, lo, hi):
                dve.wait_ge(y_sqrt, q + 1)
                inverse_root(yst[:, 0, lo:hi], yst[:, 1, lo:hi], yst[:, 3, lo:hi], yst[:, 2, lo:hi], y_rc, 5 * q + 1)

            def add_residual(hf, m):
                for c in range(2):
                    n = 8 * hf + 2 * BLOCKS.index(m) + c
                    dve.wait_ge(xr_in[n % 3], 16 * (n // 3 + 1))
                    r = slice(c * 1024, (c + 1) * 1024)
                    dve.scalar_tensor_tensor(y[:, m, r], y[:, m, r], yst[:, 2, m:m + 1], xr_slot(n), ALU.mult, ALU.add).then_inc(y_out, 1)

            mem_job_1 = mem_job(1, 0)

            def last_tile_job(k):
                mem_job_1(k)
                for n in pieces_at(-1, k):
                    piece(n)

            tile(T_MQ0 + 3, (T_MQ0 + 1) % 2, ev_copy, last_tile_job, gate)
            dve.wait_ge(lo_done, 4 * T_END + 4)
            for c in range(LAST):
                for k in range(KT):
                    for unit_ in splits_at(c, k):
                        osplit(*unit_)
                    for n in pieces_at(c, k):
                        piece(n)
                    if c == 0:
                        mem_job(1, 1)(k)
                        if k == DIRECT_AT:
                            direct()
                        if k == KT - 1:
                            dve.wait_ge(wpost_in, 16)
                    if c == 4:
                        if k == 0:
                            mean(0, 0, 4)
                        if k == 1:
                            rstd(0, 0, 4)
                        if k in (2, 4, 6, 8):
                            add_residual(0, BLOCKS[(k - 2) // 2])
                for m in BLOCKS:
                    y_copy(c, m)
            for i, m in enumerate(BLOCKS):
                y_copy(LAST, m)
                mean(1 + i, m, m + 1)
                rstd(1 + i, m, m + 1)
                add_residual(1, m)

        @block.tensor
        def _(pe):
            def tile(T, par, job=None, cols=SEQ):
                halves = [(0, HALF), (1, HALF)] if cols == SEQ else [(0, cols)]
                in_hi, in_lo = (hT_hi, hT_lo) if cols == SEQ else (memT_hi, memT_lo)
                if not isinstance(T, int) or T >= 2:
                    pe.wait_ge(evac_act, T - 1)
                    pe.wait_ge(evac_dve, T - 1)
                for k in range(KT):
                    j = k // 4
                    if k % 4 == 0:
                        pe.wait_ge(lo_done, 4 * T + j + 1)
                    whi = w_hi[:, j, (k % 4) * P:(k % 4 + 1) * P]
                    wlo = w_lo[:, j, (k % 4) * P:(k % 4 + 1) * P]
                    if isinstance(T, int) and T == T_LR:
                        passes = ((whi, in_hi, True, False), (whi, in_lo, False, True))
                    else:
                        passes = ((whi, in_hi, True, False), (whi, in_lo, False, False), (wlo, in_hi, False, True))
                    for w, h, first, final in passes:
                        for q, n in halves:
                            mm = pe.matmul(ps[:, (2 * par if cols == SEQ else par) + q, 0:n], w, h[:, k, q * HALF:q * HALF + n],
                                           start=(k == 0 and first), stop=(k == KT - 1 and final))
                    if k % 4 == 3:
                        mm.then_inc(unit_used, 1)
                    if job:
                        job(k)

            pe.wait_ge(s_rel, 32)
            pe.wait_ge(s_id, 3)
            for c in range(3):
                n = min(512, TABLE - 512 * c)
                mm = pe.matmul(ps[0:N_DIL, L + c, 0:n], rel_sb[:, :], tab_sb[:, 512 * c:512 * c + n], start=True, stop=True)
            mm.then_inc(s_bias, 1)
            pe.wait_ge(s_biasc, 1)

            def turn(n):
                pe.wait_ge(x_scaled, n + 1)
                for k in range(KT):
                    if n >= 2 and k == KT // 2:
                        pe.wait_ge(x_scaled_b, n - 1)
                    if n > 0 and k % 4 == 0:
                        pe.wait_ge(x_lo, 4 * (n - 1) + k // 4 + 1)
                    mm = pe.transpose(ps[:, L + k // 4, (k % 4) * P:(k % 4 + 1) * P], xs[:, n % 3, k * P:(k + 1) * P], ident[:, :])
                    if k % 4 == 3:
                        mm.then_inc(x_turned, 1)

            def turn_values(src, blocks):
                for b, t in enumerate(blocks):
                    mm = pe.transpose(ps[:, TB, b * P:(b + 1) * P], src[:, t * P:(t + 1) * P], ident[:, :])
                mm.then_inc(v_turned, 1)

            def mem_values(j):
                pe.wait_ge(evac_act, 3 + j)
                pe.wait_ge(x_lo, 4 * ROWS)
                if j > 0:
                    pe.wait_ge(v_dve, j)
                turn_values(vtm[:, j, :], (0, 1))

            for n in range(ROWS):
                turn(n)
                if n in MEM_TILE_AFTER:
                    pe.wait_ge(x_lo, 8)
                    tile(MEM_TILE_AFTER[n], MEM_TILE_AFTER[n] % 2, None, MEM)
            mem_values(0)
            pe.wait_ge(evac_act, 4)
            pe.wait_ge(x_sq, 2 * ROWS)

            def gla_v(T, q):
                def job(k):
                    if k == VALUES_AT:
                        pe.wait_ge(evac_act, T)
                        pe.wait_ge(evac_dve, T)
                        pe.wait_ge(v_dve, 2 + q)
                        turn_values(e2, range(0, 4))
                    if k == VALUES_AT + 1:
                        pe.wait_ge(v_act, 2 + q + 1)
                        turn_values(e2, range(4, 8))
                return job

            NV = 2 + 2 * N_GLA

            def dil_v(T, g):
                def job(k):
                    if k == VALUES_AT:
                        pe.wait_ge(evac_act, T)
                        pe.wait_ge(evac_dve, T)
                        turn_values(sc[:, 0, :], range(0, 4))
                    if k == VALUES_AT + 1:
                        pe.wait_ge(v_dve, NV + 2 * g + 1)
                        turn_values(sc[:, 0, :], range(4, 8))
                return job

            def soft(kind, a, hd, width, keys_hi, keys_lo, values):
                s = J[kind]
                causal = kind == "dil"
                groups = GROUPS if causal else [(i, 0, 2) for i in range(NBLK)]
                ng = len(groups)

                def scores(i):
                    w = width(i)
                    if i >= 2 or (hd == 1 and not causal):
                        pe.wait_ge(s["negmax" if causal else "exps"], NBLK * a + (i - 1 if w <= 512 else i))
                    elif hd == 1:
                        pe.wait_ge(s["negmax"], NBLK * a)
                    out_ = logits(i, w)
                    hi_rows = slice(hd * DH, hd * DH + DH)
                    for c in range(0, w, 512):
                        n = min(512, w - c)
                        pe.matmul(out_[:, c:c + n], qs[:, hd, i * P:(i + 1) * P], keys_hi[:, c:c + n], start=True, stop=False)
                        mm = pe.matmul(out_[:, c:c + n], qs[hi_rows, hd, i * P:(i + 1) * P], keys_lo[hi_rows, c:c + n], start=False, stop=True)
                    mm.then_inc(s["logits"], 1)

                def turned(n):
                    i, jb, nb = groups[n]
                    if jb == 0:
                        pe.wait_ge(s["probs"], NBLK * a + i + 1)
                    if n >= 1 or hd == 1:
                        pe.wait_ge(s["lo"], ng * a + n)
                    for b in range(nb):
                        mm = pe.transpose(ps[:, TB, b * P:(b + 1) * P], sc[:, i % 2, (jb + b) * P:(jb + b + 1) * P], ident[:, :])
                    mm.then_inc(s["turned"], 1)

                def values_(n):
                    i, jb, nb = groups[n]
                    pe.wait_ge(s["lo"], ng * a + n + 1)
                    if i == 5 and jb == 0:
                        pe.wait_ge(s["osum"], 2 * a + 1)
                    if i == 1 and hd == 1:
                        pe.wait_ge(s["osum"], 2 * a)
                    final = i - 1 if causal else 1

                    def product(j, part):
                        alone = causal and j == i
                        return pe.matmul(ps[:, OB, (i % 4 - (not alone)) * P:(i % 4 + 1) * P], values[:, j, :],
                                         part[:, place(kind, i, j), alone:2, :],
                                         start=(j == 0 and part is pT_hi), stop=(j == final and part is pT_lo))

                    for j in range(jb, min(jb + nb, final)):
                        product(j, pT_hi)
                        product(j, pT_lo)
                    if jb <= final < jb + nb:
                        product(final, pT_hi)
                    if causal and jb + nb - 1 == i:
                        product(i, pT_hi)
                        product(i, pT_lo)
                    if jb <= final < jb + nb:
                        mm = product(final, pT_lo)
                        if i % 4 == 3:
                            mm.then_inc(s["half"], 1)

                return scores, turned, values_

            def causal_job(g, part):
                def job(k):
                    if k == START[0] and part == 0:
                        pe.wait_ge(lo_a, 2 + 2 * g + 2)
                        pe.wait_ge(v_dve, NV + 2 * g + 2)
                    for hd in range(2):
                        scores, turned, values_ = soft("dil", 2 * g + hd, hd, lambda i: (i + 1) * P, kh[:, hd, :], kl[:, :], vv[:, hd, :, :])
                        r = k + 16 * part - START[hd]
                        if r in TURN_AT:
                            turned(TURN_AT[r])
                        if r in USE_AT:
                            values_(USE_AT[r])
                        if r in QK_AT:
                            if r == 0 and hd == 1:
                                pe.wait_ge(evac_dve, T_D + 4 * g + 2)
                            scores(QK_AT[r])
                return job

            def mem_job(j, part):
                def parts(n):
                    hd = n // NBLK
                    return soft("mem", 2 * j + hd, hd, lambda i: MEM, mkh[:, 2 * j + hd, :], mkl[:, j, :], mv[:, 2 * j + hd, :, :])

                def job(k):
                    r = k + 16 * part
                    if r == MEM_START:
                        pe.wait_ge(evac_dve, T_MQ0 + 2 * j + 1)
                        pe.wait_ge(J["dil" if j == 0 else "mem"]["osum"], 2 * N_DIL if j == 0 else 4)
                    if r in MEM_TURN_AT:
                        n = MEM_TURN_AT[r]
                        parts(n)[1](n % NBLK)
                    if r in MEM_USE_AT:
                        n = MEM_USE_AT[r]
                        parts(n)[2](n % NBLK)
                    if r in MEM_QK_AT:
                        n = MEM_QK_AT[r]
                        parts(n)[0](n % NBLK)
                return job

            def gla(h, part):
                def job(k0):
                    k = k0 + 16 * part
                    if k == -4:
                        pe.wait_ge(g_par, 32 * h + 32)
                        for q in range(2):
                            mm = pe.matmul(ps[:, L + q, :], w2h[:, :], lrT[:, q * HALF:(q + 1) * HALF], start=True, stop=True)
                        mm.then_inc(g_z, 1)
                    if k in (8, 9):
                        q = k - 8
                        if q == 0:
                            pe.wait_ge(g_ks, h + 1)
                            pe.wait_ge(v_dve, 2 + 2 * h + 2)
                        else:
                            pe.wait_ge(g_kcopied, 2 * h + 1)
                        for b in range(4):
                            t = 4 * q + b
                            mm = pe.transpose(ps[:, TB, b * P:(b + 1) * P], gk[:, t * P:(t + 1) * P], ident[:, :])
                        mm.then_inc(g_kturned, 1)
                    if 12 <= k < 28 and k % 2 == 0:
                        i = (k - 12) // 2
                        blk = slice(i * P, (i + 1) * P)
                        if i == 0:
                            pe.wait_ge(g_kcopied, 2 * h + 2)
                            pe.wait_ge(g_kt, h + 1)
                            pe.wait_ge(g_min, h + 1)
                        else:
                            pe.wait_ge(g_am, 8 * h + i)
                            pe.wait_ge(g_st, 15 * h + 2 * i)
                        pe.matmul(ps[:, TB, 0:P], bcum[:, blk], gq[:, blk], start=True, stop=True).then_inc(g_a, 1)
                        for c in range(2):
                            if 2 * i + c == 2 * NBLK - 1:
                                continue
                            r = slice(c * CHUNK, (c + 1) * CHUNK)
                            pe.matmul(ps[:, L + c, 0:DV], ks[r, i, :], gv[r, i, :], start=True, stop=True).then_inc(g_kv, 1)
                    if 13 <= k < 29 and k % 2 == 1:
                        i = (k - 13) // 2
                        pe.wait_ge(g_am, 8 * h + i + 1)
                        pe.wait_ge(g_st, 15 * h + min(2 * i + 1, 15))
                        if i >= 1:
                            pe.wait_ge(g_ocopied, 8 * h + i)
                        pe.matmul(ps[:, OB, 0:DV], am[:, i % 2, :], gv[:, i, :], start=True, stop=False)
                        for c in range(2):
                            t = i * P + c * CHUNK
                            mm = pe.matmul(ps[c * CHUNK:(c + 1) * CHUNK, OB, 0:DV], gq[:, t:t + CHUNK], state[:, (2 * i + c) % 4, :],
                                           start=False, stop=True)
                        mm.then_inc(g_o, 1)
                    if 35 <= k < 39:
                        q = k - 35
                        j, t = q // 2, q % 2
                        if q == 0:
                            pe.wait_ge(g_scaled, h + 1)
                        else:
                            pe.wait_ge(g_mixo, 4 * h + q)
                        for b in range(4):
                            mm = pe.transpose(ps[:, TB, b * P:(b + 1) * P], osb[:, 4 * t + b, j * P:(j + 1) * P], ident[:, :])
                        mm.then_inc(g_turned, 1)
                return job

            tile(T_LR, T_LR % 2, lambda k: mem_values(1) if k == MEM_VALUES_AT else None)
            tile(T_GV0, T_GV0 % 2)

            def gla_head(h):
                T = T_G + 6 * h
                tile(T, 0, gla_v(T, 2 * h))
                tile(T + 1, 1, gla_v(T + 1, 2 * h + 1))
                tile(T + 2, 0, gla(h, -1))
                tile(T + 3, 1, gla(h, 0))
                tile(T + 4, 0, gla(h, 1))
                tile(T + 5, 1, gla(h, 2))

            with pe.Fori(0, N_GLA) as h:
                gla_head(h)

            def dil_pair(g):
                T = T_D + 4 * g
                tile(T, 0, dil_v(T, g))
                tile(T + 1, 1)
                tile(T + 2, 0, causal_job(g, 0))
                tile(T + 3, 1, causal_job(g, 1))

            with pe.Fori(0, N_DIL // 2) as g:
                dil_pair(g)
            tile(T_MQ0 + 1, (T_MQ0 + 1) % 2, mem_job(0, 0))
            tile(T_MQ0 + 2, T_MQ0 % 2, mem_job(0, 1))
            tile(T_MQ0 + 3, (T_MQ0 + 1) % 2, mem_job(1, 0))

            def bank_free(c, m):
                if c == 0 and m == BLOCKS[0]:
                    pe.wait_ge(evac_act, T_END - 1)
                    pe.wait_ge(evac_dve, T_END - 1)
                if c == 0 and m == BLOCKS[2]:
                    pe.wait_ge(evac_act, T_END)
                    pe.wait_ge(evac_dve, T_END)
                if c == 1 and m == BLOCKS[0]:
                    pe.wait_ge(J["mem"]["osum"], 8)
                if c >= 2:
                    pe.wait_ge(y_sq, 4 * (c - 2) + BLOCKS.index(m) + 1)

            def mix_ready(hf, k):
                pe.wait_ge(m_lo, piece_no(DIRECT * hf + k) if k < KT - 1 else DIRECT + 1 + hf)

            def products(c, m, k, whi, wlo):
                hf = c // 4
                t = slice(hf * HALF + m * P, hf * HALF + (m + 1) * P)
                bank = ps[:, 4 * (c % 2) + m, :]
                pe.matmul(bank, hT_hi[:, k, t], whi, start=(k == 0), stop=False)
                pe.matmul(bank, hT_hi[:, k, t], wlo, start=False, stop=False)
                return pe.matmul(bank, hT_lo[:, k, t], whi, start=False, stop=(k == KT - 1))

            for c in range(LAST):
                for k in range(KT):
                    pe.wait_ge(lo_done, UNIT_NO[c, k] + 1)
                    mix_ready(c // 4, k)
                    for m in BLOCKS:
                        if k == 0:
                            bank_free(c, m)
                        mm = products(c, m, k, w_hi[:, k % 4, :], w_lo[:, k % 4, :])
                        if m != BLOCKS[3] and k == KT - 1:
                            mm.then_inc(y_done, 1)
                    mm.then_inc(unit_used, 1)
                    if c == 0:
                        mem_job(1, 1)(k)
            for m in BLOCKS:
                bank_free(LAST, m)
                for k in range(KT):
                    if m == BLOCKS[0]:
                        pe.wait_ge(lo_done, UNIT_NO[LAST, k] + 1)
                    mm = products(LAST, m, k, hT_hi[:, k, 0:HALF], hT_lo[:, k, 0:HALF])
                mm.then_inc(y_done, 1)


_INS = ['x', 'mem', 'norm_pre_w', 'w_in', 'rel_bias', 'w_gla_gate2', 'b_gla_gate', 'gla_norm_w',
        'mem_norm_w', 'w_mem_kv', 'w_out', 'norm_post_w']


def kernel(**inputs):
    import numpy as _np
    import concourse.bacc as _bacc
    from concourse import mybir as _mybir
    from concourse.bass_utils import run_bass_kernel_spmd as _run

    nc = _bacc.Bacc("TRN2", target_bir_lowering=False, num_devices=1, dynamic_dma_scratch_size=1024)
    arrays, args = {}, []
    for name in _INS:
        a = _np.ascontiguousarray(inputs[name])
        arrays[f"in_{name}_dram"] = a
        args.append(nc.dram_tensor(f"in_{name}_dram", a.shape, _mybir.dt.from_np(a.dtype), kind="ExternalInput").ap())
    arrays["dist_table_dram"] = distance_table()
    f32 = _mybir.dt.float32
    args.append(nc.dram_tensor("dist_table_dram", (BUCKETS + 1, TABLE), f32, kind="ExternalInput").ap())
    args.append(nc.dram_tensor("bias_rows", (N_DIL, TABLE), f32, kind="Internal").ap())
    args.append(nc.dram_tensor("bias_tables", (N_DIL, P * TABLE), f32, kind="Internal").ap())
    args.append(nc.dram_tensor("mix", (D, SEQ), f32, kind="Internal").ap())
    args.append(nc.dram_tensor("out_dram", (1, SEQ, D), f32, kind="ExternalOutput").ap())
    with nc.allow_non_contiguous_dma(reason="norm weights and gate biases, one element a partition"):
        build(nc, *args)
    r = _run(nc, [arrays], core_ids=[0])
    return r.results[0]["out_dram"]
```
